# Optimizing a Trainium2 kernel written in Bass

```python
import jax
import jax.numpy as jnp
from jax import lax
import numpy as np

D_MODEL = 2048
BATCH = 1
SEQ = 128
DEPTH = 1
DEC_BATCH = 1
DEC_SEQ = 512
PAST_LEN = 128

GRID_W = 64
DN_HEADS = 8
DN_DK = 128
DN_DV = 128
DN_CONV = 5
ML_HEADS = 4
ML_DK = 128
ML_DV = 256
CHUNK = 64
N_EXPERTS = 16
EC_CAPACITY = 2
D_EXPERT = 1024
N_MOD = 6
EPS = 1e-6

DN_QK = DN_HEADS * DN_DK
DN_V = DN_HEADS * DN_DV
ML_QK = ML_HEADS * ML_DK
ML_V = ML_HEADS * ML_DV
DN_CONV_CH = 2 * DN_QK + DN_V
IN_SIZES = (DN_QK, DN_QK, DN_V, DN_V, 2 * DN_HEADS, 2 * DN_HEADS,
            ML_QK, ML_QK, ML_V, ML_V, 2 * ML_HEADS, 2 * ML_HEADS,
            D_MODEL, D_MODEL)
D_IN = sum(IN_SIZES)

kernel_name = 'hybrid_deltanet_mlstm_ec_diffusion_step'

def rmsnorm(x, gain):
    xf = x.astype(jnp.float32)
    y = xf * lax.rsqrt(jnp.mean(xf * xf, axis=-1, keepdims=True) + EPS)
    return (y * gain.astype(jnp.float32)).astype(x.dtype)

def l2norm(x):
    return x * lax.rsqrt(jnp.sum(x * x, axis=-1, keepdims=True) + EPS)

def split_columns(a):
    offsets = np.cumsum(IN_SIZES)[:-1].tolist()
    return jnp.split(a, offsets, axis=-1)

def centred_dwconv(x, w):
    pad = w.shape[0] // 2
    return lax.conv_general_dilated(
        x, w[:, None, :].astype(x.dtype), window_strides=(1,), padding=[(pad, pad)],
        dimension_numbers=('NWC', 'WIO', 'NWC'), feature_group_count=x.shape[-1])

def to_chunks(a):
    b, t = a.shape[:2]
    a = a.reshape((b, t // CHUNK, CHUNK) + a.shape[2:])
    return jnp.moveaxis(a, (1, 3), (0, 2))

def from_chunks(a):
    a = jnp.moveaxis(a, (0, 2), (1, 3))
    return a.reshape((a.shape[0], a.shape[1] * a.shape[2]) + a.shape[3:])

def raster_to_column(a, rows):
    b = a.shape[0]
    a = a.reshape((b, rows, GRID_W) + a.shape[2:])
    return jnp.swapaxes(a, 1, 2).reshape((b, rows * GRID_W) + a.shape[3:])

def column_to_raster(a, rows):
    b = a.shape[0]
    a = a.reshape((b, GRID_W, rows) + a.shape[2:])
    return jnp.swapaxes(a, 1, 2).reshape((b, rows * GRID_W) + a.shape[3:])

def flip(a):
    return jnp.flip(a, axis=1)

def gated_delta_scan(q, k, v, beta, g, s0):
    dv = v.shape[-1]
    qc, kc, vc, bc, gc = (to_chunks(a) for a in (q, k, v, beta, g))
    G = jnp.cumsum(gc, axis=-1)
    tril = jnp.tril(jnp.ones((CHUNK, CHUNK), bool))
    strict = jnp.tril(jnp.ones((CHUNK, CHUNK), bool), -1)
    decay = jnp.exp(jnp.where(tril, G[..., :, None] - G[..., None, :], -jnp.inf))
    kb = kc * bc[..., None]
    a_low = jnp.where(strict, jnp.einsum('nbhid,nbhjd->nbhij', kb, kc) * decay, 0.0)
    m_unit = a_low + jnp.eye(CHUNK, dtype=kc.dtype)
    rhs = jnp.concatenate([vc * bc[..., None], kb * jnp.exp(G)[..., None]], axis=-1)
    sol = lax.linalg.triangular_solve(m_unit, rhs, left_side=True, lower=True, unit_diagonal=True)
    w_v, u_k = sol[..., :dv], sol[..., dv:]

    def step(s, xs):
        q_i, k_i, g_i, dec_i, wv_i, uk_i = xs
        v_new = wv_i - jnp.einsum('bhlk,bhkv->bhlv', uk_i, s)
        scores = jnp.einsum('bhik,bhjk->bhij', q_i, k_i) * dec_i
        out = (jnp.einsum('bhlk,bhkv->bhlv', q_i * jnp.exp(g_i)[..., None], s)
               + jnp.einsum('bhij,bhjv->bhiv', scores, v_new))
        g_last = g_i[..., -1]
        s = (s * jnp.exp(g_last)[..., None, None]
             + jnp.einsum('bhlk,bhlv->bhkv', k_i * jnp.exp(g_last[..., None] - g_i)[..., None], v_new))
        return s, out

    s_final, out = lax.scan(step, s0.astype(jnp.float32), (qc, kc, G, decay, w_v, u_k))
    return from_chunks(out), s_final

def mlstm_scan(q, k, v, log_i, log_f, c0, n0, m0):
    qc, kc, vc, ic, fc = (to_chunks(a) for a in (q, k, v, log_i, log_f))
    b = jnp.cumsum(fc, axis=-1)
    tril = jnp.tril(jnp.ones((CHUNK, CHUNK), bool))
    d_log = jnp.where(tril, b[..., :, None] - b[..., None, :] + ic[..., None, :], -jnp.inf)
    w_end = b[..., -1:] - b + ic

    def step(carry, xs):
        c_st, n_st, m_st = carry
        q_i, k_i, v_i, b_i, d_i, we_i = xs
        a_i = b_i + m_st[..., None]
        m_t = jnp.maximum(a_i, jnp.max(d_i, axis=-1))
        inter = jnp.exp(a_i - m_t)
        p_ij = jnp.exp(d_i - m_t[..., None]) * jnp.einsum('bhik,bhjk->bhij', q_i, k_i)
        num = (inter[..., None] * jnp.einsum('bhlk,bhkv->bhlv', q_i, c_st)
               + jnp.einsum('bhij,bhjv->bhiv', p_ij, v_i))
        den = inter * jnp.einsum('bhlk,bhk->bhl', q_i, n_st) + jnp.sum(p_ij, axis=-1)
        h_i = num / jnp.maximum(jnp.abs(den), jnp.exp(-m_t))[..., None]
        m_new = jnp.maximum(b_i[..., -1] + m_st, jnp.max(we_i, axis=-1))
        carry_decay = jnp.exp(b_i[..., -1] + m_st - m_new)
        w_i = jnp.exp(we_i - m_new[..., None])
        c_new = carry_decay[..., None, None] * c_st + jnp.einsum('bhl,bhlk,bhlv->bhkv', w_i, k_i, v_i)
        n_new = carry_decay[..., None] * n_st + jnp.einsum('bhl,bhlk->bhk', w_i, k_i)
        return (c_new, n_new, m_new), h_i

    f32 = jnp.float32
    (c_f, n_f, m_f), h = lax.scan(step, (c0.astype(f32), n0.astype(f32), m0.astype(f32)),
                                  (qc, kc, vc, b, d_log, w_end))
    return from_chunks(h), c_f, n_f, m_f

def token_mix(h, l, p, dn_s0, ml_c0, ml_n0, ml_m0, rows):
    f32 = jnp.float32
    bsz, t, _ = h.shape
    proj = h @ p['w_in'][l] + p['b_in'][l]
    (dq, dk, dv, dz, db, da, mq, mk, mv, mo, mi, mf, ga, gb) = split_columns(proj)

    qkv = jax.nn.silu(centred_dwconv(jnp.concatenate([dq, dk, dv], axis=-1), p['dn_conv_w'][l]))
    dq, dk, dv = jnp.split(qkv, [DN_QK, 2 * DN_QK], axis=-1)
    dq = l2norm(dq.reshape(bsz, t, DN_HEADS, DN_DK).astype(f32)) * (DN_DK ** -0.5)
    dk = l2norm(dk.reshape(bsz, t, DN_HEADS, DN_DK).astype(f32))
    dv = dv.reshape(bsz, t, DN_HEADS, DN_DV).astype(f32)
    beta = jax.nn.sigmoid(db.astype(f32).reshape(bsz, t, 2, DN_HEADS))
    g = -jnp.exp(p['dn_a_log'][l].astype(f32)) * jax.nn.softplus(
        da.astype(f32).reshape(bsz, t, 2, DN_HEADS) + p['dn_dt_bias'][l].astype(f32))
    o_f, s_f = gated_delta_scan(dq, dk, dv, beta[:, :, 0], g[:, :, 0], dn_s0[:, 0])
    o_b, s_b = gated_delta_scan(flip(dq), flip(dk), flip(dv), flip(beta[:, :, 1]), flip(g[:, :, 1]), dn_s0[:, 1])
    o_dn = o_f + flip(o_b)
    y_a = (rmsnorm(o_dn, p['dn_onorm'][l]) * jax.nn.silu(dz.reshape(bsz, t, DN_HEADS, DN_DV).astype(f32)))
    y_a = y_a.reshape(bsz, t, DN_V).astype(h.dtype)

    mq = mq.reshape(bsz, t, ML_HEADS, ML_DK).astype(f32)
    mk = mk.reshape(bsz, t, ML_HEADS, ML_DK).astype(f32) * (ML_DK ** -0.5)
    mv = mv.reshape(bsz, t, ML_HEADS, ML_DV).astype(f32)
    log_i = mi.astype(f32).reshape(bsz, t, 2, ML_HEADS) + p['ml_i_bias'][l].astype(f32)
    log_f = jax.nn.log_sigmoid(mf.astype(f32).reshape(bsz, t, 2, ML_HEADS) + p['ml_f_bias'][l].astype(f32))
    if rows is not None:
        mq, mk, mv, log_i, log_f = (raster_to_column(a, rows) for a in (mq, mk, mv, log_i, log_f))
    h_f, c_f, n_f, m_f = mlstm_scan(mq, mk, mv, log_i[:, :, 0], log_f[:, :, 0],
                                    ml_c0[:, 0], ml_n0[:, 0], ml_m0[:, 0])
    h_b, c_b, n_b, m_b = mlstm_scan(flip(mq), flip(mk), flip(mv), flip(log_i[:, :, 1]), flip(log_f[:, :, 1]),
                                    ml_c0[:, 1], ml_n0[:, 1], ml_m0[:, 1])
    h_ml = h_f + flip(h_b)
    if rows is not None:
        h_ml = column_to_raster(h_ml, rows)
    y_b = rmsnorm(h_ml, p['ml_onorm'][l]) * jax.nn.sigmoid(mo.reshape(bsz, t, ML_HEADS, ML_DV).astype(f32))
    y_b = y_b.reshape(bsz, t, ML_V).astype(h.dtype)

    y = jax.nn.sigmoid(ga) * (y_a @ p['w_up_a'][l]) + jax.nn.sigmoid(gb) * (y_b @ p['w_up_b'][l])
    y = y @ p['w_out'][l]
    states = (jnp.stack([s_f, s_b], axis=1), jnp.stack([c_f, c_b], axis=1),
              jnp.stack([n_f, n_b], axis=1), jnp.stack([m_f, m_b], axis=1))
    return y, states

def expert_choice_ffn(h, w_router, w_gate, w_up, w_down):
    bsz, t, _ = h.shape
    cap = EC_CAPACITY * t // N_EXPERTS
    aff = jax.nn.softmax((h @ w_router).astype(jnp.float32), axis=-1)
    gate, idx = lax.top_k(jnp.swapaxes(aff, 1, 2), cap)
    bi = jnp.arange(bsz)[:, None, None]
    xe = h[bi, idx]
    a = jnp.einsum('becd,edf->becf', xe, w_gate)
    u = jnp.einsum('becd,edf->becf', xe, w_up)
    ye = jnp.einsum('becf,efd->becd', jax.nn.silu(a) * u, w_down) * gate[..., None].astype(h.dtype)
    return jnp.zeros_like(h).at[bi, idx].add(ye)

def trunk_layer(x, cond, l, p, dn_s0, ml_c0, ml_n0, ml_m0, rows):
    mod = (cond @ p['w_mod'][l] + p['b_mod'][l])[:, None, :]
    shift1, scale1, gate1, shift2, scale2, gate2 = jnp.split(mod, N_MOD, axis=-1)
    h = rmsnorm(x, p['pre1_gain'][l]) * (1 + scale1) + shift1
    y, states = token_mix(h, l, p, dn_s0, ml_c0, ml_n0, ml_m0, rows)
    x = x + gate1 * rmsnorm(y, p['post1_gain'][l])
    h = rmsnorm(x, p['pre2_gain'][l]) * (1 + scale2) + shift2
    y = expert_choice_ffn(h, p['w_router'][l], p['w_gate'][l], p['w_up'][l], p['w_down'][l])
    x = x + gate2 * rmsnorm(y, p['post2_gain'][l])
    return x, states

def setup_inputs(seed: int = 0) -> dict:
    key = jax.random.key(seed)
    ks = iter(jax.random.split(key, 40))
    f32 = jnp.float32
    D = D_MODEL

    def nrm(shape, scale):
        return jax.random.normal(next(ks), shape, f32) * scale

    def gain(shape):
        return 1.0 + nrm(shape, 0.02)

    dt = jnp.exp(jax.random.uniform(next(ks), (DEPTH, 2, DN_HEADS), f32, -6.9, -2.3))
    a_init = jax.random.uniform(next(ks), (DEPTH, 2, DN_HEADS), f32, 1.0, 16.0)
    f_bias = jax.random.uniform(next(ks), (DEPTH, 2, ML_HEADS), f32, 3.0, 6.0)
    return {
        'x_prompt': nrm((BATCH, SEQ, D), 1.0),
        'x_sample': nrm((DEC_BATCH, DEC_SEQ, D), 1.0),
        'state_dn': nrm((DEC_BATCH, DEPTH, 2, DN_HEADS, DN_DK, DN_DV), 0.1),
        'state_ml_c': nrm((DEC_BATCH, DEPTH, 2, ML_HEADS, ML_DK, ML_DV), 0.1),
        'state_ml_n': nrm((DEC_BATCH, DEPTH, 2, ML_HEADS, ML_DK), 0.1),
        'state_ml_m': nrm((DEC_BATCH, DEPTH, 2, ML_HEADS), 0.5),
        'c': nrm((DEC_BATCH, D), 1.0),
        'c_ctx': nrm((D,), 1.0),
        'w_mod': nrm((DEPTH, D, N_MOD * D), 0.5 * D ** -0.5),
        'b_mod': nrm((DEPTH, N_MOD * D), 0.02),
        'pre1_gain': gain((DEPTH, D)),
        'w_in': nrm((DEPTH, D, D_IN), D ** -0.5),
        'b_in': nrm((DEPTH, D_IN), 0.02),
        'dn_conv_w': nrm((DEPTH, DN_CONV, DN_CONV_CH), DN_CONV ** -0.5),
        'dn_a_log': jnp.log(a_init),
        'dn_dt_bias': dt + jnp.log(-jnp.expm1(-dt)),
        'dn_onorm': gain((DEPTH, DN_DV)),
        'ml_i_bias': nrm((DEPTH, 2, ML_HEADS), 0.1),
        'ml_f_bias': f_bias,
        'ml_onorm': gain((DEPTH, ML_HEADS, ML_DV)),
        'w_up_a': nrm((DEPTH, DN_V, D), DN_V ** -0.5),
        'w_up_b': nrm((DEPTH, ML_V, D), ML_V ** -0.5),
        'w_out': nrm((DEPTH, D, D), D ** -0.5),
        'post1_gain': gain((DEPTH, D)),
        'pre2_gain': gain((DEPTH, D)),
        'w_router': nrm((DEPTH, D, N_EXPERTS), D ** -0.5),
        'w_gate': nrm((DEPTH, N_EXPERTS, D, D_EXPERT), D ** -0.5),
        'w_up': nrm((DEPTH, N_EXPERTS, D, D_EXPERT), D ** -0.5),
        'w_down': nrm((DEPTH, N_EXPERTS, D_EXPERT, D), D_EXPERT ** -0.5),
        'post2_gain': gain((DEPTH, D)),
    }

def reference(x_prompt, x_sample, state_dn, state_ml_c, state_ml_n, state_ml_m, c, c_ctx,
              w_mod, b_mod, pre1_gain, w_in, b_in, dn_conv_w, dn_a_log, dn_dt_bias, dn_onorm,
              ml_i_bias, ml_f_bias, ml_onorm, w_up_a, w_up_b, w_out, post1_gain,
              pre2_gain, w_router, w_gate, w_up, w_down, post2_gain):
    p = dict(w_mod=w_mod, b_mod=b_mod, pre1_gain=pre1_gain, w_in=w_in, b_in=b_in,
             dn_conv_w=dn_conv_w, dn_a_log=dn_a_log, dn_dt_bias=dn_dt_bias, dn_onorm=dn_onorm,
             ml_i_bias=ml_i_bias, ml_f_bias=ml_f_bias, ml_onorm=ml_onorm,
             w_up_a=w_up_a, w_up_b=w_up_b, w_out=w_out, post1_gain=post1_gain,
             pre2_gain=pre2_gain, w_router=w_router, w_gate=w_gate, w_up=w_up,
             w_down=w_down, post2_gain=post2_gain)
    f32 = jnp.float32

    bp = x_prompt.shape[0]
    zero_dn = jnp.zeros((bp, 2, DN_HEADS, DN_DK, DN_DV), f32)
    zero_c = jnp.zeros((bp, 2, ML_HEADS, ML_DK, ML_DV), f32)
    zero_n = jnp.zeros((bp, 2, ML_HEADS, ML_DK), f32)
    zero_m = jnp.zeros((bp, 2, ML_HEADS), f32)
    cond_ctx = jax.nn.silu(c_ctx)[None, :]
    x = x_prompt
    new_dn, new_c, new_n, new_m = [], [], [], []
    for l in range(DEPTH):
        x, (s_dn, s_c, s_n, s_m) = trunk_layer(x, cond_ctx, l, p, zero_dn, zero_c, zero_n, zero_m, None)
        new_dn.append(s_dn)
        new_c.append(s_c)
        new_n.append(s_n)
        new_m.append(s_m)
    y_prompt = x

    rows = x_sample.shape[1] // GRID_W
    cond = jax.nn.silu(c)
    x = x_sample
    for l in range(DEPTH):
        x, _ = trunk_layer(x, cond, l, p, state_dn[:, l], state_ml_c[:, l], state_ml_n[:, l],
                           state_ml_m[:, l], rows)
    y_sample = x

    return (y_prompt, y_sample, jnp.stack(new_dn, axis=1), jnp.stack(new_c, axis=1),
            jnp.stack(new_n, axis=1), jnp.stack(new_m, axis=1))


_drawn_inputs = setup_inputs


def setup_inputs(seed=0):
    import zlib

    import numpy as np

    out = dict(_drawn_inputs(seed))
    spreads = {}
    factors = {'state_ml_c': 2.963,
     'state_ml_n': 4.22,
     'state_ml_m': 2.889,
     'ml_onorm': 4.866,
     'post1_gain': 3.479,
     'post2_gain': 8.0}
    for name, (base, spread) in spreads.items():
        noise = np.random.default_rng([zlib.crc32(name.encode()), seed]).standard_normal(out[name].shape)
        drawn = base * np.exp(spread * noise) if base else spread * noise
        out[name] = jnp.asarray(drawn.astype(out[name].dtype))
    for name, factor in factors.items():
        out[name] = (out[name] * factor).astype(out[name].dtype)
    return out
```

```python
from contextlib import ExitStack

import numpy as np

import concourse.bass as bass
from concourse import mybir

ALU = mybir.AluOpType
ACT = mybir.ActivationFunctionType
F32 = mybir.dt.float32
U32 = mybir.dt.uint32
AX = mybir.AxisListType

P = 128
D = 2048
KT = D // P
NP_TOK, NS_TOK = 128, 512
T = NP_TOK + NS_TOK
TT = T // P
GRID_W = 64
ROWS = NS_TOK // GRID_W
H_DN, H_ML, DV_ML = 8, 4, 256
N_EXP, F_EXP = 16, 1024
CAP_P, CAP_S = 2 * NP_TOK // N_EXP, 2 * NS_TOK // N_EXP
CAP = CAP_P + CAP_S
EPS = 1e-6
K_SCALE = float(P) ** -0.5
NEG = -1e30
LEVELS = [1, 2, 4, 8, 16, 32, 64]

QK_TILES, V_TILES, PERM_TILES, RASTER_TILES = 16, 8, 16, 48
T_MLQ, T_Z, T_MO, T_GA, T_GB = 24, 40, 48, 56, 72
N_TILES = 88
N_MOD_TILES = 6 * KT

C_ID, C_TRI, C_NEG, C_ONES, C_LEV = 0, 128, 384, 640, 768
N_CONST = C_LEV + 2 * len(LEVELS) * P

V_COND = 0
V_BMOD = V_COND + 2 * KT
V_PRE1 = V_BMOD + N_MOD_TILES
V_POST1 = V_PRE1 + KT
V_PRE2 = V_POST1 + KT
V_POST2 = V_PRE2 + KT
V_BIN = V_POST2 + KT
V_CONV = V_BIN + N_TILES
V_L2S = V_CONV + 24 * 5
V_L2B = V_L2S + 16
V_DNG = V_L2B + 16
V_MLG = V_DNG + 1
N_CHAN = V_MLG + 8

R_GB, R_DT, R_FB, R_IB, R_AL, R_M0 = 0, 48, 64, 72, 80, 96
N_ROWP = 104

MASKED_ROW = -1.0


def wait(eng, sem, value):
    if not (isinstance(value, int) and value == 0):
        eng.wait_ge(sem, value)


class Bank:

    def __init__(self, tensor, filled, emptied, fills):
        self.t, self.filled, self.emptied = tensor, filled, emptied
        self.order = {f: n for n, f in enumerate(fills)}
        self.per_step = len(fills)

    def wait_free(self, eng, step, fill):
        wait(eng, self.emptied, step * self.per_step + self.order[fill])

    def wait_filled(self, eng, step, fill):
        wait(eng, self.filled, step * self.per_step + self.order[fill] + 1)

    def wait_emptied(self, eng, step, fill):
        wait(eng, self.emptied, step * self.per_step + self.order[fill] + 1)


class Chip:

    def __init__(self, sem, ins, outs, scratch):
        self.sem = sem
        (self.d_const, self.d_chan, self.d_rowp, self.d_x, self.d_wmod, self.d_win, self.d_wgates, self.d_sdn,
         self.d_smc, self.d_smn, self.d_wup, self.d_wout, self.d_wrouter, self.d_wgate, self.d_wup_e,
         self.d_wdown) = (ins[n] for n in (
             "d_const", "d_chan", "d_rowp", "d_x", "d_wmod", "d_win", "d_wgates", "d_sdn", "d_smc", "d_smn",
             "d_wup", "d_wout", "d_wrouter", "d_wgate", "d_wup_e", "d_wdown"))
        self.o_yp, self.o_ys, self.o_sdn, self.o_smc, self.o_smn, self.o_smm = (
            outs[n] for n in ("o_yp", "o_ys", "o_sdn", "o_smc", "o_smn", "o_smm"))
        self.d_proj, self.d_x1, self.d_h2, self.d_y, self.d_g2 = (
            scratch[n] for n in ("d_proj", "d_x1", "d_h2", "d_y", "d_g2"))


def h4(ap):
    return ap.rearrange("p (h n) -> p h n", h=4)


def per_head(ap, n):
    return ap.unsqueeze(2).to_broadcast([P, ap.shape[1], n])


def all_heads(ap, heads=4):
    return ap.unsqueeze(1).to_broadcast([P, heads, ap.shape[1]])


def col(ap3, t, a, b):
    n = ap3.shape[2]
    return ap3.rearrange("p t n -> p (t n)")[:, bass.ds(t * n + a, b - a)]


def phase_modulation(nc, k):
    with ExitStack() as mem:
        def sb(name, shape):
            return mem.enter_context(nc.sbuf_tensor(name, shape, F32))
        w = sb("wmod_ring", [P, 4, KT, P])
        xin = sb("x_in", [P, D])
        xsq = sb("x_sq", [P, D])
        ssq = sb("x_ssq", [P, 1])
        root = sb("x_root", [P, 1])
        rstd = sb("x_rstd", [P, 1])
        xn = sb("x_normed", [P, D])
        cond = sb("cond", [P, KT, 2])
        a1 = sb("a1", [P, KT, 2])
        s = {n: k.sem(n) for n in ("params_in", "x_landed", "x_squared", "x_meaned", "x_rooted", "x_normed",
                                   "x_turned", "hT_written", "cond_ready", "mod_summed",
                                   "mod_bank_free", "mod_stored")}
        landed = [k.sem(f"wmod_landed{u}") for u in range(4)]
        with nc.Block() as block:
            @block.sync
            def _(sp):
                sp.dma_start(k.const[:], k.d_const).then_inc(s["params_in"], 16)
                sp.dma_start(k.chan[:], k.d_chan).then_inc(s["params_in"], 16)
                sp.dma_start(k.rowp[:], k.d_rowp).then_inc(s["params_in"], 16)
                with sp.Fori(0, TT) as t:
                    sp.wait_ge(s["x_normed"], t + 1)
                    sp.dma_start(xin[:], k.d_x[bass.ds(t * P, P), :]).then_inc(s["x_landed"], 16)

            @block.gpsimd
            def _(pool):
                with pool.Fori(0, N_MOD_TILES // 4) as i:
                    for u in range(4):
                        pool.wait_ge(s["mod_summed"], i * 4 + u + 1)
                        pool.dma_start(w[:, u], k.d_wmod[bass.ds(i * 4 + u, 1)].rearrange("a p k n -> p (a k) n")
                                       ).then_inc(landed[u], 16)

            @block.tensor
            def _(pe):
                pe.sem_inc(s["mod_summed"], 4)
                pe.wait_ge(s["params_in"], 48)
                with pe.Fori(0, TT) as t:
                    pe.wait_ge(s["x_normed"], t + 2)
                    pe.wait_ge(s["hT_written"], t + 1)
                    for kk in range(KT):
                        mm = pe.transpose(k.bank[kk // 4][:, (kk % 4) * P:(kk % 4 + 1) * P],
                                          xn[:, kk * P:(kk + 1) * P], k.ident)
                    mm.then_inc(s["x_turned"], 1)
                pe.wait_ge(s["cond_ready"], 1)
                with pe.Fori(0, N_MOD_TILES // 4) as i:
                    for u in range(4):
                        pe.wait_ge(landed[u], i * 16 + 16)
                        pe.wait_ge(s["mod_bank_free"], i * 4 + u + 1)
                        for kk in range(KT):
                            mm = pe.matmul(k.bank[4 + u % 2][:, 0:2], w[:, u, kk, :], cond[:, kk, :],
                                           start=(kk == 0), stop=(kk == KT - 1))
                        mm.then_inc(s["mod_summed"], 1)

            @block.scalar
            def _(act):
                act.wait_ge(s["params_in"], 48)
                act.activation(cond[:].rearrange("p k c -> p (k c)"), k.chan[:, V_COND:V_COND + 2 * KT],
                               ACT.Silu).then_inc(s["cond_ready"], 1)
                act.sem_inc(s["hT_written"], 1)
                with act.Fori(0, TT) as t:
                    act.wait_ge(s["x_landed"], t * 16 + 16)
                    act.activation(xsq[:], xin[:], ACT.Square, accum_out=ssq[:]).then_inc(s["x_squared"], 1)
                    act.wait_ge(s["x_meaned"], t + 1)
                    act.activation(root[:], ssq[:], ACT.Sqrt).then_inc(s["x_rooted"], 1)
                    act.wait_ge(s["x_turned"], t + 1)
                    for b in range(4):
                        ev = act.activation(k.hT[:, 4 * b:4 * b + 4, bass.ds(t * P, P)],
                                            h4(k.bank[b][:]), ACT.Copy)
                    ev.then_inc(s["hT_written"], 1)

            @block.vector
            def _(dve):
                dve.sem_inc(s["x_normed"], 1)
                dve.sem_inc(s["mod_bank_free"], 2)
                dve.wait_ge(s["params_in"], 48)
                with dve.Fori(0, TT) as t:
                    dve.wait_ge(s["x_squared"], t + 1)
                    dve.tensor_scalar(ssq[:], ssq[:], 1.0 / D, EPS, ALU.mult, ALU.add).then_inc(s["x_meaned"], 1)
                    dve.wait_ge(s["x_rooted"], t + 1)
                    dve.reciprocal(rstd[:], root[:])
                    dve.drain()
                    dve.wait_ge(s["hT_written"], t + 1)
                    dve.tensor_scalar(xn[:], xin[:], rstd[:, 0:1], None, ALU.mult).then_inc(s["x_normed"], 1)
                with dve.Fori(0, N_MOD_TILES // 4) as i:
                    for u in range(4):
                        m = i * 4 + u
                        dve.wait_ge(s["mod_summed"], m + 5)
                        dve.tensor_scalar(k.modT[:].rearrange("p m c -> p (m c)")[:, bass.ds(m * 2, 2)],
                                          k.bank[4 + u % 2][:, 0:2], k.chan[:, bass.ds(m + V_BMOD, 1)], None,
                                          ALU.add).then_inc(s["mod_bank_free"], 1)
                dve.drain()
                for c in range(2):
                    for out, gain, part, plus in ((a1, V_PRE1, 1, 1.0), (k.a2, V_PRE2, 4, 1.0),
                                                  (k.g1, V_POST1, 2, 0.0), (k.g2, V_POST2, 5, 0.0)):
                        dve.scalar_tensor_tensor(out=out[:, :, c], in0=k.modT[:, part * KT:(part + 1) * KT, c],
                                                 scalar=plus, in1=k.chan[:, gain:gain + KT],
                                                 op0=ALU.add, op1=ALU.mult)
                dve.drain()
                dve.wait_ge(s["hT_written"], TT + 1)
                for kk in range(KT):
                    for c, (lo, hi) in enumerate(((0, NP_TOK), (NP_TOK, T))):
                        dve.tensor_scalar(k.hT[:, kk, lo:hi], k.hT[:, kk, lo:hi], a1[:, kk, c:c + 1],
                                          k.modT[:, kk, c:c + 1], ALU.mult, ALU.add)


def phase_projection(nc, k):
    with ExitStack() as mem:
        def sb(name, shape):
            return mem.enter_context(nc.sbuf_tensor(name, shape, F32))
        w = sb("win_ring", [P, 4, KT, P])
        wg = sb("win_gates", [P, KT, 48])
        RAW = T + 8
        CV = T + 4
        S_RAW, S_CV = NP_TOK + 6, NP_TOK + 4
        raw = [sb(f"raw{b}", [P, RAW]) for b in range(2)]
        cv = sb("convolved", [P, CV])
        sl = sb("silu_out", [P, T])
        sq = sb("squares", [P, T])
        rt = sb("roots", [P, T])
        ob = [sb(f"proj_out{b}", [P, T]) for b in range(2)]
        s = {n: k.sem(n) for n in ("proj_summed", "evac", "conv", "silu", "sq", "ones", "root",
                                   "normed", "gates_in", "gates_summed", "gates_turned", "raw_zeroed")}
        gm = mem.enter_context(nc.sbuf_tensor("ml_gates", [16, T], F32))
        landed = [k.sem(f"win_landed{u}") for u in range(4)]
        stored = [k.sem(f"proj_stored{b}") for b in range(2)]
        bankS = [k.bank[0], k.bank[1]]
        bankP = [k.bank[2], k.bank[3]]

        with nc.Block() as block:
            @block.gpsimd
            def _(pool):
                pool.dma_start(wg[:], k.d_wgates).then_inc(s["gates_in"], 16)
                with pool.Fori(0, N_TILES // 4) as i:
                    for u in range(4):
                        pool.wait_ge(s["proj_summed"], i * 4 + u + 1)
                        pool.dma_start(w[:, u], k.d_win[bass.ds(i * 4 + u, 1)].rearrange("a p k n -> p (a k) n")
                                     ).then_inc(landed[u], 16)

            @block.tensor
            def _(pe):
                pe.sem_inc(s["proj_summed"], 4)
                pe.sem_inc(s["ones"], 1)

                def project(i, base, u):
                    n = i * 4 + (base + u)
                    pe.wait_ge(landed[u], i * 16 + 16 * (base // 4 + 1))
                    pe.wait_ge(s["evac"], n + 1)
                    for kk in range(KT):
                        pe.matmul(bankS[u % 2][:], w[:, u, kk, :], k.hT[:, kk, NP_TOK:T],
                                  start=(kk == 0), stop=(kk == KT - 1))
                        mm = pe.matmul(bankP[u % 2][:, 0:P], w[:, u, kk, :], k.hT[:, kk, 0:NP_TOK],
                                       start=(kk == 0), stop=(kk == KT - 1))
                    mm.then_inc(s["proj_summed"], 1)

                def sum_squares(i, u):
                    n = i * 4 + u
                    pe.wait_ge(s["sq"], n + 1)
                    pe.wait_ge(s["root"], n + 1)
                    pe.matmul(k.bank[4][:], k.ones, sq[:, NP_TOK:T], start=True, stop=True)
                    pe.matmul(k.bank[5][:, 0:P], k.ones, sq[:, 0:NP_TOK], start=True, stop=True
                              ).then_inc(s["ones"], 1)

                with pe.Fori(0, QK_TILES // 4) as i:
                    for u in range(4):
                        project(i, 0, u)
                        if u >= 1:
                            sum_squares(i, u - 1)
                    sum_squares(i, 3)
                with pe.Fori(0, (N_TILES - QK_TILES) // 4) as i:
                    for u in range(4):
                        project(i, QK_TILES, u)
                pe.wait_ge(s["gates_in"], 16)
                for t in range(TT):
                    for kk in range(KT):
                        mm = pe.matmul(k.bank[6][:, t * 48:t * 48 + 32], k.hT[:, kk, t * P:(t + 1) * P],
                                       wg[:, kk, 0:32], start=(kk == 0), stop=(kk == KT - 1))
                for kk in range(KT):
                    pe.matmul(k.bank[4][0:16, :], wg[:, kk, 32:48], k.hT[:, kk, NP_TOK:T],
                              start=(kk == 0), stop=(kk == KT - 1))
                for kk in range(KT):
                    mm = pe.matmul(k.bank[5][0:16, 0:P], wg[:, kk, 32:48], k.hT[:, kk, 0:NP_TOK],
                                   start=(kk == 0), stop=(kk == KT - 1))
                mm.then_inc(s["gates_summed"], 1)
                pe.wait_ge(s["gates_turned"], 1)
                for t in range(TT):
                    mm = pe.transpose(k.bank[6][:, t * 48 + 32:t * 48 + 48], gm[:, t * P:(t + 1) * P],
                                      k.ident[0:16, 0:16])
                mm.then_inc(s["gates_summed"], 1)

            def bias(n):
                return k.chan[:, bass.ds(n + V_BIN, 1)]

            def wait_store(eng, i, base, u):
                eng.wait_ge(stored[u % 2], i * 32 + (base // 2 + u // 2 + 1) * 16)

            @block.scalar
            def _(act):
                act.sem_inc(s["evac"], 2)
                act.sem_inc(s["silu"], 1)
                act.sem_inc(s["root"], 1)
                act.wait_ge(s["raw_zeroed"], 1)

                def to_raw(i, base, u):
                    n = i * 4 + (base + u)
                    act.wait_ge(s["proj_summed"], n + 5)
                    act.wait_ge(s["conv"], n + 1)
                    act.activation(raw[u % 2][:, 2:2 + NP_TOK], bankP[u % 2][:, 0:P], ACT.Identity, bias=bias(n))
                    act.activation(raw[u % 2][:, S_RAW:S_RAW + NS_TOK], bankS[u % 2][:], ACT.Identity,
                                   bias=bias(n)).then_inc(s["evac"], 1)

                def silu(n, out):
                    act.wait_ge(s["conv"], n + 3)
                    act.activation(out[:, 0:NP_TOK], cv[:, 0:NP_TOK], ACT.Silu)
                    act.activation(out[:, NP_TOK:T], cv[:, S_CV:S_CV + NS_TOK], ACT.Silu).then_inc(s["silu"], 1)

                with act.Fori(0, QK_TILES // 4) as i:
                    for u in range(4):
                        n = i * 4 + u
                        to_raw(i, 0, u)
                        act.wait_ge(s["normed"], n + 1)
                        silu(n, sl)
                        act.wait_ge(s["ones"], n + 2)
                        sc, bi = k.chan[:, bass.ds(n + V_L2S, 1)], k.chan[:, bass.ds(n + V_L2B, 1)]
                        act.activation(rt[:, 0:NP_TOK], k.bank[5][:, 0:P], ACT.Sqrt, bias=bi, scale=sc)
                        act.activation(rt[:, NP_TOK:T], k.bank[4][:], ACT.Sqrt, bias=bi, scale=sc
                                       ).then_inc(s["root"], 1)
                with act.Fori(0, V_TILES // 4) as i:
                    for u in range(4):
                        to_raw(i, QK_TILES, u)
                        wait_store(act, i, QK_TILES, u)
                        silu(i * 4 + (QK_TILES + u), ob[u % 2])
                for base, tiles, perm in ((T_MLQ, PERM_TILES, True), (T_Z, RASTER_TILES, False)):
                    with act.Fori(0, tiles // 4) as i:
                        for u in range(4):
                            n = i * 4 + (base + u)
                            act.wait_ge(s["proj_summed"], n + 5)
                            wait_store(act, i, base, u)
                            act.activation(ob[u % 2][:, 0:NP_TOK], bankP[u % 2][:, 0:P], ACT.Identity, bias=bias(n))
                            out, src = ob[u % 2][:, NP_TOK:T], bankS[u % 2][:]
                            if perm:
                                out = out.rearrange("p (c r) -> p r c", r=ROWS)
                                src = src.rearrange("p (r c) -> p r c", r=ROWS)
                            act.activation(out, src, ACT.Identity, bias=bias(n)).then_inc(s["evac"], 1)
                act.wait_ge(s["gates_summed"], 1)
                act.activation(gm[:, 0:NP_TOK], k.bank[5][0:16, 0:P], ACT.Copy)
                act.activation(gm[:, NP_TOK:T].rearrange("p (c r) -> p r c", r=ROWS),
                               k.bank[4][0:16, :].rearrange("p (r c) -> p r c", r=ROWS), ACT.Copy)
                act.drain().then_inc(s["gates_turned"], 1)

            @block.vector
            def _(dve):
                for b in range(2):
                    dve.memset(raw[b][:], 0.0)
                dve.drain().then_inc(s["raw_zeroed"], 1)
                dve.sem_inc(s["conv"], 2)
                dve.sem_inc(s["normed"], 1)

                def convolve(i, base, u):
                    n = i * 4 + (base + u)
                    dve.wait_ge(s["evac"], n + 3)
                    dve.wait_ge(s["silu"], n + 1)
                    for j in range(5):
                        tap = k.chan[:, bass.ds(n * 5 + (V_CONV + j), 1)]
                        if j == 0:
                            dve.tensor_scalar(cv[:], raw[u % 2][:, 0:CV], tap, None, ALU.mult)
                        else:
                            last = dve.scalar_tensor_tensor(out=cv[:], in0=raw[u % 2][:, j:j + CV], scalar=tap,
                                                            in1=cv[:], op0=ALU.mult, op1=ALU.add)
                        if j < 4:
                            dve.drain()
                    last.then_inc(s["conv"], 1)

                with dve.Fori(0, QK_TILES // 4) as i:
                    for u in range(4):
                        n = i * 4 + u
                        convolve(i, 0, u)
                        dve.wait_ge(s["silu"], n + 2)
                        dve.wait_ge(s["ones"], n + 1)
                        dve.tensor_tensor(sq[:], sl[:], sl[:], ALU.mult).then_inc(s["sq"], 1)
                        dve.wait_ge(s["root"], n + 2)
                        dve.reciprocal(rt[:], rt[:])
                        dve.drain()
                        wait_store(dve, i, 0, u)
                        dve.tensor_tensor(ob[u % 2][:], sl[:], rt[:], ALU.mult).then_inc(s["normed"], 1)
                with dve.Fori(0, V_TILES // 4) as i:
                    for u in range(4):
                        convolve(i, QK_TILES, u)
                dve.wait_ge(s["gates_summed"], 2)
                dve.tensor_tensor(k.gates[:], k.bank[6][:, 0:TT * 48].rearrange("p (t n) -> p t n", t=TT),
                                  all_heads(k.rowp[:, R_GB:R_GB + 48], TT), ALU.add)

            @block.sync
            def _(sp):
                for b in range(2):
                    sp.sem_inc(stored[b], 16)
                for base, tiles, sem, ahead in ((0, QK_TILES, "normed", 2), (QK_TILES, V_TILES, "silu", 2),
                                                (T_MLQ, PERM_TILES + RASTER_TILES, "evac", 3)):
                    with sp.Fori(0, tiles // 4) as i:
                        for u in range(4):
                            n = i * 4 + (base + u)
                            sp.wait_ge(s[sem], n + ahead)
                            sp.dma_start(k.d_proj[bass.ds(n, 1)].rearrange("a p t -> p (a t)"), ob[u % 2][:]
                                           ).then_inc(stored[u % 2], 16)
                for b in range(2):
                    sp.wait_ge(stored[b], 16 * (N_TILES // 2 + 1))


def phase_gates(nc, k):
    with ExitStack() as mem:
        def sb(name, shape):
            return mem.enter_context(nc.sbuf_tensor(name, shape, F32))
        x24 = sb("gate_x", [P, TT, 24])
        e24 = sb("gate_e", [P, TT, 24])
        l24 = sb("gate_l", [P, TT, 24])
        gg = sb("gate_gg", [P, TT, 24])
        al = sb("gate_al", [P, 16])
        bf = k.sem("gates_by_vector")
        ba = k.sem("gates_by_scalar")
        bp = k.sem("gates_by_tensor")
        with nc.Block() as block:
            @block.vector
            def _(dve):
                dve.tensor_tensor(x24[:, :, 0:16], k.gates[:, :, 16:32], all_heads(k.rowp[:, R_DT:R_DT + 16], TT),
                                  ALU.add)
                dve.scalar_tensor_tensor(out=x24[:, :, 16:24], in0=k.gates[:, :, 40:48], scalar=-1.0,
                                         in1=all_heads(k.rowp[:, R_FB:R_FB + 8], TT), op0=ALU.mult, op1=ALU.subtract)
                dve.tensor_tensor(k.ci[:], k.gates[:, :, 32:40], all_heads(k.rowp[:, R_IB:R_IB + 8], TT), ALU.add)
                dve.drain()
                dve.scalar_tensor_tensor(out=e24[:], in0=x24[:], scalar=-1.0, in1=x24[:], op0=ALU.mult, op1=ALU.min
                                         ).then_inc(bf, 1)
                dve.wait_ge(ba, 1)
                dve.scalar_tensor_tensor(out=gg[:], in0=x24[:], scalar=0.0, in1=l24[:], op0=ALU.max, op1=ALU.add)
                dve.drain()
                dve.scalar_tensor_tensor(out=gg[:, :, 0:16], in0=gg[:, :, 0:16], scalar=-1.0,
                                         in1=all_heads(al[:], TT), op0=ALU.mult, op1=ALU.mult)
                dve.tensor_scalar(gg[:, :, 16:24], gg[:, :, 16:24], -1.0, None, ALU.mult)
                dve.drain().then_inc(bf, 1)
                dve.wait_ge(bp, 1)
                cum = [k.bank[d][:, 0:TT * 24].rearrange("p (t n) -> p t n", t=TT) for d in range(3)]
                for d in range(2):
                    dve.tensor_copy(k.G[:, :, 8 * d:8 * d + 8], cum[d][:, :, 8 * d:8 * d + 8])
                    dve.tensor_copy(k.b_ml[:, :, 4 * d:4 * d + 4], cum[d][:, :, 16 + 4 * d:20 + 4 * d])
                dve.tensor_copy(k.g_tot[:], cum[2][:, :, 0:16])
                dve.tensor_copy(k.b_tot[:], cum[2][:, :, 16:24])
                dve.drain()
                dve.tensor_scalar(k.nG[:], k.G[:], -1.0, None, ALU.mult)
                dve.tensor_tensor(k.wS[:], k.g_tot[:], k.G[:], ALU.subtract)
                dve.tensor_tensor(k.ci[:], k.ci[:], k.b_ml[:], ALU.subtract)
                dve.drain().then_inc(bf, 1)
                dve.wait_ge(ba, 2)
                dve.tensor_scalar(k.neg_eG[:], k.eG[:], -1.0, None, ALU.mult)
                dve.tensor_tensor(k.bw[:], k.beta[:], k.wS[:], ALU.mult)

            @block.scalar
            def _(act):
                act.activation(k.beta[:], k.gates[:, :, 0:16], ACT.Sigmoid)
                act.activation(al[:], k.rowp[:, R_AL:R_AL + 16], ACT.Exp)
                act.wait_ge(bf, 1)
                act.activation(e24[:], e24[:], ACT.Exp)
                act.drain()
                act.activation(l24[:], e24[:], ACT.Ln, bias=1.0)
                act.drain().then_inc(ba, 1)
                act.wait_ge(bf, 3)
                act.activation(k.eG[:], k.G[:], ACT.Exp)
                act.activation(k.wS[:], k.wS[:], ACT.Exp)
                act.activation(k.eT[:], k.g_tot[:], ACT.Exp)
                act.drain().then_inc(ba, 1)

            @block.tensor
            def _(pe):
                pe.wait_ge(bf, 2)
                for d, lhs in enumerate((k.tri[0], k.tri[1], k.ones)):
                    mm = pe.matmul(k.bank[d][:, 0:TT * 24], lhs, gg[:].rearrange("p t n -> p (t n)"),
                                   start=True, stop=True)
                mm.then_inc(bp, 1)


A_FILLS = (["kT", "G", "KK", "L1"] + [f"{x}{s}" for s in LEVELS[1:] for x in ("Y", "YX")] + ["KS", "P", "O"])
B_FILLS = (["vT", "QK"] + [f"XY{s}" for s in LEVELS[1:-1]] + ["QS", "S"])


def phase_deltanet(nc, k):
    with ExitStack() as mem:
        def sb(name, shape):
            return mem.enter_context(nc.sbuf_tensor(name, shape, F32))

        def quads(name):
            return [sb(f"{name}{q}", [P, 4, P]) for q in range(4)]
        staged = [sb(f"dn_staged{d}", [P, 24, P]) for d in range(2)]
        ktok, vtok, dg, DT, NT, sc = (quads(n) for n in ("ktok", "vtok", "diagG", "decayT", "LT", "scoresT"))
        X, XT, Y, tmp, R, vn, vs = (quads(n) for n in ("X", "XT", "Y", "tmp", "R", "vnew", "vweighted"))
        S = [[sb(f"S{'ps'[x]}{q}", [P, 4, P]) for q in range(4)] for x in range(2)]
        A = [Bank(k.bank[q], k.sem(f"dnA_filled{q}"), k.sem(f"dnA_emptied{q}"), A_FILLS) for q in range(4)]
        B = [Bank(k.bank[4 + q], k.sem(f"dnB_filled{q}"), k.sem(f"dnB_emptied{q}"), B_FILLS) for q in range(4)]
        landed = [k.sem(f"dn_landed{d}") for d in range(2)]
        used = [k.sem(f"dn_stage_used{d}") for d in range(2)]
        zeroed, state_in, prompt_done, state_out = (k.sem(n) for n in ("dn_zeroed", "dn_state_in", "dn_prompt_done",
                                                                       "dn_state_out"))
        dg_ready = [k.sem(f"dg_ready{q}") for q in range(4)]
        QUADS = [(q, q % 2, 4 * (q // 2)) for q in range(4)]

        def steps(eng, body):
            body(0, (0, 0), 0)
            with eng.Fori(0, TT - 1) as i:
                body(i + 1, (i + 1, i * -1 + (TT - 1)), 1)

        with nc.Block() as block:
            @block.sync
            def _(sp):
                for q, d, h0 in QUADS:
                    sp.dma_start(S[1][q][:], k.d_sdn[d, h0:h0 + 4].rearrange("h p n -> p h n")).then_inc(state_in, 16)

                def load(step, tiles, _):
                    for d in range(2):
                        if not isinstance(step, int):
                            sp.wait_ge(used[d], step * 2)
                        sp.dma_start(staged[d][:], k.d_proj.rearrange("m p t -> p m t")[
                            :, 0:24, bass.ds(tiles[d] * P, P)]).then_inc(landed[d], 16)
                steps(sp, load)
                sp.wait_ge(prompt_done, 4)
                for q, d, h0 in QUADS:
                    sp.dma_start(k.o_sdn[d, h0:h0 + 4].rearrange("h p n -> p h n"), S[0][q][:]
                                 ).then_inc(state_out, 16)
                sp.wait_ge(state_out, 64)

            @block.gpsimd
            def _(pool):
                pool.memset(k.o_dn[:], 0.0)
                for q in range(4):
                    pool.memset(S[0][q][:], 0.0)
                pool.drain().then_inc(zeroed, 1)

                def diagonals(step, tiles, _):
                    for q, d, h0 in QUADS:
                        if not isinstance(step, int):
                            A[q].wait_filled(pool, step + -1, "G")
                        c = d * 8 + h0
                        pool.tensor_tensor(dg[q][:], all_heads(k.ident), per_head(col(k.G[:], tiles[d], c, c + 4), P),
                                           ALU.mult).then_inc(dg_ready[q], 1)
                steps(pool, diagonals)

            @block.tensor
            def _(pe):
                def fill(bank, step, name, args, **more):
                    bank.wait_free(pe, step, name)
                    for h in range(4):
                        terms = args(h)
                        for n, (lhs, rhs) in enumerate(terms):
                            mm = pe.matmul(bank.t[:, h * P:(h + 1) * P], lhs, rhs, start=(n == 0),
                                           stop=(n == len(terms) - 1))
                    mm.then_inc(bank.filled, 1)

                def turn(bank, step, name, src):
                    bank.wait_free(pe, step, name)
                    for h in range(4):
                        mm = pe.transpose(bank.t[:, h * P:(h + 1) * P], src(h), k.ident)
                    mm.then_inc(bank.filled, 1)

                def body(step, tiles, x):
                    for q, d, h0 in QUADS:
                        pe.wait_ge(landed[d], step * 16 + 16)
                        turn(A[q], step, "kT", lambda h: staged[d][:, 8 + h0 + h, :])
                        turn(B[q], step, "vT", lambda h: staged[d][:, 16 + h0 + h, :])
                    for q, d, h0 in QUADS:
                        pe.wait_ge(dg_ready[q], step + 1)
                        fill(A[q], step, "G", lambda h: [(k.ones, dg[q][:, h, :]), (k.ident, k.neg[d])])
                    for q, d, h0 in QUADS:
                        kh = lambda h: staged[d][:, 8 + h0 + h, :]
                        fill(A[q], step, "KK", lambda h: [(kh(h), kh(h))])
                        fill(B[q], step, "QK", lambda h: [(kh(h), staged[d][:, h0 + h, :])])
                    for q, d, h0 in QUADS:
                        A[q].wait_emptied(pe, step, "KK")
                        fill(A[q], step, "L1", lambda h: [(NT[q][:, h, :], k.ident)])
                    for s in LEVELS[1:]:
                        for q, d, h0 in QUADS:
                            if s > 2:
                                B[q].wait_emptied(pe, step, f"XY{s // 2}")
                            fill(A[q], step, f"Y{s}", lambda h: [(NT[q][:, h, :], X[q][:, h, :])])
                        for q, d, h0 in QUADS:
                            A[q].wait_emptied(pe, step, f"Y{s}")
                            if s != LEVELS[-1]:
                                fill(B[q], step, f"XY{s}", lambda h: [(XT[q][:, h, :], Y[q][:, h, :])])
                            fill(A[q], step, f"YX{s}", lambda h: [(Y[q][:, h, :], XT[q][:, h, :])])
                    pe.wait_ge(zeroed, 1) if x == 0 else pe.wait_ge(state_in, 64)
                    for q, d, h0 in QUADS:
                        fill(B[q], step, "QS", lambda h: [(staged[d][:, h0 + h, :], S[x][q][:, h, :])])
                        fill(A[q], step, "KS", lambda h: [(staged[d][:, 8 + h0 + h, :], S[x][q][:, h, :])])
                    for q, d, h0 in QUADS:
                        A[q].wait_filled(pe, step, "KS")
                        pe.sem_inc(used[d], 1)
                        fill(A[q], step, "P", lambda h: [(XT[q][:, h, :], R[q][:, h, :])])
                    for q, d, h0 in QUADS:
                        fill(A[q], step, "O", lambda h: [(sc[q][:, h, :], vn[q][:, h, :])])
                        fill(B[q], step, "S", lambda h: [(ktok[q][:, h, :], vs[q][:, h, :])])
                steps(pe, body)

            @block.scalar
            def _(act):
                def body(step, tiles, x):
                    for q, d, h0 in QUADS:
                        A[q].wait_filled(act, step, "kT")
                        act.activation(ktok[q][:], h4(A[q].t[:]), ACT.Copy).then_inc(A[q].emptied, 1)
                        B[q].wait_filled(act, step, "vT")
                        act.activation(vtok[q][:], h4(B[q].t[:]), ACT.Copy).then_inc(B[q].emptied, 1)
                    for q, d, h0 in QUADS:
                        A[q].wait_filled(act, step, "G")
                        for h in range(4):
                            c = d * 8 + h0 + h
                            ex = act.activation(DT[q][:, h, :], A[q].t[:, h * P:(h + 1) * P], ACT.Exp,
                                                bias=col(k.nG[:], tiles[d], c, c + 1))
                        ex.then_inc(A[q].emptied, 1)
                    for q, d, h0 in QUADS:
                        A[q].wait_filled(act, step, "P")
                        for h in range(4):
                            c = d * 8 + h0 + h
                            act.activation(vn[q][:, h, :], A[q].t[:, h * P:(h + 1) * P], ACT.Copy,
                                           scale=col(k.beta[:], tiles[d], c, c + 1))
                            ex = act.activation(vs[q][:, h, :], A[q].t[:, h * P:(h + 1) * P], ACT.Copy,
                                                scale=col(k.bw[:], tiles[d], c, c + 1))
                        ex.then_inc(A[q].emptied, 1)
                steps(act, body)

            @block.vector
            def _(dve):
                dve.wait_ge(zeroed, 1)
                dve.wait_ge(state_in, 64)

                def body(step, tiles, x):
                    for q, d, h0 in QUADS:
                        A[q].wait_filled(dve, step, "KK")
                        A[q].wait_emptied(dve, step, "G")
                        for h in range(4):
                            c = d * 8 + h0 + h
                            op = dve.scalar_tensor_tensor(
                                out=NT[q][:, h, :], in0=A[q].t[:, h * P:(h + 1) * P],
                                scalar=col(k.beta[:], tiles[d], c, c + 1), in1=DT[q][:, h, :],
                                op0=ALU.mult, op1=ALU.mult)
                        op.then_inc(A[q].emptied, 1)
                        B[q].wait_filled(dve, step, "QK")
                        dve.tensor_tensor(sc[q][:], h4(B[q].t[:]), DT[q][:], ALU.mult).then_inc(B[q].emptied, 1)
                    for q, d, h0 in QUADS:
                        A[q].wait_filled(dve, step, "L1")
                        dve.tensor_tensor(tmp[q][:], NT[q][:], all_heads(k.level(d, 0)), ALU.mult)
                        dve.tensor_tensor(Y[q][:], h4(A[q].t[:]), all_heads(k.level(1 - d, 0)), ALU.mult)
                        dve.drain()
                        dve.tensor_tensor(XT[q][:], all_heads(k.ident), tmp[q][:], ALU.subtract)
                        dve.tensor_tensor(X[q][:], all_heads(k.ident), Y[q][:], ALU.subtract
                                          ).then_inc(A[q].emptied, 1)
                    for n, s in enumerate(LEVELS[1:], 1):
                        for q, d, h0 in QUADS:
                            A[q].wait_filled(dve, step, f"Y{s}")
                            dve.tensor_tensor(Y[q][:], h4(A[q].t[:]), all_heads(k.level(1 - d, n)), ALU.mult
                                              ).then_inc(A[q].emptied, 1)
                        for q, d, h0 in QUADS:
                            if s != LEVELS[-1]:
                                B[q].wait_filled(dve, step, f"XY{s}")
                                dve.tensor_tensor(X[q][:], X[q][:], h4(B[q].t[:]), ALU.subtract
                                                  ).then_inc(B[q].emptied, 1)
                            A[q].wait_filled(dve, step, f"YX{s}")
                            dve.tensor_tensor(XT[q][:], XT[q][:], h4(A[q].t[:]), ALU.subtract
                                              ).then_inc(A[q].emptied, 1)
                    for q, d, h0 in QUADS:
                        B[q].wait_filled(dve, step, "QS")
                        if x == 0 and d == 1:
                            dve.drain()
                        for h in range(4):
                            c = d * 8 + h0 + h
                            o = col(k.o_dn[:], tiles[d], (h0 + h) * P, (h0 + h + 1) * P)
                            op = dve.scalar_tensor_tensor(out=o, in0=B[q].t[:, h * P:(h + 1) * P],
                                                          scalar=col(k.eG[:], tiles[d], c, c + 1), in1=o,
                                                          op0=ALU.mult, op1=ALU.add)
                        op.then_inc(B[q].emptied, 1)
                        A[q].wait_filled(dve, step, "KS")
                        A[q].wait_emptied(dve, step, "kT")
                        B[q].wait_emptied(dve, step, "vT")
                        for h in range(4):
                            c = d * 8 + h0 + h
                            op = dve.scalar_tensor_tensor(out=R[q][:, h, :], in0=A[q].t[:, h * P:(h + 1) * P],
                                                          scalar=col(k.neg_eG[:], tiles[d], c, c + 1),
                                                          in1=vtok[q][:, h, :], op0=ALU.mult, op1=ALU.add)
                        op.then_inc(A[q].emptied, 1)
                    dve.drain()
                    for q, d, h0 in QUADS:
                        A[q].wait_filled(dve, step, "O")
                        if x == 0 and d == 1:
                            dve.drain()
                        o = col(k.o_dn[:], tiles[d], h0 * P, (h0 + 4) * P)
                        dve.tensor_tensor(o, o, A[q].t[:], ALU.add).then_inc(A[q].emptied, 1)
                        B[q].wait_filled(dve, step, "S")
                        for h in range(4):
                            c = d * 8 + h0 + h
                            op = dve.scalar_tensor_tensor(out=S[x][q][:, h, :], in0=S[x][q][:, h, :],
                                                          scalar=col(k.eT[:], tiles[d], c, c + 1),
                                                          in1=B[q].t[:, h * P:(h + 1) * P], op0=ALU.mult, op1=ALU.add)
                        op.then_inc(B[q].emptied, 1)
                    dve.drain()
                    if x == 0:
                        dve.sem_inc(prompt_done, 4)
                steps(dve, body)


M_FILLS = {"A": ["kT", "QK", "NP1", "NP3"], "B": ["v01", "NQ0", "NQ2", "S0", "S2"],
           "C": ["v23", "NQ1", "NQ3", "S1", "S3"], "D": ["Cbc", "Mbc", "NP0", "NP2"]}


def phase_mlstm(nc, k):
    DA = DV_ML + 1
    with ExitStack() as mem:
        def sb(name, shape):
            return mem.enter_context(nc.sbuf_tensor(name, shape, F32))

        def dirs(name, shape):
            return [sb(f"{name}{d}", shape) for d in range(2)]
        staged = dirs("ml_staged", [P, 16, P])
        ktok, dg, dgM, ET, PT, kw = (dirs(n, [P, 4, P]) for n in ("ml_ktok", "diagC", "diagM", "expT", "pT", "kweighted"))
        vtok = dirs("ml_vtok", [P, 4, DA])
        nu = dirs("numerator", [P, 4, DA])
        S = [dirs(f"C{'ps'[x]}", [P, 4, DA]) for x in range(2)]
        m = [dirs(f"m{'ps'[x]}", [P, 4]) for x in range(2)]
        M, nM, mx, nMl, inter, enm, carry, wS, rden, bM = (
            dirs(n, [P, 4]) for n in ("M", "negM", "maxC", "negMend", "inter", "exp_neg_m", "carry", "wend",
                                      "rden", "bM"))
        bank = [{f: Bank(k.bank[4 * d + n], k.sem(f"ml{f}_filled{d}"), k.sem(f"ml{f}_emptied{d}"), M_FILLS[f])
                 for n, f in enumerate("ABCD")} for d in range(2)]
        landed = [k.sem(f"ml_landed{d}") for d in range(2)]
        sems = ("ready", "dgC", "dgM", "max", "expo", "scalars", "kw", "nu", "den")
        s = [{n: k.sem(f"ml_{n}{d}") for n in sems} for d in range(2)]
        state_in, state_out, prompt_done = k.sem("ml_state_in"), k.sem("ml_state_out"), k.sem("ml_prompt_done")
        END = (P - 1, 0)

        def steps(eng, body):
            body(0, (0, 0), 0)
            with eng.Fori(0, TT - 1) as i:
                body(i + 1, (i + 1, i * -1 + (TT - 1)), 1)

        def gate(t3, tiles, d, h=None):
            a, b = (4 * d, 4 * d + 4) if h is None else (4 * d + h, 4 * d + h + 1)
            return col(t3[:], tiles[d], a, b)

        with nc.Block() as block:
            @block.sync
            def _(sp):
                for d in range(2):
                    sp.dma_start(S[1][d][:, :, 0:DV_ML], k.d_smc[d].rearrange("h p n -> p h n")).then_inc(state_in, 16)
                    for h in range(4):
                        sp.dma_start(S[1][d][:, h, DV_ML:DA], k.d_smn[d, h:h + 1, :].rearrange("a p -> p a")
                                     ).then_inc(state_in, 16)

                def load(step, tiles, _):
                    for d in range(2):
                        if not isinstance(step, int):
                            bank[d]["A"].wait_filled(sp, step + -1, "NP3")
                        sp.dma_start(staged[d][:], k.d_proj.rearrange("m p t -> p m t")[
                            :, T_MLQ:T_MLQ + 16, bass.ds(tiles[d] * P, P)]).then_inc(landed[d], 16)
                steps(sp, load)
                sp.wait_ge(prompt_done, 1)
                for d in range(2):
                    sp.dma_start(k.o_smc[d].rearrange("h p n -> p h n"), S[0][d][:, :, 0:DV_ML]).then_inc(state_out, 16)
                    for h in range(4):
                        sp.dma_start(k.o_smn[d, h:h + 1, :].rearrange("a p -> p a"), S[0][d][:, h, DV_ML:DA]
                                     ).then_inc(state_out, 16)
                    sp.dma_start(k.o_smm[d:d + 1, :], m[0][d][0:1, :]).then_inc(state_out, 16)
                sp.wait_ge(state_out, 16 * 12)

            @block.gpsimd
            def _(pool):
                for d in range(2):
                    pool.memset(vtok[d][:], 1.0)
                    pool.memset(S[0][d][:], 0.0)
                    pool.memset(m[0][d][:], 0.0)
                pool.memset(k.o_ml[:], 0.0)
                pool.drain().then_inc(s[0]["ready"], 1)

                def body(step, tiles, _):
                    for d in range(2):
                        if not isinstance(step, int):
                            bank[d]["D"].wait_filled(pool, step + -1, "Cbc")
                        pool.tensor_tensor(dg[d][:], all_heads(k.ident), per_head(gate(k.ci, tiles, d), P), ALU.mult
                                           ).then_inc(s[d]["dgC"], 1)
                steps(pool, body)

            @block.tensor
            def _(pe):
                pe.wait_ge(s[0]["ready"], 1)

                def body(step, tiles, x):
                    for d in range(2):
                        b = bank[d]
                        pe.wait_ge(landed[d], step * 16 + 16)
                        b["A"].wait_free(pe, step, "kT")
                        for h in range(4):
                            mm = pe.transpose(b["A"].t[:, h * P:(h + 1) * P], staged[d][:, 4 + h, :], k.ident)
                        mm.then_inc(b["A"].filled, 1)
                        for n, f in enumerate("BC"):
                            b[f].wait_free(pe, step, ("v01", "v23")[n])
                            for j in range(4):
                                mm = pe.transpose(b[f].t[:, j * P:(j + 1) * P], staged[d][:, 8 + 4 * n + j, :], k.ident)
                            mm.then_inc(b[f].filled, 1)
                        pe.wait_ge(s[d]["dgC"], step + 1)
                        b["D"].wait_free(pe, step, "Cbc")
                        for h in range(4):
                            o = b["D"].t[:, h * P:(h + 1) * P]
                            pe.matmul(o, k.ones, dg[d][:, h, :], start=True, stop=False)
                            mm = pe.matmul(o, k.ident, k.neg[1 - d], start=False, stop=True)
                        mm.then_inc(b["D"].filled, 1)
                    for d in range(2):
                        b = bank[d]
                        b["A"].wait_free(pe, step, "QK")
                        for h in range(4):
                            mm = pe.matmul(b["A"].t[:, h * P:(h + 1) * P], staged[d][:, 4 + h, :], staged[d][:, h, :],
                                           start=True, stop=True)
                        mm.then_inc(b["A"].filled, 1)
                    for d in range(2):
                        b = bank[d]
                        pe.wait_ge(s[d]["dgM"], step + 1)
                        b["D"].wait_free(pe, step, "Mbc")
                        for h in range(4):
                            o = b["D"].t[:, h * P:(h + 1) * P]
                            pe.matmul(o, k.ones, dgM[d][:, h, :], start=True, stop=False)
                            mm = pe.matmul(o, k.ident, k.neg[d], start=False, stop=True)
                        mm.then_inc(b["D"].filled, 1)
                    if x == 1:
                        pe.wait_ge(state_in, 16 * 10)
                    for h in range(4):
                        for d in range(2):
                            b = bank[d]
                            fq, fp = ("B", "D") if h % 2 == 0 else ("C", "A")
                            b[fq].wait_free(pe, step, f"NQ{h}")
                            if h == 0:
                                b["C"].wait_free(pe, step, "NQ1")
                            pe.matmul(b[fq].t[:, 0:DA], staged[d][:, h, :], S[x][d][:, h, :], start=True, stop=True
                                      ).then_inc(b[fq].filled, 1)
                            b["A"].wait_emptied(pe, step, "QK")
                            b[fp].wait_free(pe, step, f"NP{h}")
                            pe.matmul(b[fp].t[:, 0:DA], PT[d][:, h, :], vtok[d][:, h, :], start=True, stop=True
                                      ).then_inc(b[fp].filled, 1)
                    for h in range(4):
                        for d in range(2):
                            b = bank[d]
                            f = "BC"[h % 2]
                            pe.wait_ge(s[d]["kw"], step + 1)
                            b[f].wait_free(pe, step, f"S{h}")
                            pe.matmul(b[f].t[:, 0:DA], kw[d][:, h, :], vtok[d][:, h, :], start=True, stop=True
                                      ).then_inc(b[f].filled, 1)
                steps(pe, body)

            @block.scalar
            def _(act):
                act.wait_ge(s[0]["ready"], 1)

                def body(step, tiles, x):
                    for d in range(2):
                        b = bank[d]
                        b["A"].wait_filled(act, step, "kT")
                        if not isinstance(step, int):
                            act.wait_ge(s[d]["kw"], step)
                        act.activation(ktok[d][:], h4(b["A"].t[:]), ACT.Copy).then_inc(b["A"].emptied, 1)
                        for n, f in enumerate("BC"):
                            b[f].wait_filled(act, step, ("v01", "v23")[n])
                            act.activation(vtok[d][:, 2 * n:2 * n + 2, 0:DV_ML],
                                           b[f].t[:].rearrange("p (h n) -> p h n", h=2), ACT.Copy
                                           ).then_inc(b[f].emptied, 1)
                    for d in range(2):
                        b = bank[d]
                        b["D"].wait_filled(act, step, "Mbc")
                        if not isinstance(step, int):
                            act.wait_ge(s[d]["scalars"], step)
                        act.activation(nMl[d][:].unsqueeze(2), h4(b["D"].t[:])[:, :, END[d]:END[d] + 1], ACT.Copy)
                        for h in range(4):
                            act.activation(ET[d][:, h, :], b["D"].t[:, h * P:(h + 1) * P], ACT.Exp,
                                           bias=gate(k.ci, tiles, d, h))
                        act.drain().then_inc(b["D"].emptied, 1)
                    for d in range(2):
                        act.wait_ge(s[d]["expo"], step + 1)
                        for t4 in (inter, enm, carry, wS):
                            act.activation(t4[d][:], t4[d][:], ACT.Exp)
                        act.drain().then_inc(s[d]["scalars"], 1)
                    for h in range(4):
                        for d in range(2):
                            fq = "BC"[h % 2]
                            bank[d][fq].wait_filled(act, step, f"NQ{h}")
                            act.activation(nu[d][:, h, :], bank[d][fq].t[:, 0:DA], ACT.Copy,
                                           scale=inter[d][:, h:h + 1]).then_inc(bank[d][fq].emptied, 1)
                steps(act, body)

            @block.vector
            def _(dve):
                dve.wait_ge(s[0]["ready"], 1)
                for d in range(2):
                    dve.tensor_copy(m[1][d][:], k.rowp[:, R_M0 + 4 * d:R_M0 + 4 * d + 4])
                dve.drain()

                def body(step, tiles, x):
                    for d in range(2):
                        b = bank[d]
                        b["D"].wait_filled(dve, step, "Cbc")
                        dve.tensor_reduce(mx[d][:], h4(b["D"].t[:]), AX.X, ALU.max).then_inc(b["D"].emptied, 1)
                        dve.drain()
                        dve.tensor_tensor(M[d][:], mx[d][:], m[x][d][:], ALU.max)
                        dve.drain()
                        dve.tensor_scalar(nM[d][:], M[d][:], -1.0, None, ALU.mult)
                        dve.tensor_tensor(inter[d][:], m[x][d][:], M[d][:], ALU.subtract)
                        dve.tensor_tensor(bM[d][:], M[d][:], gate(k.b_ml, tiles, d), ALU.add)
                        dve.drain()
                        dve.tensor_scalar(enm[d][:], bM[d][:], -1.0, None, ALU.mult)
                        dve.tensor_tensor(dgM[d][:], all_heads(k.ident), per_head(nM[d][:], P), ALU.mult
                                          ).then_inc(s[d]["dgM"], 1)
                    for d in range(2):
                        b = bank[d]
                        b["D"].wait_emptied(dve, step, "Mbc")
                        dve.tensor_tensor(carry[d][:], m[x][d][:], nMl[d][:], ALU.add)
                        dve.tensor_tensor(wS[d][:], gate(k.ci, tiles, d), nMl[d][:], ALU.add)
                        dve.drain().then_inc(s[d]["expo"], 1)
                        dve.tensor_tensor(m[x][d][:], gate(k.b_tot, tiles, d), nMl[d][:], ALU.subtract)
                        b["A"].wait_filled(dve, step, "QK")
                        dve.scalar_tensor_tensor(out=PT[d][:], in0=h4(b["A"].t[:]), scalar=K_SCALE, in1=ET[d][:],
                                                 op0=ALU.mult, op1=ALU.mult).then_inc(b["A"].emptied, 1)
                    for d in range(2):
                        dve.wait_ge(s[d]["scalars"], step + 1)
                        bank[d]["A"].wait_emptied(dve, step, "kT")
                        dve.tensor_scalar(wS[d][:], wS[d][:], K_SCALE, None, ALU.mult)
                        dve.drain()
                        dve.tensor_tensor(kw[d][:], ktok[d][:], per_head(wS[d][:], P), ALU.mult
                                          ).then_inc(s[d]["kw"], 1)
                    for h in range(4):
                        for d in range(2):
                            b = bank[d]
                            fq, fp = ("B", "D") if h % 2 == 0 else ("C", "A")
                            b[fq].wait_emptied(dve, step, f"NQ{h}")
                            b[fp].wait_filled(dve, step, f"NP{h}")
                            dve.tensor_tensor(nu[d][:, h, :], nu[d][:, h, :], b[fp].t[:, 0:DA], ALU.add
                                              ).then_inc(b[fp].emptied, 1)
                    dve.drain()
                    for d in range(2):
                        dve.tensor_tensor(rden[d][:].unsqueeze(2), nu[d][:, :, DV_ML:DA], nu[d][:, :, DV_ML:DA], ALU.mult)
                        dve.tensor_scalar(mx[d][:].unsqueeze(2), nu[d][:, :, DV_ML:DA], -1.0, None, ALU.mult)
                        dve.drain()
                        dve.tensor_tensor(rden[d][:].unsqueeze(2), nu[d][:, :, DV_ML:DA], mx[d][:].unsqueeze(2), ALU.max)
                        dve.drain()
                        dve.tensor_tensor(rden[d][:], rden[d][:], enm[d][:], ALU.max)
                        dve.drain()
                        dve.reciprocal(rden[d][:], rden[d][:])
                        dve.drain()
                        for h in range(4):
                            o = col(k.o_ml[:], tiles[d], h * DV_ML, (h + 1) * DV_ML)
                            dve.scalar_tensor_tensor(out=o, in0=nu[d][:, h, 0:DV_ML], scalar=rden[d][:, h:h + 1],
                                                     in1=o, op0=ALU.mult, op1=ALU.add)
                        dve.drain()
                    for h in range(4):
                        for d in range(2):
                            f = bank[d]["BC"[h % 2]]
                            f.wait_filled(dve, step, f"S{h}")
                            dve.scalar_tensor_tensor(out=S[x][d][:, h, :], in0=S[x][d][:, h, :],
                                                     scalar=carry[d][:, h:h + 1], in1=f.t[:, 0:DA],
                                                     op0=ALU.mult, op1=ALU.add).then_inc(f.emptied, 1)
                    dve.drain()
                    if x == 0:
                        dve.sem_inc(prompt_done, 1)
                steps(dve, body)


def phase_branch_outputs(nc, k):
    with ExitStack() as mem:
        def sb(name, shape):
            return mem.enter_context(nc.sbuf_tensor(name, shape, F32))
        gate = [sb("z_gate", [P, 8, T]), sb("mo_gate", [P, 8, T])]
        sq = sb("o_squares", [P, TT, 1024])
        ms = [sb("dn_ms", [P, TT * H_DN]), sb("ml_ms", [P, TT * H_ML])]
        rs = [sb("dn_rs", [P, TT * H_DN]), sb("ml_rs", [P, TT * H_ML])]
        gate_in = [k.sem("z_in"), k.sem("mo_in")]
        gated, meaned, rooted, scaled, turned, read = (k.sem(n) for n in ("bo_gated", "bo_meaned", "bo_rooted",
                                                                         "bo_scaled", "bo_turned", "bo_read"))
        o = [k.o_dn, k.o_ml]
        heads = [H_DN, H_ML]
        with nc.Block() as block:
            @block.sync
            def _(sp):
                for b, t0 in enumerate((T_Z, T_MO)):
                    sp.dma_start(gate[b][:], k.d_proj[t0:t0 + 8].rearrange("m p t -> p m t")).then_inc(gate_in[b], 16)

            @block.scalar
            def _(act):
                for b in range(2):
                    act.wait_ge(meaned, b + 1)
                    act.activation(rs[b][:], ms[b][:], ACT.Sqrt).then_inc(rooted, 1)
                for b, f in enumerate((ACT.Silu, ACT.Sigmoid)):
                    act.wait_ge(gate_in[b], 16)
                    act.activation(gate[b][:], gate[b][:], f).then_inc(gated, 1)

            @block.vector
            def _(dve):
                for b in range(2):
                    per = 1024 // heads[b]
                    dve.tensor_tensor(sq[:], o[b][:], o[b][:], ALU.mult)
                    dve.drain()
                    dve.tensor_reduce(ms[b][:], sq[:].rearrange("p t (h n) -> p (t h) n", n=per), AX.X, ALU.add)
                    dve.drain()
                    dve.tensor_scalar(ms[b][:], ms[b][:], 1.0 / per, EPS, ALU.mult, ALU.add).then_inc(meaned, 1)
                for b in range(2):
                    per = 1024 // heads[b]
                    dve.wait_ge(rooted, b + 1)
                    dve.reciprocal(rs[b][:], rs[b][:])
                    dve.drain()
                    v = o[b][:].rearrange("p t (h n) -> p (t h) n", n=per)
                    dve.tensor_tensor(v, v, rs[b][:].unsqueeze(2).to_broadcast([P, TT * heads[b], per]), ALU.mult
                                      ).then_inc(scaled, 1)
                dve.wait_ge(gated, 2)
                n = 0
                for b in range(2):
                    y = (k.yaT, k.ybT)[b]
                    for t in range(TT):
                        for half in range(2):
                            bank = k.bank[n % 8]
                            dve.wait_ge(turned, n + 1)
                            for j in range(4):
                                c = 4 * half + j
                                gain = k.chan[:, V_DNG:V_DNG + 1] if b == 0 else k.chan[:, V_MLG + c:V_MLG + c + 1]
                                src = bank[:, j * P:(j + 1) * P]
                                if b == 1 and t > 0:
                                    w0, wn = (t - 1) * (P // ROWS), P // ROWS
                                    src = src.rearrange("p (c r) -> p c r", r=ROWS)

                                    def raster(a):
                                        return a[:, c, NP_TOK:T].rearrange("p (r c) -> p c r", r=ROWS)[:, w0:w0 + wn, :]
                                    out, g = raster(y), raster(gate[b])
                                else:
                                    out, g = y[:, c, t * P:(t + 1) * P], gate[b][:, c, t * P:(t + 1) * P]
                                op = dve.scalar_tensor_tensor(out=out, in0=src, scalar=gain, in1=g,
                                                              op0=ALU.mult, op1=ALU.mult)
                            op.then_inc(read, 1)
                            n += 1

            @block.tensor
            def _(pe):
                n = 0
                for b in range(2):
                    pe.wait_ge(scaled, b + 1)
                    for t in range(TT):
                        for half in range(2):
                            if n >= 8:
                                pe.wait_ge(read, n - 7)
                            for j in range(4):
                                c = 4 * half + j
                                mm = pe.transpose(k.bank[n % 8][:, j * P:(j + 1) * P], o[b][:, t, c * P:(c + 1) * P],
                                                  k.ident)
                            mm.then_inc(turned, 1)
                            n += 1


def phase_merge(nc, k):
    with ExitStack() as mem:
        def sb(name, shape):
            return mem.enter_context(nc.sbuf_tensor(name, shape, F32))
        w = sb("merge_ring", [P, 4, KT, P])
        yT = sb("yT", [P, KT, T])
        gt = [sb(f"merge_gates{b}", [P, 2, T]) for b in range(2)]
        ta = [sb(f"merge_a{b}", [P, T]) for b in range(2)]
        tb = [sb(f"merge_b{b}", [P, T]) for b in range(2)]
        xin = sb("x_again", [P, D])
        s = {n: k.sem(n) for n in ("merge_summed", "merge_sig", "merge_read", "merged", "out_summed", "out_read",
                                   "xa_landed", "xa_turned", "xa_read")}
        landed = [k.sem(f"merge_landed{u}") for u in range(4)]
        gates_in = [k.sem(f"merge_gates_in{u}") for u in range(2)]
        with nc.Block() as block:
            @block.sync
            def _(sp):
                with sp.Fori(0, TT) as t:
                    sp.wait_ge(s["xa_turned"], t + 1)
                    sp.dma_start(xin[:], k.d_x[bass.ds(t * P, P), :]).then_inc(s["xa_landed"], 16)
                for half, (src, sem) in enumerate(((k.d_wup, "merge_summed"), (k.d_wout, "out_summed"))):
                    with sp.Fori(0, KT // 4) as i:
                        for u in range(4):
                            if half == 1:
                                sp.wait_ge(s["merge_summed"], KT + 1 + u)
                            sp.wait_ge(s[sem], i * 4 + u + 1)
                            sp.dma_start(w[:, u], src[bass.ds(i * 4 + u, 1)].rearrange("a p k n -> p (a k) n")
                                         ).then_inc(landed[u], 16)

            @block.gpsimd
            def _(pool):
                with pool.Fori(0, KT // 4) as i:
                    for u in range(4):
                        pool.wait_ge(s["merge_read"], i * 4 + u + 1)
                        for j, t0 in enumerate((T_GA, T_GB)):
                            pool.dma_start(gt[u % 2][:, j, :], k.d_proj[bass.ds(i * 4 + (u + t0), 1)].rearrange(
                                "a p t -> p (a t)")).then_inc(gates_in[u % 2], 16)

            @block.tensor
            def _(pe):
                pe.sem_inc(s["xa_turned"], 1)
                pe.sem_inc(s["merge_summed"], 4)
                pe.sem_inc(s["out_summed"], 4)
                with pe.Fori(0, TT) as t:
                    pe.wait_ge(s["xa_landed"], t * 16 + 16)
                    pe.wait_ge(s["xa_read"], t + 1)
                    for kk in range(KT):
                        mm = pe.transpose(k.bank[kk // 4][:, (kk % 4) * P:(kk % 4 + 1) * P],
                                          xin[:, kk * P:(kk + 1) * P], k.ident)
                    mm.then_inc(s["xa_turned"], 1)
                pe.wait_ge(s["xa_read"], TT + 1)
                with pe.Fori(0, KT // 4) as i:
                    for u in range(4):
                        pe.wait_ge(landed[u], i * 16 + 16)
                        pe.wait_ge(s["merge_read"], i * 4 + u + 1)
                        for j, y in enumerate((k.yaT, k.ybT)):
                            for part, (bank, off, lo, hi) in enumerate((
                                    (k.bank[3 * (u % 2) + j], 0, NP_TOK, T),
                                    (k.bank[3 * (u % 2) + 2], j * P, 0, NP_TOK))):
                                for kk in range(8):
                                    mm = pe.matmul(bank[:, off:off + hi - lo], w[:, u, 8 * j + kk, :],
                                                   y[:, kk, lo:hi], start=(kk == 0), stop=(kk == 7))
                        mm.then_inc(s["merge_summed"], 1)
                pe.wait_ge(s["merged"], KT)
                with pe.Fori(0, KT // 4) as i:
                    for u in range(4):
                        pe.wait_ge(landed[u], i * 16 + (16 * (KT // 4) + 16))
                        pe.wait_ge(s["out_read"], i * 4 + u + 1)
                        for kk in range(KT):
                            pe.matmul(k.bank[u % 2][:], w[:, u, kk, :], yT[:, kk, NP_TOK:T],
                                      start=(kk == 0), stop=(kk == KT - 1))
                            mm = pe.matmul(k.bank[6 + u % 2][:, 0:P], w[:, u, kk, :], yT[:, kk, 0:NP_TOK],
                                           start=(kk == 0), stop=(kk == KT - 1))
                        mm.then_inc(s["out_summed"], 1)

            @block.scalar
            def _(act):
                act.sem_inc(s["xa_read"], 1)
                act.sem_inc(s["out_read"], 2)
                with act.Fori(0, TT) as t:
                    act.wait_ge(s["xa_turned"], t + 2)
                    for b in range(4):
                        ev = act.activation(k.xT[:, 4 * b:4 * b + 4, bass.ds(t * P, P)], h4(k.bank[b][:]), ACT.Copy)
                    ev.then_inc(s["xa_read"], 1)
                with act.Fori(0, KT // 4) as i:
                    for u in range(4):
                        act.wait_ge(gates_in[u % 2], i * 64 + 32 * (u // 2 + 1))
                        act.activation(gt[u % 2][:], gt[u % 2][:], ACT.Sigmoid).then_inc(s["merge_sig"], 1)
                with act.Fori(0, KT // 4) as i:
                    for u in range(4):
                        m = i * 4 + u
                        act.wait_ge(s["out_summed"], m + 5)
                        dst = k.y2T[:].rearrange("p m t -> p (m t)")
                        act.activation(dst[:, bass.ds(m * T, NP_TOK)], k.bank[6 + u % 2][:, 0:P], ACT.Copy)
                        act.activation(dst[:, bass.ds(m * T + NP_TOK, NS_TOK)], k.bank[u % 2][:], ACT.Copy
                                       ).then_inc(s["out_read"], 1)

            @block.vector
            def _(dve):
                dve.sem_inc(s["merge_read"], 2)
                with dve.Fori(0, KT // 4) as i:
                    for u in range(4):
                        m = i * 4 + u
                        dve.wait_ge(s["merge_summed"], m + 5)
                        dve.wait_ge(s["merge_sig"], m + 1)
                        for j, dst in enumerate((ta, tb)):
                            dve.tensor_tensor(dst[u % 2][:, NP_TOK:T], k.bank[3 * (u % 2) + j][:],
                                              gt[u % 2][:, j, NP_TOK:T], ALU.mult)
                            op = dve.tensor_tensor(dst[u % 2][:, 0:NP_TOK],
                                                   k.bank[3 * (u % 2) + 2][:, j * P:(j + 1) * P],
                                                   gt[u % 2][:, j, 0:NP_TOK], ALU.mult)
                        op.then_inc(s["merge_read"], 1)
                        dve.drain()
                        dve.tensor_tensor(yT[:].rearrange("p m t -> p (m t)")[:, bass.ds(m * T, T)], ta[u % 2][:],
                                          tb[u % 2][:], ALU.add).then_inc(s["merged"], 1)


def phase_residual_router(nc, k):
    with ExitStack() as mem:
        def sb(name, shape):
            return mem.enter_context(nc.sbuf_tensor(name, shape, F32))
        sq = [sb(f"rr_sq{b}", [P, T]) for b in range(2)]
        R = sb("rr_R", [P, T])
        wr = sb("w_router", [P, KT, N_EXP])
        tok = [sb(f"rr_tok{b}", [P, D]) for b in range(2)]
        mx = sb("aff_max", [P, TT])
        sm = sb("aff_sum", [P, TT])
        aff = sb("aff", [P, TT, N_EXP])
        s = {n: k.sem(n) for n in ("rr_w", "rr_sq", "rr_sum", "rr_root", "rr_rr", "rr_x1", "rr_h2", "rr_turned",
                                   "rr_copied", "rr_logits", "rr_sub", "rr_exp", "rr_aff", "rr_affT")}
        stored = [k.sem(f"rr_stored{b}") for b in range(2)]
        src = (k.y2T, k.xT)
        order = [(what, t) for what in range(2) for t in range(TT)]
        with nc.Block() as block:
            @block.sync
            def _(sp):
                sp.dma_start(wr[:], k.d_wrouter).then_inc(s["rr_w"], 16)
                for n, (what, t) in enumerate(order):
                    sp.wait_ge(s["rr_copied"], 4 * n + 4)
                    sp.dma_start((k.d_x1, k.d_h2)[what][t * P:(t + 1) * P, :], tok[n % 2][:]).then_inc(stored[n % 2], 16)
                for b in range(2):
                    sp.wait_ge(stored[b], 16 * TT)

            @block.gpsimd
            def _(pool):
                for r in range(2):
                    if r == 1:
                        pool.wait_ge(s["rr_x1"], 1)
                    for kk in range(KT):
                        if r * KT + kk >= 2:
                            pool.wait_ge(s["rr_sum"], r * KT + kk - 1)
                        pool.tensor_tensor(sq[kk % 2][:], src[r][:, kk, :], src[r][:, kk, :], ALU.mult
                                           ).then_inc(s["rr_sq"], 1)

            @block.tensor
            def _(pe):
                for r in range(2):
                    for kk in range(KT):
                        pe.wait_ge(s["rr_sq"], r * KT + kk + 1)
                        pe.matmul(k.bank[0][:], k.ones, sq[kk % 2][:, NP_TOK:T], start=(kk == 0), stop=(kk == KT - 1))
                        pe.matmul(k.bank[1][:, 0:P], k.ones, sq[kk % 2][:, 0:NP_TOK], start=(kk == 0),
                                  stop=(kk == KT - 1)).then_inc(s["rr_sum"], 1)
                for n, (what, t) in enumerate(order):
                    if n == 0:
                        pe.wait_ge(s["rr_x1"], 1)
                    if n == TT:
                        pe.wait_ge(s["rr_h2"], 1)
                    for b in range(4):
                        i = 4 * n + b
                        if i >= 4:
                            pe.wait_ge(s["rr_copied"], i - 3)
                        for j in range(4):
                            mm = pe.transpose(k.bank[2 + b][:, j * P:(j + 1) * P],
                                              (k.xT, k.y2T)[what][:, 4 * b + j, t * P:(t + 1) * P], k.ident)
                        mm.then_inc(s["rr_turned"], 1)
                pe.wait_ge(s["rr_w"], 16)
                for t in range(TT):
                    for kk in range(KT):
                        mm = pe.matmul(k.bank[6][:, t * N_EXP:(t + 1) * N_EXP], k.y2T[:, kk, t * P:(t + 1) * P],
                                       wr[:, kk, :], start=(kk == 0), stop=(kk == KT - 1))
                mm.then_inc(s["rr_logits"], 1)
                pe.wait_ge(s["rr_aff"], 1)
                for t in range(TT):
                    mm = pe.transpose(k.bank[7][0:N_EXP, 0:P] if t == 0 else
                                      k.bank[0][0:N_EXP, (t - 1) * P:t * P], aff[:, t, :], k.ident)
                mm.then_inc(s["rr_affT"], 1)

            @block.scalar
            def _(act):
                for r in range(2):
                    act.wait_ge(s["rr_sum"], (r + 1) * KT)
                    if r == 1:
                        act.wait_ge(s["rr_x1"], 1)
                    act.activation(R[:, NP_TOK:T], k.bank[0][:], ACT.Sqrt, bias=k.eps, scale=1.0 / D)
                    act.activation(R[:, 0:NP_TOK], k.bank[1][:, 0:P], ACT.Sqrt, bias=k.eps, scale=1.0 / D
                                   ).then_inc(s["rr_root"], 1)
                for n, _ in enumerate(order):
                    if n >= 2:
                        act.wait_ge(stored[n % 2], 16 * (n // 2))
                    for b in range(4):
                        act.wait_ge(s["rr_turned"], 4 * n + b + 1)
                        act.activation(tok[n % 2][:, 4 * b * P:(4 * b + 4) * P], k.bank[2 + b][:], ACT.Copy
                                       ).then_inc(s["rr_copied"], 1)
                act.wait_ge(s["rr_sub"], 1)
                act.activation(aff[:], aff[:], ACT.Exp).then_inc(s["rr_exp"], 1)

            @block.vector
            def _(dve):
                for r in range(2):
                    dve.wait_ge(s["rr_root"], r + 1)
                    dve.reciprocal(R[:], R[:])
                    dve.drain()
                    for kk in range(KT):
                        dve.tensor_tensor(k.y2T[:, kk, :], src[r][:, kk, :], R[:], ALU.mult)
                    dve.drain()
                    for kk in range(KT):
                        for c, (lo, hi) in enumerate(((0, NP_TOK), (NP_TOK, T))):
                            v = k.y2T[:, kk, lo:hi]
                            if r == 0:
                                dve.scalar_tensor_tensor(out=k.xT[:, kk, lo:hi], in0=v, scalar=k.g1[:, kk, c:c + 1],
                                                         in1=k.xT[:, kk, lo:hi], op0=ALU.mult, op1=ALU.add)
                            else:
                                dve.tensor_scalar(v, v, k.a2[:, kk, c:c + 1], k.modT[:, 3 * KT + kk, c:c + 1],
                                                  ALU.mult, ALU.add)
                    dve.drain().then_inc(s[("rr_x1", "rr_h2")[r]], 1)
                dve.wait_ge(s["rr_logits"], 1)
                lg = k.bank[6][:, 0:TT * N_EXP].rearrange("p (t n) -> p t n", t=TT)
                dve.tensor_reduce(mx[:], lg, AX.X, ALU.max)
                dve.drain()
                dve.tensor_tensor(aff[:], lg, mx[:].unsqueeze(2).to_broadcast([P, TT, N_EXP]), ALU.subtract
                                  ).then_inc(s["rr_sub"], 1)
                dve.wait_ge(s["rr_exp"], 1)
                dve.tensor_reduce(sm[:], aff[:], AX.X, ALU.add)
                dve.drain()
                dve.reciprocal(sm[:], sm[:])
                dve.drain()
                dve.tensor_tensor(aff[:], aff[:], sm[:].unsqueeze(2).to_broadcast([P, TT, N_EXP]), ALU.mult
                                  ).then_inc(s["rr_aff"], 1)
                dve.wait_ge(s["rr_affT"], 1)
                dve.tensor_copy(k.affT[:, 0:P], k.bank[7][0:N_EXP, 0:P])
                dve.tensor_copy(k.affT[:, P:T], k.bank[0][0:N_EXP, :])


def phase_choice(nc, k):
    with ExitStack() as mem:
        val = mem.enter_context(nc.sbuf_tensor("top_val", [N_EXP, CAP], F32))
        ind = mem.enter_context(nc.sbuf_tensor("top_ind", [N_EXP, CAP], U32))
        indf = mem.enter_context(nc.sbuf_tensor("top_indf", [N_EXP, CAP], F32))
        zero = mem.enter_context(nc.sbuf_tensor("zero_rows", [P, D], F32))
        chosen, turned, zeroed, y_zeroed = (k.sem(n) for n in ("chosen", "choice_turned", "zero_made", "y_zeroed"))
        g2_out = k.sem("g2_out")
        with nc.Block() as block:
            @block.sync
            def _(sp):
                sp.wait_ge(zeroed, 1)
                for t in range(TT):
                    sp.dma_start(k.d_y[t * P:(t + 1) * P, :], zero[:]).then_inc(y_zeroed, 16)
                with nc.allow_non_contiguous_dma(reason="4096 gate values, once"):
                    for c in range(2):
                        sp.dma_start(k.d_g2[c:c + 1].rearrange("a (k p) -> p (a k)", p=P), k.g2[:, :, c]
                                     ).then_inc(g2_out, 16)
                sp.wait_ge(y_zeroed, 16 * TT)
                sp.wait_ge(g2_out, 32)

            @block.gpsimd
            def _(pool):
                pool.memset(zero[:], 0.0)
                pool.drain().then_inc(zeroed, 1)

            @block.vector
            def _(dve):
                for lo, hi, s0, cap in ((0, NP_TOK, 0, CAP_P), (NP_TOK, T, CAP_P, CAP_S)):
                    v = k.affT[:, lo:hi]
                    for r in range(cap // 8):
                        a, b = s0 + 8 * r, s0 + 8 * r + 8
                        dve.max(val[:, a:b], v)
                        dve.drain()
                        dve.max_index(ind[:, a:b], val[:, a:b], v)
                        dve.drain()
                        dve.match_replace(v, val[:, a:b], v, MASKED_ROW)
                        dve.drain()
                dve.tensor_copy(indf[:], ind[:])
                dve.drain()
                dve.tensor_scalar(indf[:, CAP_P:CAP], indf[:, CAP_P:CAP], float(NP_TOK), None, ALU.add)
                dve.drain().then_inc(chosen, 1)
                dve.wait_ge(turned, 1)
                dve.tensor_copy(k.gateT[:], k.bank[0][0:CAP, 0:N_EXP])
                dve.tensor_copy(k.idx[:], k.bank[0][0:CAP, N_EXP:2 * N_EXP])

            @block.tensor
            def _(pe):
                pe.wait_ge(chosen, 1)
                pe.transpose(k.bank[0][0:CAP, 0:N_EXP], val[:], k.ident[0:N_EXP, 0:N_EXP])
                pe.transpose(k.bank[0][0:CAP, N_EXP:2 * N_EXP], indf[:], k.ident[0:N_EXP, 0:N_EXP]
                             ).then_inc(turned, 1)


def phase_experts(nc, k):
    NW = 24
    NSLOT = 12
    FT = F_EXP // P
    DC = 256
    with ExitStack() as mem:
        def sb(name, shape):
            return mem.enter_context(nc.sbuf_tensor(name, shape, F32))
        w = sb("expert_ring", [P, NSLOT, KT, P])
        xe = [sb(f"xe{b}", [CAP, D]) for b in range(2)]
        xT = sb("xeT", [P, KT, CAP])
        sg = sb("silu_gate", [P, 2, CAP])
        hT = sb("hiddenT", [P, FT, CAP])
        ye = [sb(f"ye{b}", [CAP, D]) for b in range(2)]
        s = {n: k.sem(n) for n in ("xe_landed0", "xe_landed1", "xe_turned", "xeT_copied", "w_used", "silu_done",
                                   "hidden", "ye_done", "scattered", "rows_free")}
        landed = [k.sem(f"we_landed{j}") for j in range(NSLOT)]
        with nc.Block() as block:
            @block.sync
            def _(sp):
                with sp.Fori(0, N_EXP) as e:
                    for j in range(NW):
                        sp.wait_ge(s["w_used"], e * NW + (j + 1))
                        if j < 16:
                            src = (k.d_wgate, k.d_wup_e)[j % 2][bass.ds(e * FT + j // 2, 1)]
                            sp.dma_start(w[:, j % NSLOT], src.rearrange("a p k n -> p (a k) n")
                                         ).then_inc(landed[j % NSLOT], 16)
                        else:
                            src = k.d_wdown[bass.ds(e * 8 + (j - 16), 1)]
                            sp.dma_start(w[:, j % NSLOT].rearrange("p k n -> p (k n)"),
                                         src.rearrange("a p k n -> p (a k n)")).then_inc(landed[j % NSLOT], 16)

            @block.gpsimd
            def _(pool):
                def gather(e_col, b):
                    pool.indirect_dma_start(xe[b][:], None, k.d_h2[:, :],
                                            bass.IndirectOffsetOnAxis(ap=k.idx[:, e_col:e_col + 1], axis=0)
                                            ).then_inc(s[f"xe_landed{b}"], 16)

                pool.sem_inc(s["rows_free"], 2)
                for e in range(2):
                    gather(e, e)
                for e in range(N_EXP):
                    pool.wait_ge(s["ye_done"], 4 * e + 4 + 2)
                    if e > 0:
                        pool.wait_ge(s["scattered"], 16 * e)
                        pool.sem_inc(s["rows_free"], 1)
                    pool.indirect_dma_start(k.d_y[:, :], bass.IndirectOffsetOnAxis(ap=k.idx[:, e:e + 1], axis=0),
                                            ye[e % 2][:], None, compute_op=ALU.add).then_inc(s["scattered"], 16)
                    if e + 2 < N_EXP:
                        pool.wait_ge(s["xe_turned"], 4 * e + 4)
                        gather(e + 2, e % 2)
                pool.wait_ge(s["scattered"], 16 * N_EXP)

            def experts(eng, body):
                with eng.Fori(0, N_EXP // 2) as i:
                    for b in range(2):
                        body(i, b)

            @block.tensor
            def _(pe):
                pe.sem_inc(s["w_used"], NSLOT)

                def body(i, b):
                    def arrived(j):
                        pe.wait_ge(landed[j % NSLOT], i * 64 + (32 * b + 16 * (j // NSLOT) + 16))
                    pe.wait_ge(s[f"xe_landed{b}"], i * 16 + 16)
                    for r in range(4):
                        pe.wait_ge(s["xeT_copied"], i * 8 + (4 * b + r + 1))
                        for j in range(4):
                            kk = 4 * r + j
                            mm = pe.transpose(k.bank[r % 2][:, j * P:j * P + CAP], xe[b][:, kk * P:(kk + 1) * P],
                                              k.ident[0:CAP, 0:CAP])
                        mm.then_inc(s["xe_turned"], 1)
                    pe.wait_ge(s["xeT_copied"], i * 8 + (4 * b + 4 + 2))
                    for f in range(FT):
                        pe.wait_ge(s["hidden"], i * 16 + (8 * b + f + 1))
                        for g in range(2):
                            j = 2 * f + g
                            arrived(j)
                            for kk in range(KT):
                                mm = pe.matmul(k.bank[2 + 2 * (f % 2) + g][:, 0:CAP], w[:, j % NSLOT, kk, :],
                                               xT[:, kk, :], start=(kk == 0), stop=(kk == KT - 1))
                            mm.then_inc(s["w_used"], 1)
                    pe.wait_ge(s["hidden"], i * 16 + (8 * b + 8 + 2))
                    for c in range(8):
                        j = 16 + c
                        arrived(j)
                        wd = w[:, j % NSLOT].rearrange("p k n -> p (k n)").rearrange("p (k n) -> p k n", n=DC)
                        if c % 2 == 0:
                            pe.wait_ge(s["ye_done"], i * 8 + (4 * b + c // 2 + 1))
                        for kk in range(FT):
                            mm = pe.matmul(k.bank[6 + c // 2 % 2][0:CAP, (c % 2) * DC:(c % 2 + 1) * DC],
                                           hT[:, kk, :], wd[:, kk, :], start=(kk == 0), stop=(kk == FT - 1))
                        mm.then_inc(s["w_used"], 1)
                experts(pe, body)

            @block.scalar
            def _(act):
                act.sem_inc(s["xeT_copied"], 2)

                def body(i, b):
                    for r in range(4):
                        act.wait_ge(s["xe_turned"], i * 8 + (4 * b + r + 1))
                        act.activation(xT[:, 4 * r:4 * r + 4, :], h4(k.bank[r % 2][:])[:, :, 0:CAP], ACT.Copy
                                       ).then_inc(s["xeT_copied"], 1)
                    for f in range(FT):
                        act.wait_ge(s["w_used"], i * 48 + (24 * b + NSLOT + 2 * f + 1))
                        act.wait_ge(s["hidden"], i * 16 + (8 * b + f + 1))
                        act.activation(sg[:, f % 2, :], k.bank[2 + 2 * (f % 2)][:, 0:CAP], ACT.Silu
                                       ).then_inc(s["silu_done"], 1)
                experts(act, body)

            @block.vector
            def _(dve):
                dve.sem_inc(s["hidden"], 2)
                dve.sem_inc(s["ye_done"], 2)

                def body(i, b):
                    for f in range(FT):
                        dve.wait_ge(s["silu_done"], i * 16 + (8 * b + f + 1))
                        dve.wait_ge(s["w_used"], i * 48 + (24 * b + NSLOT + 2 * f + 2))
                        dve.tensor_tensor(hT[:, f, :], k.bank[3 + 2 * (f % 2)][:, 0:CAP], sg[:, f % 2, :], ALU.mult
                                          ).then_inc(s["hidden"], 1)
                    dve.wait_ge(s["rows_free"], i * 2 + (b + 1))
                    for c in range(4):
                        dve.wait_ge(s["w_used"], i * 48 + (24 * b + NSLOT + 16 + 2 * c + 2))
                        dve.tensor_scalar(ye[b][:, c * 512:(c + 1) * 512], k.bank[6 + c % 2][0:CAP, :],
                                          k.gateT[:, bass.ds(i * 2 + b, 1)], None, ALU.mult
                                          ).then_inc(s["ye_done"], 1)
                experts(dve, body)


def phase_final(nc, k):
    with ExitStack() as mem:
        def sb(name, shape):
            return mem.enter_context(nc.sbuf_tensor(name, shape, F32))
        row = [sb(f"g2_row{c}", [P, D]) for c in range(2)]
        y = [sb(f"y_in{b}", [P, D]) for b in range(2)]
        x1 = [sb(f"x1_in{b}", [P, D]) for b in range(2)]
        sq = sb("y_sq", [P, D])
        ms = [sb(f"y_ms{b}", [P, 1]) for b in range(2)]
        rs = [sb(f"y_rs{b}", [P, 1]) for b in range(2)]
        rows_in, summed, rooted, done = (k.sem(n) for n in ("g2_rows_in", "y_summed", "y_rooted", "y_done"))
        landed = [k.sem(f"y_landed{b}") for b in range(2)]
        stored = [k.sem(f"out_stored{b}") for b in range(2)]
        with nc.Block() as block:
            @block.sync
            def _(sp):
                for t in range(TT):
                    b = t % 2
                    if t >= 2:
                        sp.wait_ge(done, t - 1)
                        sp.wait_ge(stored[b], 16 * (t // 2))
                    sp.dma_start(y[b][:], k.d_y[t * P:(t + 1) * P, :]).then_inc(landed[b], 16)
                    sp.dma_start(x1[b][:], k.d_x1[t * P:(t + 1) * P, :]).then_inc(landed[b], 16)
                    if t < 2:
                        sp.dma_start(row[t][:], k.d_g2[t:t + 1, :].to_broadcast([P, D])).then_inc(rows_in, 16)

            @block.gpsimd
            def _(pool):
                for t in range(TT):
                    pool.wait_ge(done, t + 1)
                    dst = k.o_yp[:, :] if t == 0 else k.o_ys[(t - 1) * P:t * P, :]
                    pool.dma_start(dst, x1[t % 2][:]).then_inc(stored[t % 2], 16)
                pool.wait_ge(stored[0], 48)
                pool.wait_ge(stored[1], 32)

            @block.scalar
            def _(act):
                for t in range(TT):
                    b = t % 2
                    act.wait_ge(landed[b], 32 * (t // 2 + 1))
                    if t >= 2:
                        act.wait_ge(rooted, t - 1)
                    act.activation(sq[:], y[b][:], ACT.Square, accum_out=ms[b][:])
                    act.drain()
                    if t >= 2:
                        act.wait_ge(done, t - 1)
                    act.activation(rs[b][:], ms[b][:], ACT.Sqrt, bias=k.eps, scale=1.0 / D).then_inc(rooted, 1)

            @block.vector
            def _(dve):
                dve.wait_ge(rows_in, 32)
                for t in range(TT):
                    b = t % 2
                    dve.wait_ge(rooted, t + 1)
                    dve.reciprocal(rs[b][:], rs[b][:])
                    dve.drain()
                    dve.scalar_tensor_tensor(out=y[b][:], in0=y[b][:], scalar=rs[b][:, 0:1], in1=row[min(t, 1)][:],
                                             op0=ALU.mult, op1=ALU.mult)
                    dve.drain()
                    dve.tensor_tensor(x1[b][:], x1[b][:], y[b][:], ALU.add).then_inc(done, 1)


def build(nc, ins, outs):
    with ExitStack() as ctx:
        taken = []

        def take(name):
            taken.append(nc.alloc_semaphore(name=name))
            return taken[-1]

        def give_back():
            nc.clear_and_free_semaphores(taken)
            taken.clear()
            nc.all_engine_barrier()

        def sb(stack, name, shape, dt=F32):
            return stack.enter_context(nc.sbuf_tensor(name, shape, dt))

        scratch = {name: nc.dram_tensor(name, shape, F32).ap() for name, shape in (
            ("d_proj", [N_TILES, P, T]), ("d_x1", [T, D]), ("d_h2", [T, D]), ("d_y", [T, D]), ("d_g2", [2, D]))}
        k = Chip(take, ins, outs, scratch)
        k.bank = [ctx.enter_context(nc.psum_tensor(f"bank{b}", [P, 512], F32)) for b in range(8)]
        k.const = sb(ctx, "const", [P, N_CONST])
        k.chan = sb(ctx, "chan", [P, N_CHAN])
        k.rowp = sb(ctx, "rowp", [P, N_ROWP])
        k.modT = sb(ctx, "modT", [P, N_MOD_TILES, 2])
        k.a2, k.g1, k.g2 = (sb(ctx, n, [P, KT, 2]) for n in ("a2", "g1", "g2"))
        k.affT = sb(ctx, "affT", [N_EXP, T])
        k.gateT = sb(ctx, "gateT", [CAP, N_EXP])
        k.idx = sb(ctx, "idx", [CAP, N_EXP], U32)
        k.ident = k.const[:, C_ID:C_ID + P]
        k.tri = [k.const[:, C_TRI + d * P:C_TRI + (d + 1) * P] for d in range(2)]
        k.neg = [k.const[:, C_NEG + d * P:C_NEG + (d + 1) * P] for d in range(2)]
        k.ones = k.const[:, C_ONES:C_ONES + P]
        k.level = lambda d, n: k.const[:, C_LEV + (2 * n + d) * P:C_LEV + (2 * n + d + 1) * P]
        k.eps = k.chan[:, V_L2B + 8:V_L2B + 9]

        back = ExitStack()
        with ExitStack() as front:
            k.o_dn, k.o_ml = (sb(front, n, [P, TT, 1024]) for n in ("o_dn", "o_ml"))
            k.gates = sb(front, "gates", [P, TT, 48])
            k.beta, k.G, k.nG, k.eG, k.neg_eG, k.wS, k.bw, k.g_tot, k.eT = (
                sb(front, n, [P, TT, 16]) for n in ("beta", "G", "nG", "eG", "neg_eG", "wS", "bw", "g_tot", "eT"))
            k.ci, k.b_ml, k.b_tot = (sb(front, n, [P, TT, 8]) for n in ("ci", "b_ml", "b_tot"))
            with ExitStack() as inner:
                k.hT = sb(inner, "hT", [P, KT, T])
                phase_modulation(nc, k)
                phase_projection(nc, k)
            phase_gates(nc, k)
            phase_deltanet(nc, k)
            phase_mlstm(nc, k)
            give_back()
            k.y2T = back.enter_context(nc.sbuf_tensor("y_parts", [P, KT, T], F32, side="right"))
            k.yaT, k.ybT = k.y2T[:, 0:8, :], k.y2T[:, 8:16, :]
            phase_branch_outputs(nc, k)
        with back:
            k.xT = sb(back, "xT", [P, KT, T])
            phase_merge(nc, k)
            phase_residual_router(nc, k)
        phase_choice(nc, k)
        phase_experts(nc, k)
        phase_final(nc, k)


def constants():
    c = np.zeros((P, N_CONST), np.float32)
    j, i = np.meshgrid(np.arange(P), np.arange(P), indexing="ij")
    c[:, C_ID:C_ID + P] = j == i
    for d, ok in enumerate((j <= i, j >= i)):
        c[:, C_TRI + d * P:C_TRI + (d + 1) * P] = ok
        c[:, C_NEG + d * P:C_NEG + (d + 1) * P] = np.where(ok, 0.0, NEG)
    c[:, C_ONES:C_ONES + P] = 1.0
    for n, s in enumerate(LEVELS):
        same = j // (2 * s) == i // (2 * s)
        low, high = (j // s) % 2, (i // s) % 2
        c[:, C_LEV + 2 * n * P:C_LEV + (2 * n + 1) * P] = same & (low == 0) & (high == 1)
        c[:, C_LEV + (2 * n + 1) * P:C_LEV + (2 * n + 2) * P] = same & (low == 1) & (high == 0)
    return c


def tiles_of(w, width=P):
    kk, n = w.shape
    return np.ascontiguousarray(w.reshape(kk // P, P, n // width, width).transpose(2, 1, 0, 3))


def channels(v):
    return v.reshape(-1, P).T


def lay_out(x):
    f = np.float32
    w_in, b_in = x["w_in"][0], x["b_in"][0]
    cuts = np.cumsum([0, 1024, 1024, 1024, 1024, 16, 16, 512, 512, 1024, 1024, 8, 8, 2048, 2048])
    names = ("dq", "dk", "dv", "dz", "db", "da", "mq", "mk", "mv", "mo", "mi", "mf", "ga", "gb")
    part = {n: slice(cuts[i], cuts[i + 1]) for i, n in enumerate(names)}
    order = ("dq", "dk", "dv", "mq", "mk", "mv", "dz", "mo", "ga", "gb")
    gates = ("db", "da", "mi", "mf")
    w_tiles = np.concatenate([tiles_of(w_in[:, part[n]]) for n in order])
    w_gates = np.concatenate([w_in[:, part[n]] for n in gates], 1)
    chan = np.zeros((P, N_CHAN), f)
    cond = np.stack([x["c_ctx"], x["c"][0]], 1)
    chan[:, V_COND:V_BMOD] = cond.reshape(KT, P, 2).transpose(1, 0, 2).reshape(P, 2 * KT)
    chan[:, V_BMOD:V_PRE1] = channels(x["b_mod"][0])
    for at, n in ((V_PRE1, "pre1_gain"), (V_POST1, "post1_gain"), (V_PRE2, "pre2_gain"), (V_POST2, "post2_gain")):
        chan[:, at:at + KT] = channels(x[n][0])
    chan[:, V_BIN:V_CONV] = np.concatenate([channels(b_in[part[n]]) for n in order], 1)
    chan[:, V_CONV:V_L2S] = x["dn_conv_w"][0].reshape(5, 24, P).transpose(2, 1, 0).reshape(P, 120)
    chan[:, V_L2S:V_L2S + 8], chan[:, V_L2S + 8:V_L2S + 16] = float(P), 1.0
    chan[:, V_L2B:V_L2B + 8], chan[:, V_L2B + 8:V_L2B + 16] = P * EPS, EPS
    chan[:, V_DNG] = x["dn_onorm"][0]
    chan[:, V_MLG:V_MLG + 8] = channels(x["ml_onorm"][0].reshape(-1))
    row = np.concatenate([np.concatenate([b_in[part[n]] for n in gates]), x["dn_dt_bias"].reshape(-1),
                          x["ml_f_bias"].reshape(-1), x["ml_i_bias"].reshape(-1), x["dn_a_log"].reshape(-1),
                          x["state_ml_m"].reshape(-1)])
    return {
        "d_const": constants(), "d_chan": chan, "d_rowp": np.ascontiguousarray(np.broadcast_to(row, (P, N_ROWP))),
        "d_x": np.concatenate([x["x_prompt"][0], x["x_sample"][0]]),
        "d_wmod": tiles_of(x["w_mod"][0]), "d_win": w_tiles,
        "d_wgates": np.ascontiguousarray(w_gates.reshape(KT, P, 48).transpose(1, 0, 2)),
        "d_sdn": x["state_dn"][0, 0], "d_smc": x["state_ml_c"][0, 0], "d_smn": x["state_ml_n"][0, 0],
        "d_wup": np.concatenate([tiles_of(x["w_up_a"][0]), tiles_of(x["w_up_b"][0])], 2),
        "d_wout": tiles_of(x["w_out"][0]),
        "d_wrouter": np.ascontiguousarray(x["w_router"][0].reshape(KT, P, N_EXP).transpose(1, 0, 2)),
        "d_wgate": np.concatenate([tiles_of(w) for w in x["w_gate"][0]]),
        "d_wup_e": np.concatenate([tiles_of(w) for w in x["w_up"][0]]),
        "d_wdown": np.concatenate([tiles_of(w, 256) for w in x["w_down"][0]]),
    }


_OUTS = [("o_yp", (NP_TOK, D)), ("o_ys", (NS_TOK, D)), ("o_sdn", (2, H_DN, P, P)), ("o_smc", (2, H_ML, P, DV_ML)),
         ("o_smn", (2, H_ML, P)), ("o_smm", (2, H_ML))]


def kernel(**inputs):
    import concourse.bacc as bacc
    from concourse.bass_utils import run_bass_kernel_spmd

    arrays = lay_out({n: np.asarray(a) for n, a in inputs.items()})
    nc = bacc.Bacc("TRN2", target_bir_lowering=False, num_devices=1)
    ins = {n: nc.dram_tensor(n, a.shape, F32, kind="ExternalInput").ap() for n, a in arrays.items()}
    outs = {n: nc.dram_tensor(n, shape, F32, kind="ExternalOutput").ap() for n, shape in _OUTS}
    build(nc, ins, outs)
    r = run_bass_kernel_spmd(nc, [arrays], core_ids=[0]).results[0]
    return (r["o_yp"][None], r["o_ys"][None], r["o_sdn"][None, None], r["o_smc"][None, None],
            r["o_smn"][None, None], r["o_smm"][None, None])
```

```python
from contextlib import ExitStack

import numpy as np

import concourse.bass as bass
from concourse import mybir

ALU = mybir.AluOpType
ACT = mybir.ActivationFunctionType
F32 = mybir.dt.float32
F32R = mybir.dt.float32r
U32 = mybir.dt.uint32
AX = mybir.AxisListType

P = 128
D = 2048
KT = D // P
NP_TOK, NS_TOK = 128, 512
T = NP_TOK + NS_TOK
TT = T // P
GRID_W = 64
ROWS = NS_TOK // GRID_W
H_DN, H_ML, DV_ML = 8, 4, 256
N_EXP, F_EXP = 16, 1024
CAP_P, CAP_S = 2 * NP_TOK // N_EXP, 2 * NS_TOK // N_EXP
CAP = CAP_P + CAP_S
EPS = 1e-6
K_SCALE = float(P) ** -0.5
NEG = -1e30
LEVELS = [1, 2, 4, 8, 16, 32, 64]

QK_TILES, V_TILES, PERM_TILES, RASTER_TILES = 16, 8, 16, 48
T_MLQ, T_Z, T_MO, T_GA, T_GB = 24, 40, 48, 56, 72
N_TILES = 88
GATE_TILE = N_TILES
CHUNKS = ((0, T // 2), (T // 2, T))
N_MOD_TILES = 6 * KT

C_ID, C_TRI, C_NEG, C_ONES, C_LEV = 0, 128, 384, 640, 768
C_CMP = C_LEV + 2 * P
N_CONST = C_CMP + 2 * len(LEVELS) * (P // 2)

V_COND = 0
V_BMOD = V_COND + 2 * KT
V_PRE1 = V_BMOD + N_MOD_TILES
V_POST1 = V_PRE1 + KT
V_PRE2 = V_POST1 + KT
V_POST2 = V_PRE2 + KT
V_BIN = V_POST2 + KT
V_CONV = V_BIN + N_TILES + 1
V_L2S = V_CONV + 24 * 5
V_L2B = V_L2S + 16
V_DNG = V_L2B + 16
V_MLG = V_DNG + 1
N_CHAN = V_MLG + 8

R_DT, R_FB, R_IB, R_AL, R_M0 = 0, 16, 24, 32, 48
N_ROWP = 56

MASKED_ROW = -1.0


def wait(eng, sem, value):
    if not (isinstance(value, int) and value == 0):
        eng.wait_ge(sem, value)


class Bank:

    def __init__(self, tensor, filled, emptied, fills):
        self.t, self.filled, self.emptied = tensor, filled, emptied
        self.order = {f: n for n, f in enumerate(fills)}
        self.per_step = len(fills)

    def wait_free(self, eng, step, fill):
        wait(eng, self.emptied, step * self.per_step + self.order[fill])

    def wait_filled(self, eng, step, fill):
        wait(eng, self.filled, step * self.per_step + self.order[fill] + 1)

    def wait_emptied(self, eng, step, fill):
        wait(eng, self.emptied, step * self.per_step + self.order[fill] + 1)


class Chip:

    def __init__(self, sem, ins, outs, scratch):
        self.sem = sem
        (self.d_const, self.d_chan, self.d_rowp, self.d_x, self.d_wmod, self.d_win, self.d_sdn,
         self.d_smc, self.d_smn, self.d_wup, self.d_wout, self.d_wrouter, self.d_wgate, self.d_wup_e,
         self.d_wdown) = (ins[n] for n in (
             "d_const", "d_chan", "d_rowp", "d_x", "d_wmod", "d_win", "d_sdn", "d_smc", "d_smn",
             "d_wup", "d_wout", "d_wrouter", "d_wgate", "d_wup_e", "d_wdown"))
        self.o_yp, self.o_ys, self.o_sdn, self.o_smc, self.o_smn, self.o_smm = (
            outs[n] for n in ("o_yp", "o_ys", "o_sdn", "o_smc", "o_smn", "o_smm"))
        self.d_proj, self.d_x1, self.d_h2, self.d_y, self.d_g2 = (
            scratch[n] for n in ("d_proj", "d_x1", "d_h2", "d_y", "d_g2"))


def h4(ap):
    return ap.rearrange("p (h n) -> p h n", h=4)


def per_head(ap, n):
    return ap.unsqueeze(2).to_broadcast([P, ap.shape[1], n])


def all_heads(ap, heads=4):
    return ap.unsqueeze(1).to_broadcast([P, heads, ap.shape[1]])


def col(ap3, t, a, b):
    n = ap3.shape[2]
    return ap3.rearrange("p t n -> p (t n)")[:, bass.ds(t * n + a, b - a)]


def phase_modulation(nc, k):
    with ExitStack() as mem:
        def sb(name, shape):
            return mem.enter_context(nc.sbuf_tensor(name, shape, F32))
        w = [sb(f"wmod_ring{b}", [P, 4, KT, P]) for b in range(2)]
        mod_rows = [mem.enter_context(nc.sbuf_tensor(f"mod_rows{b}", [2, 512], F32)) for b in range(2)]
        xin = sb("x_in", [P, D])
        xsq = sb("x_sq", [P, D])
        ssq = sb("x_ssq", [P, 1])
        root = sb("x_root", [P, 1])
        rstd = sb("x_rstd", [P, 1])
        xn = sb("x_normed", [P, D])
        cond = sb("cond", [P, KT, 2])
        s = {n: k.sem(n) for n in ("params_in", "x_landed", "x_squared", "x_meaned", "x_rooted", "x_normed",
                                   "x_turned", "hT_written", "cond_ready", "mod_summed", "mod_copied",
                                   "mod_turned", "mod_stored")}
        landed = [k.sem(f"wmod_landed{b}") for b in range(2)]
        PAIRS = N_MOD_TILES // 8

        def interleaved(eng, mod_pair, x_before=None, x_after=None):
            with eng.Fori(0, TT) as i:
                if x_before:
                    x_before(i)
                mod_pair(i, 0)
                if x_after:
                    x_after(i)
            with eng.Fori(0, PAIRS - TT) as i:
                mod_pair(i, 2 * TT)
        with nc.Block() as block:
            @block.sync
            def _(sp):
                sp.dma_start(k.chan[:], k.d_chan).then_inc(s["params_in"], 16)
                sp.dma_start(k.const[:], k.d_const).then_inc(s["params_in"], 16)
                sp.dma_start(k.rowp[:], k.d_rowp).then_inc(s["params_in"], 16)
                with sp.Fori(0, PAIRS) as i:
                    for b in range(2):
                        sp.wait_ge(s["mod_summed"], i * 2 + b + 1)
                        for u in range(4):
                            sp.dma_start(w[b][:, u], k.d_wmod[bass.ds(i * 8 + (4 * b + u), 1)].rearrange(
                                "a p k n -> p (a k) n")).then_inc(landed[b], 16)

            @block.gpsimd
            def _(pool):
                with pool.Fori(0, TT) as t:
                    pool.wait_ge(s["x_normed"], t + 1)
                    pool.dma_start(xin[:], k.d_x[bass.ds(t * P, P), :]).then_inc(s["x_landed"], 16)

            @block.tensor
            def _(pe):
                pe.sem_inc(s["mod_summed"], 2)
                pe.sem_inc(s["mod_turned"], 2)
                pe.wait_ge(s["params_in"], 48)
                pe.wait_ge(s["cond_ready"], 1)

                def multiply(i, g):
                    for b in range(2):
                        pe.wait_ge(landed[b], i * 64 + (32 * g + 64))
                        pe.wait_ge(s["mod_copied"], i * 2 + (g + b + 1))
                        for kk in range(KT):
                            mm = pe.matmul(k.bank[4 + b][0:2, :].rearrange("p (u n) -> p u n", u=4), cond[:, kk, :],
                                           w[b][:, :, kk, :], start=(kk == 0), stop=(kk == KT - 1))
                        mm.then_inc(s["mod_summed"], 1)
                    for b in range(2):
                        pe.wait_ge(s["mod_copied"], i * 2 + (g + b + 3))
                        pe.wait_ge(s["mod_stored"], i * 2 + (g + b + 1))
                        for u in range(4):
                            mm = pe.matmul(k.bank[6 + b][:, 2 * u:2 * u + 2], mod_rows[b][:, u * P:(u + 1) * P],
                                           k.ident[0:2, 0:2], start=True, stop=True)
                        mm.then_inc(s["mod_turned"], 1)

                def turn_x(t):
                    pe.wait_ge(s["x_normed"], t + 2)
                    pe.wait_ge(s["hT_written"], t + 1)
                    for kk in range(KT):
                        mm = pe.transpose(k.bank[kk // 4][:, (kk % 4) * P:(kk % 4 + 1) * P],
                                          xn[:, kk * P:(kk + 1) * P], k.ident)
                    mm.then_inc(s["x_turned"], 1)
                interleaved(pe, multiply, x_after=turn_x)

            @block.scalar
            def _(act):
                act.wait_ge(s["params_in"], 48)
                act.activation(cond[:].rearrange("p k c -> p (k c)"), k.chan[:, V_COND:V_COND + 2 * KT],
                               ACT.Silu).then_inc(s["cond_ready"], 1)
                act.sem_inc(s["hT_written"], 1)
                act.sem_inc(s["mod_copied"], 2)

                def copy_rows(i, g):
                    for b in range(2):
                        act.wait_ge(s["mod_summed"], i * 2 + (g + b + 3))
                        act.wait_ge(s["mod_turned"], i * 2 + (g + b + 1))
                        act.activation(mod_rows[b][:], k.bank[4 + b][0:2, :], ACT.Copy
                                       ).then_inc(s["mod_copied"], 1)

                def square_x(t):
                    act.wait_ge(s["x_landed"], t * 16 + 16)
                    act.activation(xsq[:], xin[:], ACT.Square, accum_out=ssq[:]).then_inc(s["x_squared"], 1)
                    act.wait_ge(s["x_meaned"], t + 1)
                    act.activation(root[:], ssq[:], ACT.Sqrt).then_inc(s["x_rooted"], 1)

                def keep_turned_x(t):
                    act.wait_ge(s["x_turned"], t + 1)
                    for b in range(4):
                        ev = act.activation(k.hT[:, 4 * b:4 * b + 4, bass.ds(t * P, P)],
                                            h4(k.bank[b][:]), ACT.Copy)
                    ev.then_inc(s["hT_written"], 1)
                interleaved(act, copy_rows, square_x, keep_turned_x)

            @block.vector
            def _(dve):
                dve.sem_inc(s["x_normed"], 1)
                dve.sem_inc(s["mod_stored"], 2)
                dve.wait_ge(s["params_in"], 48)

                def add_bias(i, g):
                    for b in range(2):
                        dve.wait_ge(s["mod_turned"], i * 2 + (g + b + 3))
                        bmod = k.chan[:, bass.ds(i * 8 + (4 * g + 4 * b + V_BMOD), 4)]
                        dve.tensor_tensor(k.modT[:].rearrange("p m c -> p (m c)")[
                            :, bass.ds(i * 16 + 8 * (g + b), 8)].rearrange("p (m c) -> p m c", c=2),
                                          k.bank[6 + b][:, 0:8].rearrange("p (m c) -> p m c", c=2),
                                          bmod.unsqueeze(2).to_broadcast([P, 4, 2]), ALU.add
                                          ).then_inc(s["mod_stored"], 1)

                def normalize_x(t):
                    dve.wait_ge(s["x_squared"], t + 1)
                    dve.tensor_scalar(ssq[:], ssq[:], 1.0 / D, EPS, ALU.mult, ALU.add).then_inc(s["x_meaned"], 1)
                    dve.wait_ge(s["x_rooted"], t + 1)
                    dve.reciprocal(rstd[:], root[:])
                    dve.drain()
                    dve.wait_ge(s["hT_written"], t + 1)
                    dve.tensor_scalar(xn[:], xin[:], rstd[:, 0:1], None, ALU.mult).then_inc(s["x_normed"], 1)
                interleaved(dve, add_bias, x_before=normalize_x)
                dve.drain()
                for c in range(2):
                    for out, gain, part, plus in ((k.a1, V_PRE1, 1, 1.0), (k.a2, V_PRE2, 4, 1.0),
                                                  (k.g1, V_POST1, 2, 0.0), (k.g2, V_POST2, 5, 0.0)):
                        dve.scalar_tensor_tensor(out=out[:, :, c], in0=k.modT[:, part * KT:(part + 1) * KT, c],
                                                 scalar=plus, in1=k.chan[:, gain:gain + KT],
                                                 op0=ALU.add, op1=ALU.mult)


def phase_first_norm(nc, k):
    shifted, high = k.sem("h_shifted"), k.sem("h_high")
    with nc.Block() as block:
        @block.scalar
        def _(act):
            for kk in range(KT):
                act.wait_ge(shifted, kk + 1)
                act.activation(k.h_hi[:, kk, :], k.hT[:, kk, :], ACT.Copy).then_inc(high, 1)

        @block.vector
        def _(dve):
            def low(kk):
                dve.wait_ge(high, kk + 1)
                dve.tensor_tensor(k.h_lo[:, kk, :], k.hT[:, kk, :], k.h_hi[:, kk, :].bitcast(F32), ALU.subtract)
            for kk in range(KT):
                for c, (lo, hi) in enumerate(((0, NP_TOK), (NP_TOK, T))):
                    op = dve.tensor_scalar(k.hT[:, kk, lo:hi], k.hT[:, kk, lo:hi], k.a1[:, kk, c:c + 1],
                                           k.modT[:, kk, c:c + 1], ALU.mult, ALU.add)
                dve.drain().then_inc(shifted, 1)
                if kk > 0:
                    low(kk - 1)
            low(KT - 1)


def phase_projection(nc, k):
    with ExitStack() as mem:
        def sb(name, shape, dt=F32):
            return mem.enter_context(nc.sbuf_tensor(name, shape, dt))
        w = sb("win_ring", [P, 4, KT, P])
        w_hi, w_lo = ([sb(f"{n}{b}", [P, KT, P], F32R) for b in range(2)] for n in ("win_hi", "win_lo"))
        RAW = T + 8
        CV = T + 4
        S_RAW, S_CV = NP_TOK + 6, NP_TOK + 4
        CUT = CHUNKS[0][1] - NP_TOK
        raw = [sb(f"raw{b}", [P, RAW]) for b in range(2)]
        cv = sb("convolved", [P, CV])
        sl = [sb(f"silu_out{b}", [P, T]) for b in range(2)]
        sq = sb("squares", [P, T])
        rt = sb("roots", [P, T])
        ob = [sb(f"proj_out{b}", [P, T]) for b in range(2)]
        gm = sb("gates_by_channel", [48, T])
        s = {n: k.sem(n) for n in ("win_high", "win_low", "proj_summed", "evac", "conv", "silu", "sq", "ones",
                                   "root", "normed", "gates_read", "gates_turned", "raw_zeroed")}
        landed = [k.sem(f"win_landed{u}") for u in range(4)]
        stored = [k.sem(f"proj_stored{b}") for b in range(2)]
        bank = [[k.bank[2 * b], k.bank[2 * b + 1]] for b in range(2)]

        with nc.Block() as block:
            @block.gpsimd
            def _(pool):
                def load(i, u):
                    pool.wait_ge(s["win_low"], i * 4 + u + 1)
                    pool.dma_start(w[:, u], k.d_win[bass.ds(i * 4 + u, 1)].rearrange("a p k n -> p (a k) n")
                                   ).then_inc(landed[u], 16)
                with pool.Fori(0, N_TILES // 4) as i:
                    for u in range(4):
                        load(i, u)
                load(N_TILES // 4, 0)

            @block.tensor
            def _(pe):
                pe.sem_inc(s["ones"], 1)

                def project(i, base, u):
                    n, b = i * 4 + (base + u), (base + u) % 2
                    pe.wait_ge(s["win_low"], n + 5)
                    pe.wait_ge(s["evac"], n + 1)
                    for kk in range(KT):
                        for wt, hs in ((w_hi[b], (k.h_hi, k.h_lo)), (w_lo[b], (k.h_hi,))):
                            for h in hs:
                                for c, (lo, hi) in enumerate(CHUNKS):
                                    mm = pe.matmul(bank[b][c][:, 0:hi - lo], wt[:, kk, :], h[:, kk, lo:hi],
                                                   start=(kk == 0 and wt is w_hi[b] and h is k.h_hi),
                                                   stop=(kk == KT - 1 and wt is w_lo[b]))
                    mm.then_inc(s["proj_summed"], 1)

                def sum_squares(i, base, u):
                    n = i * 4 + (base + u)
                    pe.wait_ge(s["sq"], n + 1)
                    pe.wait_ge(s["root"], n + 1)
                    pe.matmul(k.bank[4][:], k.ones, sq[:, NP_TOK:T], start=True, stop=True)
                    pe.matmul(k.bank[5][:, 0:P], k.ones, sq[:, 0:NP_TOK], start=True, stop=True
                              ).then_inc(s["ones"], 1)

                project(0, 0, 0)
                with pe.Fori(0, QK_TILES // 4) as i:
                    for u in range(4):
                        project(i, 1, u)
                        sum_squares(i, 0, u)
                with pe.Fori(0, (N_TILES - QK_TILES) // 4) as i:
                    for u in range(4):
                        project(i, QK_TILES + 1, u)
                pe.wait_ge(s["gates_read"], 1)
                for t in range(TT):
                    mm = pe.transpose(k.bank[6][:, t * 48:(t + 1) * 48], gm[:, t * P:(t + 1) * P],
                                      k.ident[0:48, 0:48])
                mm.then_inc(s["gates_turned"], 1)

            def bias(n):
                return k.chan[:, bass.ds(n + V_BIN, 1)]

            def wait_store(eng, i, base, u):
                eng.wait_ge(stored[u % 2], i * 32 + (base // 2 + u // 2 + 1) * 16)

            @block.scalar
            def _(act):
                act.sem_inc(s["evac"], 2)
                act.sem_inc(s["silu"], 1)
                act.sem_inc(s["root"], 1)

                def high(i, base, u):
                    v = base + u
                    act.wait_ge(landed[v % 4], i * 16 + 16 * (v // 4 + 1))
                    act.activation(w_hi[v % 2][:], w[:, v % 4], ACT.Copy).then_inc(s["win_high"], 1)

                def to_raw(i, base, u):
                    n, b = i * 4 + (base + u), (base + u) % 2
                    act.wait_ge(s["proj_summed"], n + 1)
                    act.wait_ge(s["conv"], n + 1)
                    act.activation(raw[b][:, 2:2 + NP_TOK], bank[b][0][:, 0:P], ACT.Identity, bias=bias(n))
                    act.activation(raw[b][:, S_RAW:S_RAW + CUT], bank[b][0][:, P:P + CUT], ACT.Identity, bias=bias(n))
                    act.activation(raw[b][:, S_RAW + CUT:S_RAW + NS_TOK], bank[b][1][:, 0:NS_TOK - CUT],
                                   ACT.Identity, bias=bias(n)).then_inc(s["evac"], 1)

                def silu(n, out):
                    act.wait_ge(s["conv"], n + 3)
                    act.activation(out[:, 0:NP_TOK], cv[:, 0:NP_TOK], ACT.Silu)
                    act.activation(out[:, NP_TOK:T], cv[:, S_CV:S_CV + NS_TOK], ACT.Silu).then_inc(s["silu"], 1)

                def roots(i, base, u):
                    n = i * 4 + (base + u)
                    act.wait_ge(s["ones"], n + 2)
                    act.wait_ge(s["normed"], n + 1)
                    sc, bi = k.chan[:, bass.ds(n + V_L2S, 1)], k.chan[:, bass.ds(n + V_L2B, 1)]
                    act.activation(rt[:, 0:NP_TOK], k.bank[5][:, 0:P], ACT.Sqrt, bias=bi, scale=sc)
                    act.activation(rt[:, NP_TOK:T], k.bank[4][:], ACT.Sqrt, bias=bi, scale=sc
                                   ).then_inc(s["root"], 1)

                def qk_tile(i, base, u):
                    to_raw(i, base, u)
                    high(i, base + 2, u)
                    roots(i, base - 1, u)
                    silu(i * 4 + (base + u), sl[(base + u) % 2])

                high(0, 0, 0)
                high(0, 1, 0)
                act.wait_ge(s["raw_zeroed"], 1)
                to_raw(0, 0, 0)
                high(0, 2, 0)
                silu(0, sl[0])
                with act.Fori(0, QK_TILES // 4 - 1) as i:
                    for u in range(4):
                        qk_tile(i, 1, u)
                for u in range(3):
                    qk_tile(0, QK_TILES - 3, u)
                for u in range(V_TILES):
                    to_raw(0, QK_TILES, u)
                    high(0, QK_TILES + 2, u)
                    if u == 0:
                        roots(0, QK_TILES - 1, 0)
                    wait_store(act, 0, QK_TILES, u)
                    silu(QK_TILES + u, ob[u % 2])

                def plain_tile(i, base, u, perm):
                    n, b = i * 4 + (base + u), u % 2
                    act.wait_ge(s["proj_summed"], n + 1)
                    wait_store(act, i, base, u)
                    if perm:
                        act.activation(ob[b][:, 0:NP_TOK], bank[b][0][:, 0:P], ACT.Identity, bias=bias(n))
                        to_columns(ob[b], bank[b], bias(n)).then_inc(s["evac"], 1)
                    else:
                        for c, (lo, hi) in enumerate(CHUNKS):
                            ev = act.activation(ob[b][:, lo:hi], bank[b][c][:, 0:hi - lo], ACT.Identity,
                                                bias=bias(n))
                        ev.then_inc(s["evac"], 1)
                    if isinstance(i, int) and base + u + 2 > GATE_TILE:
                        return
                    high(i, base + 2, u)

                def to_columns(out, banks, b, r0=0, r1=P):
                    out = out[r0:r1, NP_TOK:T].rearrange("p (c r) -> p r c", r=ROWS)
                    cut = CUT // GRID_W
                    for dst, src in ((out[:, 0:cut, :], banks[0][r0:r1, P:P + CUT]),
                                     (out[:, cut:ROWS, :], banks[1][r0:r1, 0:NS_TOK - CUT])):
                        ev = act.activation(dst, src.rearrange("p (r c) -> p r c", c=GRID_W), ACT.Identity, bias=b)
                    return ev

                with act.Fori(0, PERM_TILES // 4) as i:
                    for u in range(4):
                        plain_tile(i, T_MLQ, u, True)
                with act.Fori(0, RASTER_TILES // 4 - 1) as i:
                    for u in range(4):
                        plain_tile(i, T_Z, u, False)
                for u in range(4):
                    plain_tile(0, N_TILES - 4, u, False)
                act.wait_ge(s["proj_summed"], GATE_TILE + 1)
                gate_banks = bank[GATE_TILE % 2]
                act.activation(gm[:, 0:NP_TOK], gate_banks[0][0:48, 0:P], ACT.Identity, bias=bias(GATE_TILE)[0:48])
                act.activation(gm[0:32, NP_TOK:NP_TOK + CUT], gate_banks[0][0:32, P:P + CUT], ACT.Identity,
                               bias=bias(GATE_TILE)[0:32])
                act.activation(gm[0:32, NP_TOK + CUT:T], gate_banks[1][0:32, 0:NS_TOK - CUT], ACT.Identity,
                               bias=bias(GATE_TILE)[0:32])
                to_columns(gm, gate_banks, bias(GATE_TILE)[32:48], 32, 48)
                act.drain().then_inc(s["gates_read"], 1)

            @block.vector
            def _(dve):
                dve.sem_inc(s["win_low"], 4)
                dve.sem_inc(s["conv"], 2)
                dve.sem_inc(s["normed"], 1)

                def low(i, base, u):
                    v = base + u
                    dve.wait_ge(s["win_high"], i * 4 + (v + 1))
                    dve.tensor_tensor(w_lo[v % 2][:], w[:, v % 4], w_hi[v % 2][:].bitcast(F32), ALU.subtract
                                      ).then_inc(s["win_low"], 1)

                def convolve(i, base, u):
                    n = i * 4 + (base + u)
                    dve.wait_ge(s["evac"], n + 3)
                    dve.wait_ge(s["silu"], n + 1)
                    for j in range(5):
                        tap = k.chan[:, bass.ds(n * 5 + (V_CONV + j), 1)]
                        src = raw[(base + u) % 2][:, j:j + CV]
                        if j == 0:
                            dve.tensor_scalar(cv[:], src, tap, None, ALU.mult)
                        else:
                            last = dve.scalar_tensor_tensor(out=cv[:], in0=src, scalar=tap, in1=cv[:],
                                                            op0=ALU.mult, op1=ALU.add)
                        if j < 4:
                            dve.drain()
                    last.then_inc(s["conv"], 1)

                def square(i, base, u):
                    n = i * 4 + (base + u)
                    dve.wait_ge(s["silu"], n + 2)
                    dve.wait_ge(s["ones"], n + 1)
                    dve.tensor_tensor(sq[:], sl[(base + u) % 2][:], sl[(base + u) % 2][:], ALU.mult
                                      ).then_inc(s["sq"], 1)

                def normalize(i, base, u):
                    b = (base + u) % 2
                    dve.wait_ge(s["root"], i * 4 + (base + u) + 2)
                    dve.reciprocal(rt[:], rt[:])
                    dve.drain()
                    dve.wait_ge(stored[b], i * 32 + 16 * ((base + u) // 2 + 1))
                    dve.tensor_tensor(ob[b][:], sl[b][:], rt[:], ALU.mult).then_inc(s["normed"], 1)

                def qk_tile(i, base, u):
                    convolve(i, base, u)
                    low(i, base + 2, u)
                    square(i, base, u)
                    normalize(i, base - 1, u)

                low(0, 0, 0)
                low(0, 1, 0)
                for b in range(2):
                    dve.memset(raw[b][:], 0.0)
                dve.drain().then_inc(s["raw_zeroed"], 1)
                convolve(0, 0, 0)
                low(0, 2, 0)
                square(0, 0, 0)
                with dve.Fori(0, QK_TILES // 4 - 1) as i:
                    for u in range(4):
                        qk_tile(i, 1, u)
                for u in range(3):
                    qk_tile(0, QK_TILES - 3, u)
                for u in range(V_TILES):
                    convolve(0, QK_TILES, u)
                    low(0, QK_TILES + 2, u)
                    if u == 0:
                        normalize(0, QK_TILES - 1, 0)
                rest = GATE_TILE + 1 - (T_MLQ + 2)
                with dve.Fori(0, rest // 4) as i:
                    for u in range(4):
                        low(i, T_MLQ + 2, u)
                for u in range(rest % 4):
                    low(0, GATE_TILE + 1 - rest % 4, u)
                dve.wait_ge(s["gates_turned"], 1)
                dve.tensor_copy(k.gates[:], k.bank[6][:, 0:TT * 48].rearrange("p (t n) -> p t n", t=TT))

            @block.sync
            def _(sp):
                for b in range(2):
                    sp.sem_inc(stored[b], 16)
                for base, tiles, sem, ahead in ((0, QK_TILES, "normed", 2), (QK_TILES, V_TILES, "silu", 2),
                                                (T_MLQ, PERM_TILES + RASTER_TILES, "evac", 3)):
                    with sp.Fori(0, tiles // 4) as i:
                        for u in range(4):
                            n = i * 4 + (base + u)
                            sp.wait_ge(s[sem], n + ahead)
                            sp.dma_start(k.d_proj[bass.ds(n, 1)].rearrange("a p t -> p (a t)"), ob[u % 2][:]
                                         ).then_inc(stored[u % 2], 16)
                for b in range(2):
                    sp.wait_ge(stored[b], 16 * (N_TILES // 2 + 1))


def phase_gates(nc, k):
    with ExitStack() as mem:
        def sb(name, shape):
            return mem.enter_context(nc.sbuf_tensor(name, shape, F32))
        x24 = sb("gate_x", [P, TT, 24])
        e24 = sb("gate_e", [P, TT, 24])
        l24 = sb("gate_l", [P, TT, 24])
        gg = sb("gate_gg", [P, TT, 24])
        al = sb("gate_al", [P, 16])
        bf = k.sem("gates_by_vector")
        ba = k.sem("gates_by_scalar")
        bp = k.sem("gates_by_tensor")
        with nc.Block() as block:
            @block.vector
            def _(dve):
                dve.tensor_tensor(x24[:, :, 0:16], k.gates[:, :, 16:32], all_heads(k.rowp[:, R_DT:R_DT + 16], TT),
                                  ALU.add)
                dve.scalar_tensor_tensor(out=x24[:, :, 16:24], in0=k.gates[:, :, 40:48], scalar=-1.0,
                                         in1=all_heads(k.rowp[:, R_FB:R_FB + 8], TT), op0=ALU.mult, op1=ALU.subtract)
                dve.tensor_tensor(k.ci[:], k.gates[:, :, 32:40], all_heads(k.rowp[:, R_IB:R_IB + 8], TT), ALU.add)
                dve.drain()
                dve.scalar_tensor_tensor(out=e24[:], in0=x24[:], scalar=-1.0, in1=x24[:], op0=ALU.mult, op1=ALU.min
                                         ).then_inc(bf, 1)
                dve.wait_ge(ba, 1)
                dve.scalar_tensor_tensor(out=gg[:], in0=x24[:], scalar=0.0, in1=l24[:], op0=ALU.max, op1=ALU.add)
                dve.drain()
                dve.scalar_tensor_tensor(out=gg[:, :, 0:16], in0=gg[:, :, 0:16], scalar=-1.0,
                                         in1=all_heads(al[:], TT), op0=ALU.mult, op1=ALU.mult)
                dve.tensor_scalar(gg[:, :, 16:24], gg[:, :, 16:24], -1.0, None, ALU.mult)
                dve.drain().then_inc(bf, 1)
                dve.wait_ge(bp, 1)
                cum = [k.bank[d][:, 0:TT * 24].rearrange("p (t n) -> p t n", t=TT) for d in range(3)]
                for d in range(2):
                    dve.tensor_copy(k.G[:, :, 8 * d:8 * d + 8], cum[d][:, :, 8 * d:8 * d + 8])
                    dve.tensor_copy(k.b_ml[:, :, 4 * d:4 * d + 4], cum[d][:, :, 16 + 4 * d:20 + 4 * d])
                dve.tensor_copy(k.g_tot[:], cum[2][:, :, 0:16])
                dve.tensor_copy(k.b_tot[:], cum[2][:, :, 16:24])
                dve.drain()
                dve.tensor_scalar(k.nG[:], k.G[:], -1.0, None, ALU.mult)
                dve.tensor_tensor(k.wS[:], k.g_tot[:], k.G[:], ALU.subtract)
                dve.tensor_tensor(k.ci[:], k.ci[:], k.b_ml[:], ALU.subtract)
                dve.drain().then_inc(bf, 1)
                dve.wait_ge(ba, 2)
                dve.tensor_scalar(k.neg_eG[:], k.eG[:], -1.0, None, ALU.mult)
                dve.tensor_tensor(k.bw[:], k.beta[:], k.wS[:], ALU.mult)

            @block.scalar
            def _(act):
                act.activation(k.beta[:], k.gates[:, :, 0:16], ACT.Sigmoid)
                act.activation(al[:], k.rowp[:, R_AL:R_AL + 16], ACT.Exp)
                act.wait_ge(bf, 1)
                act.activation(e24[:], e24[:], ACT.Exp)
                act.drain()
                act.activation(l24[:], e24[:], ACT.Ln, bias=1.0)
                act.drain().then_inc(ba, 1)
                act.wait_ge(bf, 3)
                act.activation(k.eG[:], k.G[:], ACT.Exp)
                act.activation(k.wS[:], k.wS[:], ACT.Exp)
                act.activation(k.eT[:], k.g_tot[:], ACT.Exp)
                act.drain().then_inc(ba, 1)

            @block.tensor
            def _(pe):
                pe.wait_ge(bf, 2)
                for d, lhs in enumerate((k.tri[0], k.tri[1], k.ones)):
                    mm = pe.matmul(k.bank[d][:, 0:TT * 24], lhs, gg[:].rearrange("p t n -> p (t n)"),
                                   start=True, stop=True)
                mm.then_inc(bp, 1)


A_FILLS = (["kT", "G", "KK", "L1"] + [f"{x}{s}" for s in LEVELS[1:] for x in ("Y", "XT")] + ["KS", "P", "O"])
B_FILLS = (["vT", "QK"] + [f"XY{s}" for s in LEVELS[1:]] + ["QS", "S"])


def phase_deltanet(nc, k):
    with ExitStack() as mem:
        def sb(name, shape):
            return mem.enter_context(nc.sbuf_tensor(name, shape, F32))

        def quads(name):
            return [sb(f"{name}{q}", [P, 4, P]) for q in range(4)]
        staged = [sb(f"dn_staged{d}", [P, 24, P]) for d in range(2)]
        ktok, vtok, dg, DT, NT, sc = (quads(n) for n in ("ktok", "vtok", "diagG", "decayT", "LT", "scoresT"))
        X, XT, R, vn, vs = (quads(n) for n in ("X", "XT", "R", "vnew", "vweighted"))
        Y = [sb(f"Y{q}", [P, 4, P // 2]) for q in range(4)]
        S = [[sb(f"S{'ps'[x]}{q}", [P, 4, P]) for q in range(4)] for x in range(2)]
        A = [Bank(k.bank[q], k.sem(f"dnA_filled{q}"), k.sem(f"dnA_emptied{q}"), A_FILLS) for q in range(4)]
        B = [Bank(k.bank[4 + q], k.sem(f"dnB_filled{q}"), k.sem(f"dnB_emptied{q}"), B_FILLS) for q in range(4)]
        landed = [k.sem(f"dn_landed{d}") for d in range(2)]
        used = [k.sem(f"dn_stage_used{d}") for d in range(2)]
        zeroed, state_in, prompt_done, state_out = (k.sem(n) for n in ("dn_zeroed", "dn_state_in", "dn_prompt_done",
                                                                       "dn_state_out"))
        dg_ready = [k.sem(f"dg_ready{q}") for q in range(4)]
        QUADS = [(q, q % 2, 4 * (q // 2)) for q in range(4)]

        def sources(ap, s, d):
            return ap.rearrange("p (b two s) -> p b two s", two=2, s=s)[:, :, d, :]

        def steps(eng, body):
            body(0, (0, 0), 0)
            with eng.Fori(0, TT - 1) as i:
                body(i + 1, (i + 1, i * -1 + (TT - 1)), 1)

        with nc.Block() as block:
            @block.sync
            def _(sp):
                for q, d, h0 in QUADS:
                    sp.dma_start(S[1][q][:], k.d_sdn[d, h0:h0 + 4].rearrange("h p n -> p h n")).then_inc(state_in, 16)

                def load(step, tiles, _):
                    for d in range(2):
                        if not isinstance(step, int):
                            sp.wait_ge(used[d], step * 2)
                        sp.dma_start(staged[d][:], k.d_proj.rearrange("m p t -> p m t")[
                            :, 0:24, bass.ds(tiles[d] * P, P)]).then_inc(landed[d], 16)
                steps(sp, load)
                sp.wait_ge(prompt_done, 4)
                for q, d, h0 in QUADS:
                    sp.dma_start(k.o_sdn[d, h0:h0 + 4].rearrange("h p n -> p h n"), S[0][q][:]
                                 ).then_inc(state_out, 16)
                sp.wait_ge(state_out, 64)

            @block.gpsimd
            def _(pool):
                pool.memset(k.o_dn[:], 0.0)
                for q in range(4):
                    pool.memset(S[0][q][:], 0.0)
                pool.drain().then_inc(zeroed, 1)

                def diagonals(step, tiles, _):
                    for q, d, h0 in QUADS:
                        if not isinstance(step, int):
                            A[q].wait_filled(pool, step + -1, "G")
                        c = d * 8 + h0
                        pool.tensor_tensor(dg[q][:], all_heads(k.ident), per_head(col(k.G[:], tiles[d], c, c + 4), P),
                                           ALU.mult).then_inc(dg_ready[q], 1)
                steps(pool, diagonals)

            @block.tensor
            def _(pe):
                def fill(bank, step, name, args, width=P):
                    bank.wait_free(pe, step, name)
                    for h in range(4):
                        terms = args(h)
                        for n, (lhs, rhs) in enumerate(terms):
                            mm = pe.matmul(bank.t[:, h * width:(h + 1) * width], lhs, rhs, start=(n == 0),
                                           stop=(n == len(terms) - 1))
                    mm.then_inc(bank.filled, 1)

                def turn(bank, step, name, src):
                    bank.wait_free(pe, step, name)
                    for h in range(4):
                        mm = pe.transpose(bank.t[:, h * P:(h + 1) * P], src(h), k.ident)
                    mm.then_inc(bank.filled, 1)

                def body(step, tiles, x):
                    for q, d, h0 in QUADS:
                        pe.wait_ge(landed[d], step * 16 + 16)
                        turn(A[q], step, "kT", lambda h: staged[d][:, 8 + h0 + h, :])
                        turn(B[q], step, "vT", lambda h: staged[d][:, 16 + h0 + h, :])
                    for q, d, h0 in QUADS:
                        pe.wait_ge(dg_ready[q], step + 1)
                        fill(A[q], step, "G", lambda h: [(k.ones, dg[q][:, h, :]), (k.ident, k.neg[d])])
                    for q, d, h0 in QUADS:
                        kh = lambda h: staged[d][:, 8 + h0 + h, :]
                        fill(A[q], step, "KK", lambda h: [(kh(h), kh(h))])
                        fill(B[q], step, "QK", lambda h: [(kh(h), staged[d][:, h0 + h, :])])
                    for q, d, h0 in QUADS:
                        A[q].wait_emptied(pe, step, "KK")
                        turn(A[q], step, "L1", lambda h: NT[q][:, h, :])
                    for s in LEVELS[1:]:
                        for q, d, h0 in QUADS:
                            if s > 2:
                                B[q].wait_emptied(pe, step, f"XY{s // 2}")
                                turn(A[q], step, f"XT{s // 2}", lambda h: X[q][:, h, :])
                        for q, d, h0 in QUADS:
                            fill(A[q], step, f"Y{s}", lambda h: [(NT[q][:, h, :], sources(X[q][:, h, :], s, d))],
                                 P // 2)
                        for q, d, h0 in QUADS:
                            A[q].wait_emptied(pe, step, f"Y{s}")
                            fill(B[q], step, f"XY{s}", lambda h: [(XT[q][:, h, :], Y[q][:, h, :])], P // 2)
                    for q, d, h0 in QUADS:
                        B[q].wait_emptied(pe, step, f"XY{LEVELS[-1]}")
                        turn(A[q], step, f"XT{LEVELS[-1]}", lambda h: X[q][:, h, :])
                    pe.wait_ge(zeroed, 1) if x == 0 else pe.wait_ge(state_in, 64)
                    for q, d, h0 in QUADS:
                        fill(B[q], step, "QS", lambda h: [(staged[d][:, h0 + h, :], S[x][q][:, h, :])])
                        fill(A[q], step, "KS", lambda h: [(staged[d][:, 8 + h0 + h, :], S[x][q][:, h, :])])
                    for q, d, h0 in QUADS:
                        A[q].wait_filled(pe, step, "KS")
                        pe.sem_inc(used[d], 1)
                        fill(A[q], step, "P", lambda h: [(XT[q][:, h, :], R[q][:, h, :])])
                    for q, d, h0 in QUADS:
                        fill(A[q], step, "O", lambda h: [(sc[q][:, h, :], vn[q][:, h, :])])
                        fill(B[q], step, "S", lambda h: [(ktok[q][:, h, :], vs[q][:, h, :])])
                steps(pe, body)

            @block.scalar
            def _(act):
                def body(step, tiles, x):
                    for q, d, h0 in QUADS:
                        A[q].wait_filled(act, step, "kT")
                        act.activation(ktok[q][:], h4(A[q].t[:]), ACT.Copy).then_inc(A[q].emptied, 1)
                        B[q].wait_filled(act, step, "vT")
                        act.activation(vtok[q][:], h4(B[q].t[:]), ACT.Copy).then_inc(B[q].emptied, 1)
                    for q, d, h0 in QUADS:
                        A[q].wait_filled(act, step, "G")
                        for h in range(4):
                            c = d * 8 + h0 + h
                            ex = act.activation(DT[q][:, h, :], A[q].t[:, h * P:(h + 1) * P], ACT.Exp,
                                                bias=col(k.nG[:], tiles[d], c, c + 1))
                        ex.then_inc(A[q].emptied, 1)
                    for s in LEVELS[1:]:
                        for q, d, h0 in QUADS:
                            A[q].wait_filled(act, step, f"XT{s}")
                            act.activation(XT[q][:], h4(A[q].t[:]), ACT.Copy).then_inc(A[q].emptied, 1)
                    for q, d, h0 in QUADS:
                        A[q].wait_filled(act, step, "P")
                        for h in range(4):
                            c = d * 8 + h0 + h
                            act.activation(vn[q][:, h, :], A[q].t[:, h * P:(h + 1) * P], ACT.Copy,
                                           scale=col(k.beta[:], tiles[d], c, c + 1))
                            ex = act.activation(vs[q][:, h, :], A[q].t[:, h * P:(h + 1) * P], ACT.Copy,
                                                scale=col(k.bw[:], tiles[d], c, c + 1))
                        ex.then_inc(A[q].emptied, 1)
                steps(act, body)

            @block.vector
            def _(dve):
                dve.wait_ge(zeroed, 1)
                dve.wait_ge(state_in, 64)

                def body(step, tiles, x):
                    for q, d, h0 in QUADS:
                        A[q].wait_filled(dve, step, "KK")
                        A[q].wait_emptied(dve, step, "G")
                        for h in range(4):
                            c = d * 8 + h0 + h
                            op = dve.scalar_tensor_tensor(
                                out=NT[q][:, h, :], in0=A[q].t[:, h * P:(h + 1) * P],
                                scalar=col(k.beta[:], tiles[d], c, c + 1), in1=DT[q][:, h, :],
                                op0=ALU.mult, op1=ALU.mult)
                        op.then_inc(A[q].emptied, 1)
                        B[q].wait_filled(dve, step, "QK")
                        dve.tensor_tensor(sc[q][:], h4(B[q].t[:]), DT[q][:], ALU.mult).then_inc(B[q].emptied, 1)
                    for q, d, h0 in QUADS:
                        A[q].wait_filled(dve, step, "L1")
                        dve.tensor_tensor(XT[q][:], NT[q][:], all_heads(k.level1(d)), ALU.mult)
                        dve.tensor_tensor(X[q][:], h4(A[q].t[:]), all_heads(k.level1(1 - d)), ALU.mult)
                        dve.drain()
                        dve.tensor_tensor(XT[q][:], all_heads(k.ident), XT[q][:], ALU.subtract)
                        dve.tensor_tensor(X[q][:], all_heads(k.ident), X[q][:], ALU.subtract
                                          ).then_inc(A[q].emptied, 1)
                    for n, s in enumerate(LEVELS[1:], 1):
                        for q, d, h0 in QUADS:
                            A[q].wait_filled(dve, step, f"Y{s}")
                            dve.tensor_tensor(Y[q][:], A[q].t[:, 0:2 * P].rearrange("p (h n) -> p h n", h=4),
                                              all_heads(k.level(d, n)), ALU.mult).then_inc(A[q].emptied, 1)
                        for q, d, h0 in QUADS:
                            B[q].wait_filled(dve, step, f"XY{s}")
                            xs = sources(X[q][:].rearrange("p h n -> p (h n)"), s, d)
                            dve.tensor_tensor(xs, xs, B[q].t[:, 0:2 * P].rearrange("p (b s) -> p b s", s=s),
                                              ALU.subtract).then_inc(B[q].emptied, 1)
                    for q, d, h0 in QUADS:
                        B[q].wait_filled(dve, step, "QS")
                        if x == 0 and d == 1:
                            dve.drain()
                        for h in range(4):
                            c = d * 8 + h0 + h
                            o = col(k.o_dn[:], tiles[d], (h0 + h) * P, (h0 + h + 1) * P)
                            op = dve.scalar_tensor_tensor(out=o, in0=B[q].t[:, h * P:(h + 1) * P],
                                                          scalar=col(k.eG[:], tiles[d], c, c + 1), in1=o,
                                                          op0=ALU.mult, op1=ALU.add)
                        op.then_inc(B[q].emptied, 1)
                        A[q].wait_filled(dve, step, "KS")
                        A[q].wait_emptied(dve, step, "kT")
                        B[q].wait_emptied(dve, step, "vT")
                        for h in range(4):
                            c = d * 8 + h0 + h
                            op = dve.scalar_tensor_tensor(out=R[q][:, h, :], in0=A[q].t[:, h * P:(h + 1) * P],
                                                          scalar=col(k.neg_eG[:], tiles[d], c, c + 1),
                                                          in1=vtok[q][:, h, :], op0=ALU.mult, op1=ALU.add)
                        op.then_inc(A[q].emptied, 1)
                    dve.drain()
                    for q, d, h0 in QUADS:
                        A[q].wait_filled(dve, step, "O")
                        if x == 0 and d == 1:
                            dve.drain()
                        o = col(k.o_dn[:], tiles[d], h0 * P, (h0 + 4) * P)
                        dve.tensor_tensor(o, o, A[q].t[:], ALU.add).then_inc(A[q].emptied, 1)
                        B[q].wait_filled(dve, step, "S")
                        for h in range(4):
                            c = d * 8 + h0 + h
                            op = dve.scalar_tensor_tensor(out=S[x][q][:, h, :], in0=S[x][q][:, h, :],
                                                          scalar=col(k.eT[:], tiles[d], c, c + 1),
                                                          in1=B[q].t[:, h * P:(h + 1) * P], op0=ALU.mult, op1=ALU.add)
                        op.then_inc(B[q].emptied, 1)
                    dve.drain()
                    if x == 0:
                        dve.sem_inc(prompt_done, 4)
                steps(dve, body)


M_FILLS = {"A": ["kT", "QK", "NP1", "NP3"], "B": ["v01", "NQ0", "NQ2", "S0", "S2"],
           "C": ["v23", "NQ1", "NQ3", "S1", "S3"], "D": ["Cbc", "Mbc", "NP0", "NP2"]}


def phase_mlstm(nc, k):
    DA = DV_ML + 1
    with ExitStack() as mem:
        def sb(name, shape):
            return mem.enter_context(nc.sbuf_tensor(name, shape, F32))

        def dirs(name, shape):
            return [sb(f"{name}{d}", shape) for d in range(2)]
        staged = dirs("ml_staged", [P, 16, P])
        ktok, dg, dgM, ET, PT, kw = (dirs(n, [P, 4, P]) for n in ("ml_ktok", "diagC", "diagM", "expT", "pT", "kweighted"))
        vtok = dirs("ml_vtok", [P, 4, DA])
        nu = dirs("numerator", [P, 4, DA])
        S = [dirs(f"C{'ps'[x]}", [P, 4, DA]) for x in range(2)]
        m = [dirs(f"m{'ps'[x]}", [P, 4]) for x in range(2)]
        M, nM, mx, nMl, inter, enm, carry, wS, rden, bM = (
            dirs(n, [P, 4]) for n in ("M", "negM", "maxC", "negMend", "inter", "exp_neg_m", "carry", "wend",
                                      "rden", "bM"))
        bank = [{f: Bank(k.bank[4 * d + n], k.sem(f"ml{f}_filled{d}"), k.sem(f"ml{f}_emptied{d}"), M_FILLS[f])
                 for n, f in enumerate("ABCD")} for d in range(2)]
        landed = [k.sem(f"ml_landed{d}") for d in range(2)]
        sems = ("ready", "dgC", "dgM", "max", "expo", "scalars", "kw", "nu", "den")
        s = [{n: k.sem(f"ml_{n}{d}") for n in sems} for d in range(2)]
        state_in, state_out, prompt_done = k.sem("ml_state_in"), k.sem("ml_state_out"), k.sem("ml_prompt_done")
        END = (P - 1, 0)

        def steps(eng, body):
            body(0, (0, 0), 0)
            with eng.Fori(0, TT - 1) as i:
                body(i + 1, (i + 1, i * -1 + (TT - 1)), 1)

        def gate(t3, tiles, d, h=None):
            a, b = (4 * d, 4 * d + 4) if h is None else (4 * d + h, 4 * d + h + 1)
            return col(t3[:], tiles[d], a, b)

        with nc.Block() as block:
            @block.sync
            def _(sp):
                for d in range(2):
                    sp.dma_start(S[1][d][:, :, 0:DV_ML], k.d_smc[d].rearrange("h p n -> p h n")).then_inc(state_in, 16)
                    for h in range(4):
                        sp.dma_start(S[1][d][:, h, DV_ML:DA], k.d_smn[d, h:h + 1, :].rearrange("a p -> p a")
                                     ).then_inc(state_in, 16)

                def load(step, tiles, _):
                    for d in range(2):
                        if not isinstance(step, int):
                            bank[d]["A"].wait_filled(sp, step + -1, "NP3")
                        sp.dma_start(staged[d][:], k.d_proj.rearrange("m p t -> p m t")[
                            :, T_MLQ:T_MLQ + 16, bass.ds(tiles[d] * P, P)]).then_inc(landed[d], 16)
                steps(sp, load)
                sp.wait_ge(prompt_done, 1)
                for d in range(2):
                    sp.dma_start(k.o_smc[d].rearrange("h p n -> p h n"), S[0][d][:, :, 0:DV_ML]).then_inc(state_out, 16)
                    for h in range(4):
                        sp.dma_start(k.o_smn[d, h:h + 1, :].rearrange("a p -> p a"), S[0][d][:, h, DV_ML:DA]
                                     ).then_inc(state_out, 16)
                    sp.dma_start(k.o_smm[d:d + 1, :], m[0][d][0:1, :]).then_inc(state_out, 16)
                sp.wait_ge(state_out, 16 * 12)

            @block.gpsimd
            def _(pool):
                for d in range(2):
                    pool.memset(vtok[d][:], 1.0)
                    pool.memset(S[0][d][:], 0.0)
                    pool.memset(m[0][d][:], 0.0)
                pool.memset(k.o_ml[:], 0.0)
                pool.drain().then_inc(s[0]["ready"], 1)

                def body(step, tiles, _):
                    for d in range(2):
                        if not isinstance(step, int):
                            bank[d]["D"].wait_filled(pool, step + -1, "Cbc")
                        pool.tensor_tensor(dg[d][:], all_heads(k.ident), per_head(gate(k.ci, tiles, d), P), ALU.mult
                                           ).then_inc(s[d]["dgC"], 1)
                steps(pool, body)

            @block.tensor
            def _(pe):
                pe.wait_ge(s[0]["ready"], 1)

                def body(step, tiles, x):
                    for d in range(2):
                        b = bank[d]
                        pe.wait_ge(landed[d], step * 16 + 16)
                        b["A"].wait_free(pe, step, "kT")
                        for h in range(4):
                            mm = pe.transpose(b["A"].t[:, h * P:(h + 1) * P], staged[d][:, 4 + h, :], k.ident)
                        mm.then_inc(b["A"].filled, 1)
                        for n, f in enumerate("BC"):
                            b[f].wait_free(pe, step, ("v01", "v23")[n])
                            for j in range(4):
                                mm = pe.transpose(b[f].t[:, j * P:(j + 1) * P], staged[d][:, 8 + 4 * n + j, :], k.ident)
                            mm.then_inc(b[f].filled, 1)
                        pe.wait_ge(s[d]["dgC"], step + 1)
                        b["D"].wait_free(pe, step, "Cbc")
                        for h in range(4):
                            o = b["D"].t[:, h * P:(h + 1) * P]
                            pe.matmul(o, k.ones, dg[d][:, h, :], start=True, stop=False)
                            mm = pe.matmul(o, k.ident, k.neg[1 - d], start=False, stop=True)
                        mm.then_inc(b["D"].filled, 1)
                    for d in range(2):
                        b = bank[d]
                        b["A"].wait_free(pe, step, "QK")
                        for h in range(4):
                            mm = pe.matmul(b["A"].t[:, h * P:(h + 1) * P], staged[d][:, 4 + h, :], staged[d][:, h, :],
                                           start=True, stop=True)
                        mm.then_inc(b["A"].filled, 1)
                    for d in range(2):
                        b = bank[d]
                        pe.wait_ge(s[d]["dgM"], step + 1)
                        b["D"].wait_free(pe, step, "Mbc")
                        for h in range(4):
                            o = b["D"].t[:, h * P:(h + 1) * P]
                            pe.matmul(o, k.ones, dgM[d][:, h, :], start=True, stop=False)
                            mm = pe.matmul(o, k.ident, k.neg[d], start=False, stop=True)
                        mm.then_inc(b["D"].filled, 1)
                    if x == 1:
                        pe.wait_ge(state_in, 16 * 10)
                    for h in range(4):
                        for d in range(2):
                            b = bank[d]
                            fq, fp = ("B", "D") if h % 2 == 0 else ("C", "A")
                            b[fq].wait_free(pe, step, f"NQ{h}")
                            if h == 0:
                                b["C"].wait_free(pe, step, "NQ1")
                            pe.matmul(b[fq].t[:, 0:DA], staged[d][:, h, :], S[x][d][:, h, :], start=True, stop=True
                                      ).then_inc(b[fq].filled, 1)
                            b["A"].wait_emptied(pe, step, "QK")
                            b[fp].wait_free(pe, step, f"NP{h}")
                            pe.matmul(b[fp].t[:, 0:DA], PT[d][:, h, :], vtok[d][:, h, :], start=True, stop=True
                                      ).then_inc(b[fp].filled, 1)
                    for h in range(4):
                        for d in range(2):
                            b = bank[d]
                            f = "BC"[h % 2]
                            pe.wait_ge(s[d]["kw"], step + 1)
                            b[f].wait_free(pe, step, f"S{h}")
                            pe.matmul(b[f].t[:, 0:DA], kw[d][:, h, :], vtok[d][:, h, :], start=True, stop=True
                                      ).then_inc(b[f].filled, 1)
                steps(pe, body)

            @block.scalar
            def _(act):
                act.wait_ge(s[0]["ready"], 1)

                def body(step, tiles, x):
                    for d in range(2):
                        b = bank[d]
                        b["A"].wait_filled(act, step, "kT")
                        if not isinstance(step, int):
                            act.wait_ge(s[d]["kw"], step)
                        act.activation(ktok[d][:], h4(b["A"].t[:]), ACT.Copy).then_inc(b["A"].emptied, 1)
                        for n, f in enumerate("BC"):
                            b[f].wait_filled(act, step, ("v01", "v23")[n])
                            act.activation(vtok[d][:, 2 * n:2 * n + 2, 0:DV_ML],
                                           b[f].t[:].rearrange("p (h n) -> p h n", h=2), ACT.Copy
                                           ).then_inc(b[f].emptied, 1)
                    for d in range(2):
                        b = bank[d]
                        b["D"].wait_filled(act, step, "Mbc")
                        if not isinstance(step, int):
                            act.wait_ge(s[d]["scalars"], step)
                        act.activation(nMl[d][:].unsqueeze(2), h4(b["D"].t[:])[:, :, END[d]:END[d] + 1], ACT.Copy)
                        for h in range(4):
                            act.activation(ET[d][:, h, :], b["D"].t[:, h * P:(h + 1) * P], ACT.Exp,
                                           bias=gate(k.ci, tiles, d, h))
                        act.drain().then_inc(b["D"].emptied, 1)
                    for d in range(2):
                        act.wait_ge(s[d]["expo"], step + 1)
                        for t4 in (inter, enm, carry, wS):
                            act.activation(t4[d][:], t4[d][:], ACT.Exp)
                        act.drain().then_inc(s[d]["scalars"], 1)
                    for h in range(4):
                        for d in range(2):
                            fq = "BC"[h % 2]
                            bank[d][fq].wait_filled(act, step, f"NQ{h}")
                            act.activation(nu[d][:, h, :], bank[d][fq].t[:, 0:DA], ACT.Copy,
                                           scale=inter[d][:, h:h + 1]).then_inc(bank[d][fq].emptied, 1)
                steps(act, body)

            @block.vector
            def _(dve):
                dve.wait_ge(s[0]["ready"], 1)
                for d in range(2):
                    dve.tensor_copy(m[1][d][:], k.rowp[:, R_M0 + 4 * d:R_M0 + 4 * d + 4])
                dve.drain()

                def body(step, tiles, x):
                    for d in range(2):
                        b = bank[d]
                        b["D"].wait_filled(dve, step, "Cbc")
                        dve.tensor_reduce(mx[d][:], h4(b["D"].t[:]), AX.X, ALU.max).then_inc(b["D"].emptied, 1)
                        dve.drain()
                        dve.tensor_tensor(M[d][:], mx[d][:], m[x][d][:], ALU.max)
                        dve.drain()
                        dve.tensor_scalar(nM[d][:], M[d][:], -1.0, None, ALU.mult)
                        dve.tensor_tensor(inter[d][:], m[x][d][:], M[d][:], ALU.subtract)
                        dve.tensor_tensor(bM[d][:], M[d][:], gate(k.b_ml, tiles, d), ALU.add)
                        dve.drain()
                        dve.tensor_scalar(enm[d][:], bM[d][:], -1.0, None, ALU.mult)
                        dve.tensor_tensor(dgM[d][:], all_heads(k.ident), per_head(nM[d][:], P), ALU.mult
                                          ).then_inc(s[d]["dgM"], 1)
                    for d in range(2):
                        b = bank[d]
                        b["D"].wait_emptied(dve, step, "Mbc")
                        dve.tensor_tensor(carry[d][:], m[x][d][:], nMl[d][:], ALU.add)
                        dve.tensor_tensor(wS[d][:], gate(k.ci, tiles, d), nMl[d][:], ALU.add)
                        dve.drain().then_inc(s[d]["expo"], 1)
                        dve.tensor_tensor(m[x][d][:], gate(k.b_tot, tiles, d), nMl[d][:], ALU.subtract)
                        b["A"].wait_filled(dve, step, "QK")
                        dve.scalar_tensor_tensor(out=PT[d][:], in0=h4(b["A"].t[:]), scalar=K_SCALE, in1=ET[d][:],
                                                 op0=ALU.mult, op1=ALU.mult).then_inc(b["A"].emptied, 1)
                    for d in range(2):
                        dve.wait_ge(s[d]["scalars"], step + 1)
                        bank[d]["A"].wait_emptied(dve, step, "kT")
                        dve.tensor_scalar(wS[d][:], wS[d][:], K_SCALE, None, ALU.mult)
                        dve.drain()
                        dve.tensor_tensor(kw[d][:], ktok[d][:], per_head(wS[d][:], P), ALU.mult
                                          ).then_inc(s[d]["kw"], 1)
                    for h in range(4):
                        for d in range(2):
                            b = bank[d]
                            fq, fp = ("B", "D") if h % 2 == 0 else ("C", "A")
                            b[fq].wait_emptied(dve, step, f"NQ{h}")
                            b[fp].wait_filled(dve, step, f"NP{h}")
                            dve.tensor_tensor(nu[d][:, h, :], nu[d][:, h, :], b[fp].t[:, 0:DA], ALU.add
                                              ).then_inc(b[fp].emptied, 1)
                    dve.drain()
                    for d in range(2):
                        dve.tensor_tensor(rden[d][:].unsqueeze(2), nu[d][:, :, DV_ML:DA], nu[d][:, :, DV_ML:DA], ALU.mult)
                        dve.tensor_scalar(mx[d][:].unsqueeze(2), nu[d][:, :, DV_ML:DA], -1.0, None, ALU.mult)
                        dve.drain()
                        dve.tensor_tensor(rden[d][:].unsqueeze(2), nu[d][:, :, DV_ML:DA], mx[d][:].unsqueeze(2), ALU.max)
                        dve.drain()
                        dve.tensor_tensor(rden[d][:], rden[d][:], enm[d][:], ALU.max)
                        dve.drain()
                        dve.reciprocal(rden[d][:], rden[d][:])
                        dve.drain()
                        for h in range(4):
                            o = col(k.o_ml[:], tiles[d], h * DV_ML, (h + 1) * DV_ML)
                            dve.scalar_tensor_tensor(out=o, in0=nu[d][:, h, 0:DV_ML], scalar=rden[d][:, h:h + 1],
                                                     in1=o, op0=ALU.mult, op1=ALU.add)
                        dve.drain()
                    for h in range(4):
                        for d in range(2):
                            f = bank[d]["BC"[h % 2]]
                            f.wait_filled(dve, step, f"S{h}")
                            dve.scalar_tensor_tensor(out=S[x][d][:, h, :], in0=S[x][d][:, h, :],
                                                     scalar=carry[d][:, h:h + 1], in1=f.t[:, 0:DA],
                                                     op0=ALU.mult, op1=ALU.add).then_inc(f.emptied, 1)
                    dve.drain()
                    if x == 0:
                        dve.sem_inc(prompt_done, 1)
                steps(dve, body)


def phase_branch_outputs(nc, k):
    with ExitStack() as mem:
        def sb(name, shape):
            return mem.enter_context(nc.sbuf_tensor(name, shape, F32))
        gate = [sb("z_gate", [P, 8, T]), sb("mo_gate", [P, 8, T])]
        sq = sb("o_squares", [P, TT, 1024])
        ms = [sb("dn_ms", [P, TT * H_DN]), sb("ml_ms", [P, TT * H_ML])]
        rs = [sb("dn_rs", [P, TT * H_DN]), sb("ml_rs", [P, TT * H_ML])]
        gate_in = [k.sem("z_in"), k.sem("mo_in")]
        gated, meaned, rooted, scaled, turned, read = (k.sem(n) for n in ("bo_gated", "bo_meaned", "bo_rooted",
                                                                         "bo_scaled", "bo_turned", "bo_read"))
        o = [k.o_dn, k.o_ml]
        heads = [H_DN, H_ML]
        with nc.Block() as block:
            @block.sync
            def _(sp):
                for b, t0 in enumerate((T_Z, T_MO)):
                    sp.dma_start(gate[b][:], k.d_proj[t0:t0 + 8].rearrange("m p t -> p m t")).then_inc(gate_in[b], 16)

            @block.scalar
            def _(act):
                for b in range(2):
                    act.wait_ge(meaned, b + 1)
                    act.activation(rs[b][:], ms[b][:], ACT.Sqrt).then_inc(rooted, 1)
                for b, f in enumerate((ACT.Silu, ACT.Sigmoid)):
                    act.wait_ge(gate_in[b], 16)
                    act.activation(gate[b][:], gate[b][:], f).then_inc(gated, 1)

            @block.vector
            def _(dve):
                for b in range(2):
                    per = 1024 // heads[b]
                    dve.tensor_tensor(sq[:], o[b][:], o[b][:], ALU.mult)
                    dve.drain()
                    dve.tensor_reduce(ms[b][:], sq[:].rearrange("p t (h n) -> p (t h) n", n=per), AX.X, ALU.add)
                    dve.drain()
                    dve.tensor_scalar(ms[b][:], ms[b][:], 1.0 / per, EPS, ALU.mult, ALU.add).then_inc(meaned, 1)
                for b in range(2):
                    per = 1024 // heads[b]
                    dve.wait_ge(rooted, b + 1)
                    dve.reciprocal(rs[b][:], rs[b][:])
                    dve.drain()
                    v = o[b][:].rearrange("p t (h n) -> p (t h) n", n=per)
                    dve.tensor_tensor(v, v, rs[b][:].unsqueeze(2).to_broadcast([P, TT * heads[b], per]), ALU.mult
                                      ).then_inc(scaled, 1)
                dve.wait_ge(gated, 2)
                n = 0
                for b in range(2):
                    y = (k.yaT, k.ybT)[b]
                    for t in range(TT):
                        for half in range(2):
                            bank = k.bank[n % 8]
                            dve.wait_ge(turned, n + 1)
                            for j in range(4):
                                c = 4 * half + j
                                gain = k.chan[:, V_DNG:V_DNG + 1] if b == 0 else k.chan[:, V_MLG + c:V_MLG + c + 1]
                                src = bank[:, j * P:(j + 1) * P]
                                if b == 1 and t > 0:
                                    w0, wn = (t - 1) * (P // ROWS), P // ROWS
                                    src = src.rearrange("p (c r) -> p c r", r=ROWS)

                                    def raster(a):
                                        return a[:, c, NP_TOK:T].rearrange("p (r c) -> p c r", r=ROWS)[:, w0:w0 + wn, :]
                                    out, g = raster(y), raster(gate[b])
                                else:
                                    out, g = y[:, c, t * P:(t + 1) * P], gate[b][:, c, t * P:(t + 1) * P]
                                op = dve.scalar_tensor_tensor(out=out, in0=src, scalar=gain, in1=g,
                                                              op0=ALU.mult, op1=ALU.mult)
                            op.then_inc(read, 1)
                            n += 1

            @block.tensor
            def _(pe):
                n = 0
                for b in range(2):
                    pe.wait_ge(scaled, b + 1)
                    for t in range(TT):
                        for half in range(2):
                            if n >= 8:
                                pe.wait_ge(read, n - 7)
                            for j in range(4):
                                c = 4 * half + j
                                mm = pe.transpose(k.bank[n % 8][:, j * P:(j + 1) * P], o[b][:, t, c * P:(c + 1) * P],
                                                  k.ident)
                            mm.then_inc(turned, 1)
                            n += 1


def phase_merge(nc, k):
    with ExitStack() as mem:
        def sb(name, shape, dt=F32):
            return mem.enter_context(nc.sbuf_tensor(name, shape, dt))
        y = k.y2T
        y_hi, y_lo = (sb(n, [P, KT, T], F32R) for n in ("y_hi", "y_lo"))
        w = sb("merge_ring", [P, 2, KT, P])
        w_hi, w_lo = ([sb(f"{n}{b}", [P, KT, P], F32R) for b in range(2)] for n in ("merge_w_hi", "merge_w_lo"))
        gt = [sb(f"merge_gates{b}", [P, 2, T]) for b in range(2)]
        gated = [sb(f"merge_gated_{j}", [P, T]) for j in "ab"]
        s = {n: k.sem(n) for n in ("w_high", "w_low", "y_high", "y_low", "merge_summed", "merge_sig", "merge_read",
                                   "merged", "out_read")}
        landed = [k.sem(f"merge_landed{u}") for u in range(2)]
        gates_in = [k.sem(f"merge_gates_in{u}") for u in range(2)]
        HALF_K = KT // 2

        def tiles(eng, first, body):
            for u in range(2):
                body(0, first, u)
            with eng.Fori(0, KT // 2 - 1) as i:
                for u in range(2):
                    body(i, first + 2, u)

        with nc.Block() as block:
            @block.sync
            def _(sp):
                for src, base in ((k.d_wup, 0), (k.d_wout, KT)):
                    with sp.Fori(0, KT // 2) as i:
                        for u in range(2):
                            sp.wait_ge(s["w_low"], i * 2 + (base + u + 1))
                            sp.dma_start(w[:, u], src[bass.ds(i * 2 + u, 1)].rearrange("a p k n -> p (a k) n")
                                         ).then_inc(landed[u], 16)

            @block.gpsimd
            def _(pool):
                with pool.Fori(0, KT // 2) as i:
                    for u in range(2):
                        pool.wait_ge(s["merge_read"], i * 2 + u + 1)
                        for j, t0 in enumerate((T_GA, T_GB)):
                            pool.dma_start(gt[u][:, j, :], k.d_proj[bass.ds(i * 2 + (u + t0), 1)].rearrange(
                                "a p t -> p (a t)")).then_inc(gates_in[u], 16)

            @block.tensor
            def _(pe):
                def products(base, u, kk, banks, start, stop):
                    for wt, ys in ((w_hi[u], (y_hi, y_lo)), (w_lo[u], (y_hi,))):
                        for yy in ys:
                            for c, (lo, hi) in enumerate(CHUNKS):
                                mm = pe.matmul(banks[c][:, 0:hi - lo], wt[:, kk, :], yy[:, kk, lo:hi],
                                               start=(start and wt is w_hi[u] and yy is y_hi),
                                               stop=(stop and wt is w_lo[u]))
                    return mm

                def merge_tile(i, base, u):
                    n = i * 2 + (base + u)
                    pe.wait_ge(s["w_low"], n + 3)
                    pe.wait_ge(s["merge_read"], n + 1)
                    for kk in range(KT):
                        j = kk // HALF_K
                        if isinstance(i, int) and base + u == 0:
                            pe.wait_ge(s["y_low"], kk + 1)
                        mm = products(base, u, kk, k.bank[4 * u + 2 * j:4 * u + 2 * j + 2],
                                      kk % HALF_K == 0, kk % HALF_K == HALF_K - 1)
                    mm.then_inc(s["merge_summed"], 1)

                def out_tile(i, base, u):
                    n = i * 2 + (base + u)
                    pe.wait_ge(s["w_low"], n + 3)
                    pe.wait_ge(s["out_read"], i * 2 + (base + u - KT + 1))
                    for kk in range(KT):
                        if isinstance(i, int) and base + u == KT:
                            pe.wait_ge(s["y_low"], KT + kk + 1)
                        mm = products(base, u, kk, k.bank[4 * u:4 * u + 2], kk == 0, kk == KT - 1)
                    mm.then_inc(s["merge_summed"], 1)
                tiles(pe, 0, merge_tile)
                tiles(pe, KT, out_tile)

            @block.scalar
            def _(act):
                act.sem_inc(s["out_read"], 2)

                def high(i, base, u):
                    if isinstance(i, int):
                        act.wait_ge(landed[u], 16 * ((base + u) // 2 + 1))
                    else:
                        act.wait_ge(landed[u], i * 16 + 16 * (base // 2 + 1))
                    act.activation(w_hi[u][:], w[:, u], ACT.Copy).then_inc(s["w_high"], 1)

                def split_y(first):
                    for kk in range(KT):
                        if first:
                            act.wait_ge(s["merged"], kk + 1)
                        act.activation(y_hi[:, kk, :], y[:, kk, :], ACT.Copy).then_inc(s["y_high"], 1)

                def merge_tile(i, base, u):
                    n = i * 2 + (base + u)
                    act.wait_ge(gates_in[u], i * 32 + 32 * (base // 2 + 1))
                    act.activation(gt[u][:], gt[u][:], ACT.Sigmoid).then_inc(s["merge_sig"], 1)
                    act.wait_ge(s["merge_summed"], n + 1)
                    high(i, base + 2, u)

                def out_tile(i, base, u, more=True):
                    n = i * 2 + (base + u)
                    act.wait_ge(s["merge_summed"], n + 1)
                    for c, (lo, hi) in enumerate(CHUNKS):
                        ev = act.activation(y[:].rearrange("p m t -> p (m t)")[
                            :, bass.ds((i * 2 + (base + u - KT)) * T + lo, hi - lo)],
                            k.bank[4 * u + c][:, 0:hi - lo], ACT.Copy)
                    ev.then_inc(s["out_read"], 1)
                    if more:
                        high(i, base + 2, u)
                high(0, 0, 0)
                high(0, 0, 1)
                split_y(0)
                tiles(act, 0, merge_tile)
                split_y(KT)
                with act.Fori(0, KT // 2 - 1) as i:
                    for u in range(2):
                        out_tile(i, KT, u)
                for u in range(2):
                    out_tile(0, 2 * KT - 2, u, more=False)

            @block.vector
            def _(dve):
                dve.sem_inc(s["w_low"], 2)
                dve.sem_inc(s["merge_read"], 2)

                def low(i, base, u):
                    dve.wait_ge(s["w_high"], i * 2 + (base + u + 1))
                    dve.tensor_tensor(w_lo[u][:], w[:, u], w_hi[u][:].bitcast(F32), ALU.subtract
                                      ).then_inc(s["w_low"], 1)

                def split_y(first):
                    for kk in range(KT):
                        dve.wait_ge(s["y_high"], first + kk + 1)
                        dve.tensor_tensor(y_lo[:, kk, :], y[:, kk, :], y_hi[:, kk, :].bitcast(F32), ALU.subtract
                                          ).then_inc(s["y_low"], 1)

                def merge_tile(i, base, u):
                    n = i * 2 + (base + u)
                    dve.wait_ge(s["merge_summed"], n + 1)
                    dve.wait_ge(s["merge_sig"], n + 1)
                    for j in range(2):
                        for c, (lo, hi) in enumerate(CHUNKS):
                            op = dve.tensor_tensor(gated[j][:, lo:hi], k.bank[4 * u + 2 * j + c][:, 0:hi - lo],
                                                   gt[u][:, j, lo:hi], ALU.mult)
                    op.then_inc(s["merge_read"], 1)
                    dve.drain()
                    dve.tensor_tensor(y[:].rearrange("p m t -> p (m t)")[:, bass.ds(n * T, T)], gated[0][:],
                                      gated[1][:], ALU.add).then_inc(s["merged"], 1)
                    dve.drain()
                    if isinstance(i, int) and base + u == KT - 1:
                        split_y(KT)
                    low(i, base + 2, u)

                low(0, 0, 0)
                low(0, 0, 1)
                split_y(0)
                with dve.Fori(0, KT // 2 - 1) as i:
                    for u in range(2):
                        merge_tile(i, 0, u)
                for u in range(2):
                    merge_tile(0, KT - 2, u)
                with dve.Fori(0, KT // 2 - 1) as i:
                    for u in range(2):
                        low(i, KT + 2, u)


def phase_residual_router(nc, k):
    with ExitStack() as mem:
        def sb(name, shape):
            return mem.enter_context(nc.sbuf_tensor(name, shape, F32))
        sq = [sb(f"rr_sq{b}", [P, T]) for b in range(4)]
        R = sb("rr_R", [P, T])
        wr = sb("w_router", [P, KT, N_EXP])
        tok = [sb(f"rr_tok{b}", [P, D]) for b in range(2)]
        mx = sb("aff_max", [P, TT])
        sm = sb("aff_sum", [P, TT])
        aff = sb("aff", [P, TT, N_EXP])
        s = {n: k.sem(n) for n in ("rr_w", "rr_sq_even", "rr_sq_odd", "rr_xT_turned", "rr_xT", "rr_sum", "rr_root", "rr_rr", "rr_x1", "rr_h2", "rr_turned",
                                   "rr_copied", "rr_logits", "rr_sub", "rr_exp", "rr_aff", "rr_affT")}
        stored = [k.sem(f"rr_stored{b}") for b in range(2)]
        x_in = [k.sem(f"rr_x_in{b}") for b in range(2)]
        src = (k.y2T, k.xT)
        order = [(what, t) for what in range(2) for t in range(TT)]
        with nc.Block() as block:
            @block.sync
            def _(sp):
                for t in range(TT):
                    if t >= 2:
                        sp.wait_ge(s["rr_xT_turned"], t - 1)
                    sp.dma_start(tok[t % 2][:], k.d_x[t * P:(t + 1) * P, :]).then_inc(x_in[t % 2], 16)
                sp.dma_start(wr[:], k.d_wrouter).then_inc(s["rr_w"], 16)
                for n, (what, t) in enumerate(order):
                    sp.wait_ge(s["rr_copied"], 4 * n + 4)
                    sp.dma_start((k.d_x1, k.d_h2)[what][t * P:(t + 1) * P, :], tok[n % 2][:]).then_inc(stored[n % 2], 16)
                for b in range(2):
                    sp.wait_ge(stored[b], 16 * TT)

            @block.gpsimd
            def _(pool):
                for r in range(2):
                    for kk in range(1, KT, 2):
                        if r == 1:
                            pool.wait_ge(s["rr_x1"], kk + 1)
                        if r * KT + kk >= 4:
                            pool.wait_ge(s["rr_sum"], r * KT + kk - 3)
                        pool.tensor_tensor(sq[kk % 4][:], src[r][:, kk, :], src[r][:, kk, :], ALU.mult
                                           ).then_inc(s["rr_sq_odd"], 1)

            @block.tensor
            def _(pe):
                for r in range(2):
                    for kk in range(KT):
                        pe.wait_ge(s["rr_sq_" + ("even", "odd")[kk % 2]], (r * KT + kk) // 2 + 1)
                        pe.matmul(k.bank[0][:], k.ones, sq[kk % 4][:, NP_TOK:T], start=(kk == 0), stop=(kk == KT - 1))
                        pe.matmul(k.bank[1][:, 0:P], k.ones, sq[kk % 4][:, 0:NP_TOK], start=(kk == 0),
                                  stop=(kk == KT - 1)).then_inc(s["rr_sum"], 1)
                    if r == 0:
                        for t in range(TT):
                            pe.wait_ge(x_in[t % 2], 16 * (t // 2 + 1))
                            if t > 0:
                                pe.wait_ge(s["rr_xT"], t)
                            for kk in range(KT):
                                mm = pe.transpose(k.bank[2 + kk // 4][:, (kk % 4) * P:(kk % 4 + 1) * P],
                                                  tok[t % 2][:, kk * P:(kk + 1) * P], k.ident)
                            mm.then_inc(s["rr_xT_turned"], 1)
                for n, (what, t) in enumerate(order):
                    if n == 0:
                        pe.wait_ge(s["rr_xT"], TT)
                    if n == TT:
                        pe.wait_ge(s["rr_h2"], 1)
                    for b in range(4):
                        i = 4 * n + b
                        if i >= 4:
                            pe.wait_ge(s["rr_copied"], i - 3)
                        for j in range(4):
                            mm = pe.transpose(k.bank[2 + b][:, j * P:(j + 1) * P],
                                              (k.xT, k.y2T)[what][:, 4 * b + j, t * P:(t + 1) * P], k.ident)
                        mm.then_inc(s["rr_turned"], 1)
                pe.wait_ge(s["rr_w"], 16)
                for t in range(TT):
                    for kk in range(KT):
                        mm = pe.matmul(k.bank[6][:, t * N_EXP:(t + 1) * N_EXP], k.y2T[:, kk, t * P:(t + 1) * P],
                                       wr[:, kk, :], start=(kk == 0), stop=(kk == KT - 1))
                mm.then_inc(s["rr_logits"], 1)
                pe.wait_ge(s["rr_aff"], 1)
                for t in range(TT):
                    mm = pe.transpose(k.bank[7][0:N_EXP, 0:P] if t == 0 else
                                      k.bank[0][0:N_EXP, (t - 1) * P:t * P], aff[:, t, :], k.ident)
                mm.then_inc(s["rr_affT"], 1)

            @block.scalar
            def _(act):
                for r in range(2):
                    for kk in range(0, KT, 2):
                        if r == 1:
                            act.wait_ge(s["rr_x1"], kk + 1)
                        if r * KT + kk >= 4:
                            act.wait_ge(s["rr_sum"], r * KT + kk - 3)
                        act.activation(sq[kk % 4][:], src[r][:, kk, :], ACT.Square).then_inc(s["rr_sq_even"], 1)
                    act.wait_ge(s["rr_sum"], (r + 1) * KT)
                    act.activation(R[:, NP_TOK:T], k.bank[0][:], ACT.Sqrt, bias=k.eps, scale=1.0 / D)
                    act.activation(R[:, 0:NP_TOK], k.bank[1][:, 0:P], ACT.Sqrt, bias=k.eps, scale=1.0 / D
                                   ).then_inc(s["rr_root"], 1)
                    if r == 0:
                        for t in range(TT):
                            act.wait_ge(s["rr_xT_turned"], t + 1)
                            for b in range(4):
                                ev = act.activation(k.xT[:, 4 * b:4 * b + 4, t * P:(t + 1) * P],
                                                    h4(k.bank[2 + b][:]), ACT.Copy)
                            ev.then_inc(s["rr_xT"], 1)
                for n, _ in enumerate(order):
                    if n >= 2:
                        act.wait_ge(stored[n % 2], 16 * (n // 2))
                    for b in range(4):
                        act.wait_ge(s["rr_turned"], 4 * n + b + 1)
                        act.activation(tok[n % 2][:, 4 * b * P:(4 * b + 4) * P], k.bank[2 + b][:], ACT.Copy
                                       ).then_inc(s["rr_copied"], 1)
                act.wait_ge(s["rr_sub"], 1)
                act.activation(aff[:], aff[:], ACT.Exp).then_inc(s["rr_exp"], 1)

            @block.vector
            def _(dve):
                for r in range(2):
                    dve.wait_ge(s["rr_root"], r + 1)
                    dve.reciprocal(R[:], R[:])
                    dve.drain()
                    for kk in range(KT):
                        dve.tensor_tensor(k.y2T[:, kk, :], src[r][:, kk, :], R[:], ALU.mult)
                    dve.drain()
                    if r == 0:
                        dve.wait_ge(s["rr_xT"], TT)
                    for kk in range(KT):
                        for c, (lo, hi) in enumerate(((0, NP_TOK), (NP_TOK, T))):
                            v = k.y2T[:, kk, lo:hi]
                            if r == 0:
                                op = dve.scalar_tensor_tensor(out=k.xT[:, kk, lo:hi], in0=v, scalar=k.g1[:, kk, c:c + 1],
                                                         in1=k.xT[:, kk, lo:hi], op0=ALU.mult, op1=ALU.add)
                            else:
                                dve.tensor_scalar(v, v, k.a2[:, kk, c:c + 1], k.modT[:, 3 * KT + kk, c:c + 1],
                                                  ALU.mult, ALU.add)
                        if r == 0:
                            op.then_inc(s["rr_x1"], 1)
                    if r == 1:
                        dve.drain().then_inc(s["rr_h2"], 1)
                    else:
                        dve.drain()
                dve.wait_ge(s["rr_logits"], 1)
                lg = k.bank[6][:, 0:TT * N_EXP].rearrange("p (t n) -> p t n", t=TT)
                dve.tensor_reduce(mx[:], lg, AX.X, ALU.max)
                dve.drain()
                dve.tensor_tensor(aff[:], lg, mx[:].unsqueeze(2).to_broadcast([P, TT, N_EXP]), ALU.subtract
                                  ).then_inc(s["rr_sub"], 1)
                dve.wait_ge(s["rr_exp"], 1)
                dve.tensor_reduce(sm[:], aff[:], AX.X, ALU.add)
                dve.drain()
                dve.reciprocal(sm[:], sm[:])
                dve.drain()
                dve.tensor_tensor(aff[:], aff[:], sm[:].unsqueeze(2).to_broadcast([P, TT, N_EXP]), ALU.mult
                                  ).then_inc(s["rr_aff"], 1)
                dve.wait_ge(s["rr_affT"], 1)
                dve.tensor_copy(k.affT[:, 0:P], k.bank[7][0:N_EXP, 0:P])
                dve.tensor_copy(k.affT[:, P:T], k.bank[0][0:N_EXP, :])


def phase_choice(nc, k):
    with ExitStack() as mem:
        val = mem.enter_context(nc.sbuf_tensor("top_val", [N_EXP, CAP], F32))
        ind = mem.enter_context(nc.sbuf_tensor("top_ind", [N_EXP, CAP], U32))
        indf = mem.enter_context(nc.sbuf_tensor("top_indf", [N_EXP, CAP], F32))
        zero = mem.enter_context(nc.sbuf_tensor("zero_rows", [P, D], F32))
        chosen, turned, zeroed, y_zeroed = (k.sem(n) for n in ("chosen", "choice_turned", "zero_made", "y_zeroed"))
        g2_out = k.sem("g2_out")
        with nc.Block() as block:
            @block.sync
            def _(sp):
                sp.wait_ge(zeroed, 1)
                for t in range(TT):
                    sp.dma_start(k.d_y[t * P:(t + 1) * P, :], zero[:]).then_inc(y_zeroed, 16)
                with nc.allow_non_contiguous_dma(reason="4096 gate values, once"):
                    for c in range(2):
                        sp.dma_start(k.d_g2[c:c + 1].rearrange("a (k p) -> p (a k)", p=P), k.g2[:, :, c]
                                     ).then_inc(g2_out, 16)
                sp.wait_ge(y_zeroed, 16 * TT)
                sp.wait_ge(g2_out, 32)

            @block.gpsimd
            def _(pool):
                pool.memset(zero[:], 0.0)
                pool.drain().then_inc(zeroed, 1)

            @block.vector
            def _(dve):
                for lo, hi, s0, cap in ((0, NP_TOK, 0, CAP_P), (NP_TOK, T, CAP_P, CAP_S)):
                    v = k.affT[:, lo:hi]
                    for r in range(cap // 8):
                        a, b = s0 + 8 * r, s0 + 8 * r + 8
                        dve.max(val[:, a:b], v)
                        dve.drain()
                        dve.max_index(ind[:, a:b], val[:, a:b], v)
                        dve.drain()
                        dve.match_replace(v, val[:, a:b], v, MASKED_ROW)
                        dve.drain()
                dve.tensor_copy(indf[:], ind[:])
                dve.drain()
                dve.tensor_scalar(indf[:, CAP_P:CAP], indf[:, CAP_P:CAP], float(NP_TOK), None, ALU.add)
                dve.drain().then_inc(chosen, 1)
                dve.wait_ge(turned, 1)
                dve.tensor_copy(k.gateT[:], k.bank[0][0:CAP, 0:N_EXP])
                dve.tensor_copy(k.idx[:], k.bank[0][0:CAP, N_EXP:2 * N_EXP])

            @block.tensor
            def _(pe):
                pe.wait_ge(chosen, 1)
                pe.transpose(k.bank[0][0:CAP, 0:N_EXP], val[:], k.ident[0:N_EXP, 0:N_EXP])
                pe.transpose(k.bank[0][0:CAP, N_EXP:2 * N_EXP], indf[:], k.ident[0:N_EXP, 0:N_EXP]
                             ).then_inc(turned, 1)


def phase_experts(nc, k):
    NW = 24
    NSLOT = 12
    FT = F_EXP // P
    DC = 256
    with ExitStack() as mem:
        def sb(name, shape):
            return mem.enter_context(nc.sbuf_tensor(name, shape, F32))
        w = sb("expert_ring", [P, NSLOT, KT, P])
        xe = [sb(f"xe{b}", [CAP, D]) for b in range(2)]
        xT = sb("xeT", [P, KT, CAP])
        sg = sb("silu_gate", [P, 2, CAP])
        hT = sb("hiddenT", [P, FT, CAP])
        ye = [sb(f"ye{b}", [CAP, D]) for b in range(2)]
        s = {n: k.sem(n) for n in ("xe_landed0", "xe_landed1", "xe_turned", "xeT_copied", "w_used", "silu_done",
                                   "hidden", "ye_done", "scattered", "rows_free")}
        landed = [k.sem(f"we_landed{j}") for j in range(NSLOT)]
        with nc.Block() as block:
            @block.sync
            def _(sp):
                with sp.Fori(0, N_EXP) as e:
                    for j in range(NW):
                        sp.wait_ge(s["w_used"], e * NW + (j + 1))
                        if j < 16:
                            src = (k.d_wgate, k.d_wup_e)[j % 2][bass.ds(e * FT + j // 2, 1)]
                            sp.dma_start(w[:, j % NSLOT], src.rearrange("a p k n -> p (a k) n")
                                         ).then_inc(landed[j % NSLOT], 16)
                        else:
                            src = k.d_wdown[bass.ds(e * 8 + (j - 16), 1)]
                            sp.dma_start(w[:, j % NSLOT].rearrange("p k n -> p (k n)"),
                                         src.rearrange("a p k n -> p (a k n)")).then_inc(landed[j % NSLOT], 16)

            @block.gpsimd
            def _(pool):
                def gather(e_col, b):
                    pool.indirect_dma_start(xe[b][:], None, k.d_h2[:, :],
                                            bass.IndirectOffsetOnAxis(ap=k.idx[:, e_col:e_col + 1], axis=0)
                                            ).then_inc(s[f"xe_landed{b}"], 16)

                pool.sem_inc(s["rows_free"], 2)
                for e in range(2):
                    gather(e, e)
                for e in range(N_EXP):
                    pool.wait_ge(s["ye_done"], 4 * e + 4 + 2)
                    if e > 0:
                        pool.wait_ge(s["scattered"], 16 * e)
                        pool.sem_inc(s["rows_free"], 1)
                    pool.indirect_dma_start(k.d_y[:, :], bass.IndirectOffsetOnAxis(ap=k.idx[:, e:e + 1], axis=0),
                                            ye[e % 2][:], None, compute_op=ALU.add).then_inc(s["scattered"], 16)
                    if e + 2 < N_EXP:
                        pool.wait_ge(s["xe_turned"], 4 * e + 4)
                        gather(e + 2, e % 2)
                pool.wait_ge(s["scattered"], 16 * N_EXP)

            def experts(eng, body):
                with eng.Fori(0, N_EXP // 2) as i:
                    for b in range(2):
                        body(i, b)

            @block.tensor
            def _(pe):
                pe.sem_inc(s["w_used"], NSLOT)

                def body(i, b):
                    def arrived(j):
                        pe.wait_ge(landed[j % NSLOT], i * 64 + (32 * b + 16 * (j // NSLOT) + 16))
                    pe.wait_ge(s[f"xe_landed{b}"], i * 16 + 16)
                    for r in range(4):
                        pe.wait_ge(s["xeT_copied"], i * 8 + (4 * b + r + 1))
                        for j in range(4):
                            kk = 4 * r + j
                            mm = pe.transpose(k.bank[r % 2][:, j * P:j * P + CAP], xe[b][:, kk * P:(kk + 1) * P],
                                              k.ident[0:CAP, 0:CAP])
                        mm.then_inc(s["xe_turned"], 1)
                    pe.wait_ge(s["xeT_copied"], i * 8 + (4 * b + 4 + 2))
                    for f in range(FT):
                        pe.wait_ge(s["hidden"], i * 16 + (8 * b + f + 1))
                        for g in range(2):
                            j = 2 * f + g
                            arrived(j)
                            for kk in range(KT):
                                mm = pe.matmul(k.bank[2 + 2 * (f % 2) + g][:, 0:CAP], w[:, j % NSLOT, kk, :],
                                               xT[:, kk, :], start=(kk == 0), stop=(kk == KT - 1))
                            mm.then_inc(s["w_used"], 1)
                    pe.wait_ge(s["hidden"], i * 16 + (8 * b + 8 + 2))
                    for c in range(8):
                        j = 16 + c
                        arrived(j)
                        wd = w[:, j % NSLOT].rearrange("p k n -> p (k n)").rearrange("p (k n) -> p k n", n=DC)
                        if c % 2 == 0:
                            pe.wait_ge(s["ye_done"], i * 8 + (4 * b + c // 2 + 1))
                        for kk in range(FT):
                            mm = pe.matmul(k.bank[6 + c // 2 % 2][0:CAP, (c % 2) * DC:(c % 2 + 1) * DC],
                                           hT[:, kk, :], wd[:, kk, :], start=(kk == 0), stop=(kk == FT - 1))
                        mm.then_inc(s["w_used"], 1)
                experts(pe, body)

            @block.scalar
            def _(act):
                act.sem_inc(s["xeT_copied"], 2)

                def body(i, b):
                    for r in range(4):
                        act.wait_ge(s["xe_turned"], i * 8 + (4 * b + r + 1))
                        act.activation(xT[:, 4 * r:4 * r + 4, :], h4(k.bank[r % 2][:])[:, :, 0:CAP], ACT.Copy
                                       ).then_inc(s["xeT_copied"], 1)
                    for f in range(FT):
                        act.wait_ge(s["w_used"], i * 48 + (24 * b + NSLOT + 2 * f + 1))
                        act.wait_ge(s["hidden"], i * 16 + (8 * b + f + 1))
                        act.activation(sg[:, f % 2, :], k.bank[2 + 2 * (f % 2)][:, 0:CAP], ACT.Silu
                                       ).then_inc(s["silu_done"], 1)
                experts(act, body)

            @block.vector
            def _(dve):
                dve.sem_inc(s["hidden"], 2)
                dve.sem_inc(s["ye_done"], 2)

                def body(i, b):
                    for f in range(FT):
                        dve.wait_ge(s["silu_done"], i * 16 + (8 * b + f + 1))
                        dve.wait_ge(s["w_used"], i * 48 + (24 * b + NSLOT + 2 * f + 2))
                        dve.tensor_tensor(hT[:, f, :], k.bank[3 + 2 * (f % 2)][:, 0:CAP], sg[:, f % 2, :], ALU.mult
                                          ).then_inc(s["hidden"], 1)
                    dve.wait_ge(s["rows_free"], i * 2 + (b + 1))
                    for c in range(4):
                        dve.wait_ge(s["w_used"], i * 48 + (24 * b + NSLOT + 16 + 2 * c + 2))
                        dve.tensor_scalar(ye[b][:, c * 512:(c + 1) * 512], k.bank[6 + c % 2][0:CAP, :],
                                          k.gateT[:, bass.ds(i * 2 + b, 1)], None, ALU.mult
                                          ).then_inc(s["ye_done"], 1)
                experts(dve, body)


def phase_final(nc, k):
    with ExitStack() as mem:
        def sb(name, shape):
            return mem.enter_context(nc.sbuf_tensor(name, shape, F32))
        row = [sb(f"g2_row{c}", [P, D]) for c in range(2)]
        y = [sb(f"y_in{b}", [P, D]) for b in range(2)]
        x1 = [sb(f"x1_in{b}", [P, D]) for b in range(2)]
        sq = sb("y_sq", [P, D])
        ms = [sb(f"y_ms{b}", [P, 1]) for b in range(2)]
        rs = [sb(f"y_rs{b}", [P, 1]) for b in range(2)]
        rows_in, summed, rooted, done = (k.sem(n) for n in ("g2_rows_in", "y_summed", "y_rooted", "y_done"))
        landed = [k.sem(f"y_landed{b}") for b in range(2)]
        stored = [k.sem(f"out_stored{b}") for b in range(2)]
        with nc.Block() as block:
            @block.sync
            def _(sp):
                for t in range(TT):
                    b = t % 2
                    if t >= 2:
                        sp.wait_ge(done, t - 1)
                        sp.wait_ge(stored[b], 16 * (t // 2))
                    sp.dma_start(y[b][:], k.d_y[t * P:(t + 1) * P, :]).then_inc(landed[b], 16)
                    sp.dma_start(x1[b][:], k.d_x1[t * P:(t + 1) * P, :]).then_inc(landed[b], 16)
                    if t < 2:
                        sp.dma_start(row[t][:], k.d_g2[t:t + 1, :].to_broadcast([P, D])).then_inc(rows_in, 16)

            @block.gpsimd
            def _(pool):
                for t in range(TT):
                    pool.wait_ge(done, t + 1)
                    dst = k.o_yp[:, :] if t == 0 else k.o_ys[(t - 1) * P:t * P, :]
                    pool.dma_start(dst, x1[t % 2][:]).then_inc(stored[t % 2], 16)
                pool.wait_ge(stored[0], 48)
                pool.wait_ge(stored[1], 32)

            @block.scalar
            def _(act):
                for t in range(TT):
                    b = t % 2
                    act.wait_ge(landed[b], 32 * (t // 2 + 1))
                    if t >= 2:
                        act.wait_ge(rooted, t - 1)
                    act.activation(sq[:], y[b][:], ACT.Square, accum_out=ms[b][:])
                    act.drain()
                    if t >= 2:
                        act.wait_ge(done, t - 1)
                    act.activation(rs[b][:], ms[b][:], ACT.Sqrt, bias=k.eps, scale=1.0 / D).then_inc(rooted, 1)

            @block.vector
            def _(dve):
                dve.wait_ge(rows_in, 32)
                for t in range(TT):
                    b = t % 2
                    dve.wait_ge(rooted, t + 1)
                    dve.reciprocal(rs[b][:], rs[b][:])
                    dve.drain()
                    dve.scalar_tensor_tensor(out=y[b][:], in0=y[b][:], scalar=rs[b][:, 0:1], in1=row[min(t, 1)][:],
                                             op0=ALU.mult, op1=ALU.mult)
                    dve.drain()
                    dve.tensor_tensor(x1[b][:], x1[b][:], y[b][:], ALU.add).then_inc(done, 1)


def build(nc, ins, outs):
    with ExitStack() as ctx:
        taken = []

        def take(name):
            taken.append(nc.alloc_semaphore(name=name))
            return taken[-1]

        def give_back():
            nc.clear_and_free_semaphores(taken)
            taken.clear()
            nc.all_engine_barrier()

        def sb(stack, name, shape, dt=F32):
            return stack.enter_context(nc.sbuf_tensor(name, shape, dt))

        scratch = {name: nc.dram_tensor(name, shape, F32).ap() for name, shape in (
            ("d_proj", [N_TILES, P, T]), ("d_x1", [T, D]), ("d_h2", [T, D]), ("d_y", [T, D]), ("d_g2", [2, D]))}
        k = Chip(take, ins, outs, scratch)
        k.bank = [ctx.enter_context(nc.psum_tensor(f"bank{b}", [P, 512], F32)) for b in range(8)]
        k.const = sb(ctx, "const", [P, N_CONST])
        k.chan = sb(ctx, "chan", [P, N_CHAN])
        k.rowp = sb(ctx, "rowp", [P, N_ROWP])
        k.modT = sb(ctx, "modT", [P, N_MOD_TILES, 2])
        k.a1, k.a2, k.g1, k.g2 = (sb(ctx, n, [P, KT, 2]) for n in ("a1", "a2", "g1", "g2"))
        k.affT = sb(ctx, "affT", [N_EXP, T])
        k.gateT = sb(ctx, "gateT", [CAP, N_EXP])
        k.idx = sb(ctx, "idx", [CAP, N_EXP], U32)
        k.ident = k.const[:, C_ID:C_ID + P]
        k.tri = [k.const[:, C_TRI + d * P:C_TRI + (d + 1) * P] for d in range(2)]
        k.neg = [k.const[:, C_NEG + d * P:C_NEG + (d + 1) * P] for d in range(2)]
        k.ones = k.const[:, C_ONES:C_ONES + P]
        k.level1 = lambda d: k.const[:, C_LEV + d * P:C_LEV + (d + 1) * P]
        k.level = lambda d, n: k.const[:, C_CMP + (2 * n + d) * (P // 2):C_CMP + (2 * n + d + 1) * (P // 2)]
        k.eps = k.chan[:, V_L2B + 8:V_L2B + 9]

        back = ExitStack()
        with ExitStack() as front:
            k.gates = sb(front, "gates", [P, TT, 48])
            with ExitStack() as split:
                with ExitStack() as inner:
                    k.hT = sb(inner, "hT", [P, KT, T])
                    phase_modulation(nc, k)
                    k.h_hi, k.h_lo = (split.enter_context(nc.sbuf_tensor(n, [P, KT, T], F32R, side="right"))
                                      for n in ("h_hi", "h_lo"))
                    phase_first_norm(nc, k)
                phase_projection(nc, k)
            k.o_dn, k.o_ml = (sb(front, n, [P, TT, 1024]) for n in ("o_dn", "o_ml"))
            k.beta, k.G, k.nG, k.eG, k.neg_eG, k.wS, k.bw, k.g_tot, k.eT = (
                sb(front, n, [P, TT, 16]) for n in ("beta", "G", "nG", "eG", "neg_eG", "wS", "bw", "g_tot", "eT"))
            k.ci, k.b_ml, k.b_tot = (sb(front, n, [P, TT, 8]) for n in ("ci", "b_ml", "b_tot"))
            phase_gates(nc, k)
            phase_deltanet(nc, k)
            phase_mlstm(nc, k)
            give_back()
            k.y2T = back.enter_context(nc.sbuf_tensor("y_parts", [P, KT, T], F32, side="right"))
            k.yaT, k.ybT = k.y2T[:, 0:8, :], k.y2T[:, 8:16, :]
            phase_branch_outputs(nc, k)
        with back:
            phase_merge(nc, k)
            k.xT = sb(back, "xT", [P, KT, T])
            phase_residual_router(nc, k)
        phase_choice(nc, k)
        phase_experts(nc, k)
        phase_final(nc, k)


def constants():
    c = np.zeros((P, N_CONST), np.float32)
    j, i = np.meshgrid(np.arange(P), np.arange(P), indexing="ij")
    c[:, C_ID:C_ID + P] = j == i
    for d, ok in enumerate((j <= i, j >= i)):
        c[:, C_TRI + d * P:C_TRI + (d + 1) * P] = ok
        c[:, C_NEG + d * P:C_NEG + (d + 1) * P] = np.where(ok, 0.0, NEG)
    c[:, C_ONES:C_ONES + P] = 1.0
    for n, s in enumerate(LEVELS):
        same = j // (2 * s) == i // (2 * s)
        low, high = (j // s) % 2, (i // s) % 2
        for d in range(2):
            mask = same & (low == d) & (high == 1 - d)
            if s == 1:
                c[:, C_LEV + d * P:C_LEV + (d + 1) * P] = mask
            a = C_CMP + (2 * n + d) * (P // 2)
            c[:, a:a + P // 2] = mask.T[:, (np.arange(P) // s) % 2 == d]
    return c


def tiles_of(w, width=P):
    kk, n = w.shape
    return np.ascontiguousarray(w.reshape(kk // P, P, n // width, width).transpose(2, 1, 0, 3))


def channels(v):
    return v.reshape(-1, P).T


def lay_out(x):
    f = np.float32
    w_in, b_in = x["w_in"][0], x["b_in"][0]
    cuts = np.cumsum([0, 1024, 1024, 1024, 1024, 16, 16, 512, 512, 1024, 1024, 8, 8, 2048, 2048])
    names = ("dq", "dk", "dv", "dz", "db", "da", "mq", "mk", "mv", "mo", "mi", "mf", "ga", "gb")
    part = {n: slice(cuts[i], cuts[i + 1]) for i, n in enumerate(names)}
    order = ("dq", "dk", "dv", "mq", "mk", "mv", "dz", "mo", "ga", "gb")
    gates = ("db", "da", "mi", "mf")
    w_gates = np.concatenate([w_in[:, part[n]] for n in gates] + [np.zeros((D, P - 48), f)], 1)
    w_tiles = np.concatenate([tiles_of(w_in[:, part[n]]) for n in order] + [tiles_of(w_gates)])
    chan = np.zeros((P, N_CHAN), f)
    cond = np.stack([x["c_ctx"], x["c"][0]], 1)
    chan[:, V_COND:V_BMOD] = cond.reshape(KT, P, 2).transpose(1, 0, 2).reshape(P, 2 * KT)
    chan[:, V_BMOD:V_PRE1] = channels(x["b_mod"][0])
    for at, n in ((V_PRE1, "pre1_gain"), (V_POST1, "post1_gain"), (V_PRE2, "pre2_gain"), (V_POST2, "post2_gain")):
        chan[:, at:at + KT] = channels(x[n][0])
    chan[:, V_BIN:V_CONV - 1] = np.concatenate([channels(b_in[part[n]]) for n in order], 1)
    chan[0:48, V_CONV - 1] = np.concatenate([b_in[part[n]] for n in gates])
    chan[:, V_CONV:V_L2S] = x["dn_conv_w"][0].reshape(5, 24, P).transpose(2, 1, 0).reshape(P, 120)
    chan[:, V_L2S:V_L2S + 8], chan[:, V_L2S + 8:V_L2S + 16] = float(P), 1.0
    chan[:, V_L2B:V_L2B + 8], chan[:, V_L2B + 8:V_L2B + 16] = P * EPS, EPS
    chan[:, V_DNG] = x["dn_onorm"][0]
    chan[:, V_MLG:V_MLG + 8] = channels(x["ml_onorm"][0].reshape(-1))
    row = np.concatenate([x["dn_dt_bias"].reshape(-1), x["ml_f_bias"].reshape(-1), x["ml_i_bias"].reshape(-1),
                          x["dn_a_log"].reshape(-1), x["state_ml_m"].reshape(-1)])
    return {
        "d_const": constants(), "d_chan": chan, "d_rowp": np.ascontiguousarray(np.broadcast_to(row, (P, N_ROWP))),
        "d_x": np.concatenate([x["x_prompt"][0], x["x_sample"][0]]),
        "d_wmod": tiles_of(x["w_mod"][0]), "d_win": w_tiles,
        "d_sdn": x["state_dn"][0, 0], "d_smc": x["state_ml_c"][0, 0], "d_smn": x["state_ml_n"][0, 0],
        "d_wup": np.concatenate([tiles_of(x["w_up_a"][0]), tiles_of(x["w_up_b"][0])], 2),
        "d_wout": tiles_of(x["w_out"][0]),
        "d_wrouter": np.ascontiguousarray(x["w_router"][0].reshape(KT, P, N_EXP).transpose(1, 0, 2)),
        "d_wgate": np.concatenate([tiles_of(w) for w in x["w_gate"][0]]),
        "d_wup_e": np.concatenate([tiles_of(w) for w in x["w_up"][0]]),
        "d_wdown": np.concatenate([tiles_of(w, 256) for w in x["w_down"][0]]),
    }


_OUTS = [("o_yp", (NP_TOK, D)), ("o_ys", (NS_TOK, D)), ("o_sdn", (2, H_DN, P, P)), ("o_smc", (2, H_ML, P, DV_ML)),
         ("o_smn", (2, H_ML, P)), ("o_smm", (2, H_ML))]


def kernel(**inputs):
    import concourse.bacc as bacc
    from concourse.bass_utils import run_bass_kernel_spmd

    arrays = lay_out({n: np.asarray(a) for n, a in inputs.items()})
    nc = bacc.Bacc("TRN2", target_bir_lowering=False, num_devices=1)
    ins = {n: nc.dram_tensor(n, a.shape, F32, kind="ExternalInput").ap() for n, a in arrays.items()}
    outs = {n: nc.dram_tensor(n, shape, F32, kind="ExternalOutput").ap() for n, shape in _OUTS}
    build(nc, ins, outs)
    r = run_bass_kernel_spmd(nc, [arrays], core_ids=[0]).results[0]
    return (r["o_yp"][None], r["o_ys"][None], r["o_sdn"][None, None], r["o_smc"][None, None],
            r["o_smn"][None, None], r["o_smm"][None, None])
```

```python
from contextlib import ExitStack

import numpy as np

import concourse.bass as bass
from concourse import mybir

ALU = mybir.AluOpType
ACT = mybir.ActivationFunctionType
F32 = mybir.dt.float32
F32R = mybir.dt.float32r
BF16 = mybir.dt.bfloat16
U32 = mybir.dt.uint32
AX = mybir.AxisListType

P = 128
D = 2048
KT = D // P
NP_TOK, NS_TOK = 128, 512
T = NP_TOK + NS_TOK
TT = T // P
GRID_W = 64
ROWS = NS_TOK // GRID_W
H_DN, H_ML, DV_ML = 8, 4, 256
N_EXP, F_EXP = 16, 1024
EXP_SLOTS, EXP_AHEAD = 8, 4
CAP_P, CAP_S = 2 * NP_TOK // N_EXP, 2 * NS_TOK // N_EXP
CAP = CAP_P + CAP_S
EPS = 1e-6
K_SCALE = float(P) ** -0.5
NEG = -1e30
LEVELS = [1, 2, 4, 8, 16, 32, 64]

QK_TILES, V_TILES, PERM_TILES, RASTER_TILES = 16, 8, 16, 48
T_MLQ, T_Z, T_MO, T_GA, T_GB = 24, 40, 48, 56, 72
N_TILES = 88
GATE_TILE = N_TILES
CHUNKS = ((0, T // 2), (T // 2, T))
N_MOD_TILES = 6 * KT

C_ID, C_TRI, C_NEG, C_ONES, C_LEV = 0, 128, 384, 640, 768
C_CMP = C_LEV + 2 * P
N_CONST = C_CMP + 2 * len(LEVELS) * (P // 2)

V_COND = 0
V_BMOD = V_COND + 2 * KT
V_PRE1 = V_BMOD + N_MOD_TILES
V_POST1 = V_PRE1 + KT
V_PRE2 = V_POST1 + KT
V_POST2 = V_PRE2 + KT
V_BIN = V_POST2 + KT
V_CONV = V_BIN + N_TILES + 1
V_L2S = V_CONV + 24 * 5
V_L2B = V_L2S + 16
V_DNG = V_L2B + 16
V_MLG = V_DNG + 1
N_CHAN = V_MLG + 8

R_DT, R_FB, R_IB, R_AL, R_M0 = 0, 16, 24, 32, 48
N_ROWP = 56

MASKED_ROW = -1.0


def wait(eng, sem, value):
    if not (isinstance(value, int) and value == 0):
        eng.wait_ge(sem, value)


class Bank:

    def __init__(self, tensor, filled, emptied, fills):
        self.t, self.filled, self.emptied = tensor, filled, emptied
        self.order = {f: n for n, f in enumerate(fills)}
        self.per_step = len(fills)

    def wait_free(self, eng, step, fill):
        wait(eng, self.emptied, step * self.per_step + self.order[fill])

    def wait_filled(self, eng, step, fill):
        wait(eng, self.filled, step * self.per_step + self.order[fill] + 1)

    def wait_emptied(self, eng, step, fill):
        wait(eng, self.emptied, step * self.per_step + self.order[fill] + 1)


class Chip:

    def __init__(self, sem, ins, outs, scratch):
        self.sem = sem
        (self.d_const, self.d_chan, self.d_rowp, self.d_x, self.d_wmod, self.d_win, self.d_sdn,
         self.d_smc, self.d_smn, self.d_wup, self.d_wout, self.d_wrouter, self.d_wgate, self.d_wup_e,
         self.d_wdown) = (ins[n] for n in (
             "d_const", "d_chan", "d_rowp", "d_x", "d_wmod", "d_win", "d_sdn", "d_smc", "d_smn",
             "d_wup", "d_wout", "d_wrouter", "d_wgate", "d_wup_e", "d_wdown"))
        self.o_yp, self.o_ys, self.o_sdn, self.o_smc, self.o_smn, self.o_smm = (
            outs[n] for n in ("o_yp", "o_ys", "o_sdn", "o_smc", "o_smn", "o_smm"))
        self.d_proj, self.d_x1, self.d_h2, self.d_y, self.d_g2 = (
            scratch[n] for n in ("d_proj", "d_x1", "d_h2", "d_y", "d_g2"))


def h4(ap):
    return ap.rearrange("p (h n) -> p h n", h=4)


def per_head(ap, n):
    return ap.unsqueeze(2).to_broadcast([P, ap.shape[1], n])


def all_heads(ap, heads=4):
    return ap.unsqueeze(1).to_broadcast([P, heads, ap.shape[1]])


def add_mask(pe, k, bank, d):
    pe.matmul(h4(bank[:]), k.ident_bf[:], all_heads(k.neg_bf[:, d, :]), start=True, stop=False)


def col(ap3, t, a, b):
    n = ap3.shape[2]
    return ap3.rearrange("p t n -> p (t n)")[:, bass.ds(t * n + a, b - a)]


def phase_modulation(nc, k):
    with ExitStack() as mem:
        def sb(name, shape):
            return mem.enter_context(nc.sbuf_tensor(name, shape, F32))
        w = [sb(f"wmod_ring{b}", [P, 4, KT, P]) for b in range(2)]
        mod_rows = [mem.enter_context(nc.sbuf_tensor(f"mod_rows{b}", [2, 512], F32)) for b in range(2)]
        xin = sb("x_in", [P, D])
        xsq = sb("x_sq", [P, D])
        ssq = sb("x_ssq", [P, 1])
        root = sb("x_root", [P, 1])
        rstd = sb("x_rstd", [P, 1])
        xn = sb("x_normed", [P, D])
        cond = k.cond
        s = {n: k.sem(n) for n in ("params_in", "x_landed", "x_squared", "x_meaned", "x_rooted", "x_normed",
                                   "x_turned", "hT_written", "cond_ready", "mod_summed", "mod_copied",
                                   "mod_turned", "mod_stored")}
        landed = [k.sem(f"wmod_landed{b}") for b in range(2)]
        PAIRS = (N_MOD_TILES - KT) // 8

        def interleaved(eng, mod_pair, x_before=None, x_after=None):
            with eng.Fori(0, TT) as i:
                if x_before:
                    x_before(i)
                mod_pair(i, 0)
                if x_after:
                    x_after(i)
            with eng.Fori(0, PAIRS - TT) as i:
                mod_pair(i, 2 * TT)

        with nc.Block() as block:
            @block.sync
            def _(sp):
                sp.dma_start(k.chan[:], k.d_chan).then_inc(s["params_in"], 16)
                sp.dma_start(k.const[:], k.d_const).then_inc(s["params_in"], 16)
                sp.dma_start(k.rowp[:], k.d_rowp).then_inc(s["params_in"], 16)
                with sp.Fori(0, PAIRS) as i:
                    for b in range(2):
                        sp.wait_ge(s["mod_summed"], i * 2 + b + 1)
                        for u in range(4):
                            sp.dma_start(w[b][:, u], k.d_wmod[bass.ds(i * 8 + (4 * b + u), 1)].rearrange(
                                "a p k n -> p (a k) n")).then_inc(landed[b], 16)

            @block.gpsimd
            def _(pool):
                with pool.Fori(0, TT) as t:
                    pool.wait_ge(s["x_normed"], t + 1)
                    pool.dma_start(xin[:], k.d_x[bass.ds(t * P, P), :]).then_inc(s["x_landed"], 16)

            @block.tensor
            def _(pe):
                pe.sem_inc(s["mod_summed"], 2)
                pe.sem_inc(s["mod_turned"], 2)
                pe.wait_ge(s["params_in"], 48)
                pe.wait_ge(s["cond_ready"], 1)

                def multiply(i, g):
                    for b in range(2):
                        pe.wait_ge(landed[b], i * 64 + (32 * g + 64))
                        pe.wait_ge(s["mod_copied"], i * 2 + (g + b + 1))
                        for kk in range(KT):
                            mm = pe.matmul(k.bank[4 + b][0:2, :].rearrange("p (u n) -> p u n", u=4), cond[:, kk, :],
                                           w[b][:, :, kk, :], start=(kk == 0), stop=(kk == KT - 1))
                        mm.then_inc(s["mod_summed"], 1)
                    for b in range(2):
                        pe.wait_ge(s["mod_copied"], i * 2 + (g + b + 3))
                        pe.wait_ge(s["mod_stored"], i * 2 + (g + b + 1))
                        for u in range(4):
                            mm = pe.matmul(k.bank[6 + b][:, 2 * u:2 * u + 2], mod_rows[b][:, u * P:(u + 1) * P],
                                           k.ident[0:2, 0:2], start=True, stop=True)
                        mm.then_inc(s["mod_turned"], 1)

                def turn_x(t):
                    pe.wait_ge(s["x_normed"], t + 2)
                    pe.wait_ge(s["hT_written"], t + 1)
                    for kk in range(KT):
                        mm = pe.transpose(k.bank[kk // 4][:, (kk % 4) * P:(kk % 4 + 1) * P],
                                          xn[:, kk * P:(kk + 1) * P], k.ident)
                    mm.then_inc(s["x_turned"], 1)
                interleaved(pe, multiply, x_after=turn_x)

            @block.scalar
            def _(act):
                act.wait_ge(s["params_in"], 48)
                act.activation(cond[:].rearrange("p k c -> p (k c)"), k.chan[:, V_COND:V_COND + 2 * KT],
                               ACT.Silu).then_inc(s["cond_ready"], 1)
                act.sem_inc(s["hT_written"], 1)
                act.sem_inc(s["mod_copied"], 2)

                def copy_rows(i, g):
                    for b in range(2):
                        act.wait_ge(s["mod_summed"], i * 2 + (g + b + 3))
                        act.wait_ge(s["mod_turned"], i * 2 + (g + b + 1))
                        act.activation(mod_rows[b][:], k.bank[4 + b][0:2, :], ACT.Copy
                                       ).then_inc(s["mod_copied"], 1)

                def square_x(t):
                    act.wait_ge(s["x_landed"], t * 16 + 16)
                    act.activation(xsq[:], xin[:], ACT.Square, accum_out=ssq[:]).then_inc(s["x_squared"], 1)
                    act.wait_ge(s["x_meaned"], t + 1)
                    act.activation(root[:], ssq[:], ACT.Sqrt).then_inc(s["x_rooted"], 1)

                def keep_turned_x(t):
                    act.wait_ge(s["x_turned"], t + 1)
                    for b in range(4):
                        ev = act.activation(k.hT[:, 4 * b:4 * b + 4, bass.ds(t * P, P)],
                                            h4(k.bank[b][:]), ACT.Copy)
                    ev.then_inc(s["hT_written"], 1)
                interleaved(act, copy_rows, square_x, keep_turned_x)

            @block.vector
            def _(dve):
                dve.sem_inc(s["x_normed"], 1)
                dve.sem_inc(s["mod_stored"], 2)
                dve.wait_ge(s["params_in"], 48)

                def add_bias(i, g):
                    for b in range(2):
                        dve.wait_ge(s["mod_turned"], i * 2 + (g + b + 3))
                        bmod = k.chan[:, bass.ds(i * 8 + (4 * g + 4 * b + V_BMOD), 4)]
                        dve.tensor_tensor(k.modT[:].rearrange("p m c -> p (m c)")[
                            :, bass.ds(i * 16 + 8 * (g + b), 8)].rearrange("p (m c) -> p m c", c=2),
                                          k.bank[6 + b][:, 0:8].rearrange("p (m c) -> p m c", c=2),
                                          bmod.unsqueeze(2).to_broadcast([P, 4, 2]), ALU.add
                                          ).then_inc(s["mod_stored"], 1)

                def normalize_x(t):
                    dve.wait_ge(s["x_squared"], t + 1)
                    dve.tensor_scalar(ssq[:], ssq[:], 1.0 / D, EPS, ALU.mult, ALU.add).then_inc(s["x_meaned"], 1)
                    dve.wait_ge(s["x_rooted"], t + 1)
                    dve.reciprocal(rstd[:], root[:])
                    dve.drain()
                    dve.wait_ge(s["hT_written"], t + 1)
                    dve.tensor_scalar(xn[:], xin[:], rstd[:, 0:1], None, ALU.mult).then_inc(s["x_normed"], 1)
                interleaved(dve, add_bias, x_before=normalize_x)
                dve.drain()
                with_gain(dve, k, k.a1, V_PRE1, 1, 1.0)
                with_gain(dve, k, k.a2, V_PRE2, 4, 1.0)
                with_gain(dve, k, k.g1, V_POST1, 2, 0.0)


def with_gain(dve, k, out, gain, part, plus):
    for c in range(2):
        dve.scalar_tensor_tensor(out=out[:, :, c], in0=k.modT[:, part * KT:(part + 1) * KT, c], scalar=plus,
                                 in1=k.chan[:, gain:gain + KT], op0=ALU.add, op1=ALU.mult)


def phase_first_norm(nc, k):
    shifted, high = k.sem("h_shifted"), k.sem("h_high")
    with nc.Block() as block:
        @block.scalar
        def _(act):
            for kk in range(KT):
                act.wait_ge(shifted, kk + 1)
                act.activation(k.h_hi[:, kk, :], k.hT[:, kk, :], ACT.Copy).then_inc(high, 1)

        @block.vector
        def _(dve):
            def low(kk):
                dve.wait_ge(high, kk + 1)
                dve.tensor_tensor(k.h_lo[:, kk, :], k.hT[:, kk, :], k.h_hi[:, kk, :].bitcast(F32), ALU.subtract)
            for kk in range(KT):
                for c, (lo, hi) in enumerate(((0, NP_TOK), (NP_TOK, T))):
                    op = dve.tensor_scalar(k.hT[:, kk, lo:hi], k.hT[:, kk, lo:hi], k.a1[:, kk, c:c + 1],
                                           k.modT[:, kk, c:c + 1], ALU.mult, ALU.add)
                dve.drain().then_inc(shifted, 1)
                if kk > 0:
                    low(kk - 1)
            low(KT - 1)


def phase_projection(nc, k):
    with ExitStack() as mem:
        def sb(name, shape, dt=F32):
            return mem.enter_context(nc.sbuf_tensor(name, shape, dt))
        w = sb("win_ring", [P, 4, KT, P])
        w_hi, w_lo = ([sb(f"{n}{b}", [P, KT, P], F32R) for b in range(2)] for n in ("win_hi", "win_lo"))
        RAW = T + 8
        CV = T + 4
        S_RAW, S_CV = NP_TOK + 6, NP_TOK + 4
        CUT = CHUNKS[0][1] - NP_TOK
        raw = [sb(f"raw{b}", [P, RAW]) for b in range(2)]
        cv = sb("convolved", [P, CV])
        sl = [sb(f"silu_out{b}", [P, T]) for b in range(2)]
        sq = sb("squares", [P, T])
        rt = sb("roots", [P, T])
        ob = [sb(f"proj_out{b}", [P, T]) for b in range(2)]
        gm = sb("gates_by_channel", [48, T])
        s = {n: k.sem(n) for n in ("win_high", "win_low", "proj_summed", "evac", "conv", "silu", "sq", "ones",
                                   "root", "normed", "gates_read", "gates_turned", "raw_zeroed")}
        landed = [k.sem(f"win_landed{u}") for u in range(4)]
        stored = [k.sem(f"proj_stored{b}") for b in range(2)]
        bank = [[k.bank[2 * b], k.bank[2 * b + 1]] for b in range(2)]

        with nc.Block() as block:
            @block.gpsimd
            def _(pool):
                def load(i, u):
                    pool.wait_ge(s["win_low"], i * 4 + u + 1)
                    pool.dma_start(w[:, u], k.d_win[bass.ds(i * 4 + u, 1)].rearrange("a p k n -> p (a k) n")
                                   ).then_inc(landed[u], 16)
                with pool.Fori(0, N_TILES // 4) as i:
                    for u in range(4):
                        load(i, u)
                load(N_TILES // 4, 0)

            @block.tensor
            def _(pe):
                pe.sem_inc(s["ones"], 1)

                def project(i, base, u):
                    n, b = i * 4 + (base + u), (base + u) % 2
                    pe.wait_ge(s["win_low"], n + 5)
                    pe.wait_ge(s["evac"], n + 1)
                    for kk in range(KT):
                        for wt, hs in ((w_hi[b], (k.h_hi, k.h_lo)), (w_lo[b], (k.h_hi,))):
                            for h in hs:
                                for c, (lo, hi) in enumerate(CHUNKS):
                                    mm = pe.matmul(bank[b][c][:, 0:hi - lo], wt[:, kk, :], h[:, kk, lo:hi],
                                                   start=(kk == 0 and wt is w_hi[b] and h is k.h_hi),
                                                   stop=(kk == KT - 1 and wt is w_lo[b]))
                    mm.then_inc(s["proj_summed"], 1)

                def sum_squares(i, base, u):
                    n = i * 4 + (base + u)
                    pe.wait_ge(s["sq"], n + 1)
                    pe.wait_ge(s["root"], n + 1)
                    pe.matmul(k.bank[4][:], k.ones, sq[:, NP_TOK:T], start=True, stop=True)
                    pe.matmul(k.bank[5][:, 0:P], k.ones, sq[:, 0:NP_TOK], start=True, stop=True
                              ).then_inc(s["ones"], 1)

                project(0, 0, 0)
                with pe.Fori(0, QK_TILES // 4) as i:
                    for u in range(4):
                        project(i, 1, u)
                        sum_squares(i, 0, u)
                with pe.Fori(0, (N_TILES - QK_TILES) // 4) as i:
                    for u in range(4):
                        project(i, QK_TILES + 1, u)
                pe.wait_ge(s["gates_read"], 1)
                for t in range(TT):
                    mm = pe.transpose(k.bank[6][:, t * 48:(t + 1) * 48], gm[:, t * P:(t + 1) * P],
                                      k.ident[0:48, 0:48])
                mm.then_inc(s["gates_turned"], 1)

            def bias(n):
                return k.chan[:, bass.ds(n + V_BIN, 1)]

            def wait_store(eng, i, base, u):
                eng.wait_ge(stored[u % 2], i * 32 + (base // 2 + u // 2 + 1) * 16)

            @block.scalar
            def _(act):
                act.sem_inc(s["evac"], 2)
                act.sem_inc(s["silu"], 1)
                act.sem_inc(s["root"], 1)

                def high(i, base, u):
                    v = base + u
                    act.wait_ge(landed[v % 4], i * 16 + 16 * (v // 4 + 1))
                    act.activation(w_hi[v % 2][:], w[:, v % 4], ACT.Copy).then_inc(s["win_high"], 1)

                def to_raw(i, base, u):
                    n, b = i * 4 + (base + u), (base + u) % 2
                    act.wait_ge(s["proj_summed"], n + 1)
                    act.wait_ge(s["conv"], n + 1)
                    act.activation(raw[b][:, 2:2 + NP_TOK], bank[b][0][:, 0:P], ACT.Identity, bias=bias(n))
                    act.activation(raw[b][:, S_RAW:S_RAW + CUT], bank[b][0][:, P:P + CUT], ACT.Identity, bias=bias(n))
                    act.activation(raw[b][:, S_RAW + CUT:S_RAW + NS_TOK], bank[b][1][:, 0:NS_TOK - CUT],
                                   ACT.Identity, bias=bias(n)).then_inc(s["evac"], 1)

                def silu(n, out):
                    act.wait_ge(s["conv"], n + 3)
                    act.activation(out[:, 0:NP_TOK], cv[:, 0:NP_TOK], ACT.Silu)
                    act.activation(out[:, NP_TOK:T], cv[:, S_CV:S_CV + NS_TOK], ACT.Silu).then_inc(s["silu"], 1)

                def roots(i, base, u):
                    n = i * 4 + (base + u)
                    act.wait_ge(s["ones"], n + 2)
                    act.wait_ge(s["normed"], n + 1)
                    sc, bi = k.chan[:, bass.ds(n + V_L2S, 1)], k.chan[:, bass.ds(n + V_L2B, 1)]
                    act.activation(rt[:, 0:NP_TOK], k.bank[5][:, 0:P], ACT.Sqrt, bias=bi, scale=sc)
                    act.activation(rt[:, NP_TOK:T], k.bank[4][:], ACT.Sqrt, bias=bi, scale=sc
                                   ).then_inc(s["root"], 1)

                def qk_tile(i, base, u):
                    to_raw(i, base, u)
                    high(i, base + 2, u)
                    roots(i, base - 1, u)
                    silu(i * 4 + (base + u), sl[(base + u) % 2])

                high(0, 0, 0)
                high(0, 1, 0)
                act.wait_ge(s["raw_zeroed"], 1)
                to_raw(0, 0, 0)
                high(0, 2, 0)
                silu(0, sl[0])
                with act.Fori(0, QK_TILES // 4 - 1) as i:
                    for u in range(4):
                        qk_tile(i, 1, u)
                for u in range(3):
                    qk_tile(0, QK_TILES - 3, u)
                for u in range(V_TILES):
                    to_raw(0, QK_TILES, u)
                    high(0, QK_TILES + 2, u)
                    if u == 0:
                        roots(0, QK_TILES - 1, 0)
                    wait_store(act, 0, QK_TILES, u)
                    silu(QK_TILES + u, ob[u % 2])

                def plain_tile(i, base, u, perm):
                    n, b = i * 4 + (base + u), u % 2
                    act.wait_ge(s["proj_summed"], n + 1)
                    wait_store(act, i, base, u)
                    if perm:
                        act.activation(ob[b][:, 0:NP_TOK], bank[b][0][:, 0:P], ACT.Identity, bias=bias(n))
                        to_columns(ob[b], bank[b], bias(n)).then_inc(s["evac"], 1)
                    else:
                        for c, (lo, hi) in enumerate(CHUNKS):
                            ev = act.activation(ob[b][:, lo:hi], bank[b][c][:, 0:hi - lo], ACT.Identity,
                                                bias=bias(n))
                        ev.then_inc(s["evac"], 1)
                    if isinstance(i, int) and base + u + 2 > GATE_TILE:
                        return
                    high(i, base + 2, u)

                def to_columns(out, banks, b, r0=0, r1=P):
                    out = out[r0:r1, NP_TOK:T].rearrange("p (c r) -> p r c", r=ROWS)
                    cut = CUT // GRID_W
                    for dst, src in ((out[:, 0:cut, :], banks[0][r0:r1, P:P + CUT]),
                                     (out[:, cut:ROWS, :], banks[1][r0:r1, 0:NS_TOK - CUT])):
                        ev = act.activation(dst, src.rearrange("p (r c) -> p r c", c=GRID_W), ACT.Identity, bias=b)
                    return ev

                with act.Fori(0, PERM_TILES // 4) as i:
                    for u in range(4):
                        plain_tile(i, T_MLQ, u, True)
                with act.Fori(0, RASTER_TILES // 4 - 1) as i:
                    for u in range(4):
                        plain_tile(i, T_Z, u, False)
                for u in range(4):
                    plain_tile(0, N_TILES - 4, u, False)
                act.wait_ge(s["proj_summed"], GATE_TILE + 1)
                gate_banks = bank[GATE_TILE % 2]
                act.activation(gm[:, 0:NP_TOK], gate_banks[0][0:48, 0:P], ACT.Identity, bias=bias(GATE_TILE)[0:48])
                act.activation(gm[0:32, NP_TOK:NP_TOK + CUT], gate_banks[0][0:32, P:P + CUT], ACT.Identity,
                               bias=bias(GATE_TILE)[0:32])
                act.activation(gm[0:32, NP_TOK + CUT:T], gate_banks[1][0:32, 0:NS_TOK - CUT], ACT.Identity,
                               bias=bias(GATE_TILE)[0:32])
                to_columns(gm, gate_banks, bias(GATE_TILE)[32:48], 32, 48)
                act.drain().then_inc(s["gates_read"], 1)

            @block.vector
            def _(dve):
                dve.sem_inc(s["win_low"], 4)
                dve.sem_inc(s["conv"], 2)
                dve.sem_inc(s["normed"], 1)

                def low(i, base, u):
                    v = base + u
                    dve.wait_ge(s["win_high"], i * 4 + (v + 1))
                    dve.tensor_tensor(w_lo[v % 2][:], w[:, v % 4], w_hi[v % 2][:].bitcast(F32), ALU.subtract
                                      ).then_inc(s["win_low"], 1)

                def convolve(i, base, u):
                    n = i * 4 + (base + u)
                    dve.wait_ge(s["evac"], n + 3)
                    dve.wait_ge(s["silu"], n + 1)
                    for j in range(5):
                        tap = k.chan[:, bass.ds(n * 5 + (V_CONV + j), 1)]
                        src = raw[(base + u) % 2][:, j:j + CV]
                        if j == 0:
                            dve.tensor_scalar(cv[:], src, tap, None, ALU.mult)
                        else:
                            last = dve.scalar_tensor_tensor(out=cv[:], in0=src, scalar=tap, in1=cv[:],
                                                            op0=ALU.mult, op1=ALU.add)
                        if j < 4:
                            dve.drain()
                    last.then_inc(s["conv"], 1)

                def square(i, base, u):
                    n = i * 4 + (base + u)
                    dve.wait_ge(s["silu"], n + 2)
                    dve.wait_ge(s["ones"], n + 1)
                    dve.tensor_tensor(sq[:], sl[(base + u) % 2][:], sl[(base + u) % 2][:], ALU.mult
                                      ).then_inc(s["sq"], 1)

                def normalize(i, base, u):
                    b = (base + u) % 2
                    dve.wait_ge(s["root"], i * 4 + (base + u) + 2)
                    dve.reciprocal(rt[:], rt[:])
                    dve.drain()
                    dve.wait_ge(stored[b], i * 32 + 16 * ((base + u) // 2 + 1))
                    dve.tensor_tensor(ob[b][:], sl[b][:], rt[:], ALU.mult).then_inc(s["normed"], 1)

                def qk_tile(i, base, u):
                    convolve(i, base, u)
                    low(i, base + 2, u)
                    square(i, base, u)
                    normalize(i, base - 1, u)

                low(0, 0, 0)
                low(0, 1, 0)
                for b in range(2):
                    dve.memset(raw[b][:], 0.0)
                dve.drain().then_inc(s["raw_zeroed"], 1)
                convolve(0, 0, 0)
                low(0, 2, 0)
                square(0, 0, 0)
                with dve.Fori(0, QK_TILES // 4 - 1) as i:
                    for u in range(4):
                        qk_tile(i, 1, u)
                for u in range(3):
                    qk_tile(0, QK_TILES - 3, u)
                for u in range(V_TILES):
                    convolve(0, QK_TILES, u)
                    low(0, QK_TILES + 2, u)
                    if u == 0:
                        normalize(0, QK_TILES - 1, 0)
                rest = GATE_TILE + 1 - (T_MLQ + 2)
                with dve.Fori(0, rest // 4) as i:
                    for u in range(4):
                        low(i, T_MLQ + 2, u)
                for u in range(rest % 4):
                    low(0, GATE_TILE + 1 - rest % 4, u)
                dve.wait_ge(s["gates_turned"], 1)
                dve.tensor_copy(k.gates[:], k.bank[6][:, 0:TT * 48].rearrange("p (t n) -> p t n", t=TT))

            @block.sync
            def _(sp):
                for b in range(2):
                    sp.sem_inc(stored[b], 16)
                for base, tiles, sem, ahead in ((0, QK_TILES, "normed", 2), (QK_TILES, V_TILES, "silu", 2),
                                                (T_MLQ, PERM_TILES + RASTER_TILES, "evac", 3)):
                    with sp.Fori(0, tiles // 4) as i:
                        for u in range(4):
                            n = i * 4 + (base + u)
                            sp.wait_ge(s[sem], n + ahead)
                            sp.dma_start(k.d_proj[bass.ds(n, 1)].rearrange("a p t -> p (a t)"), ob[u % 2][:]
                                         ).then_inc(stored[u % 2], 16)
                for b in range(2):
                    sp.wait_ge(stored[b], 16 * (N_TILES // 2 + 1))


def phase_gates(nc, k):
    with ExitStack() as mem:
        def sb(name, shape):
            return mem.enter_context(nc.sbuf_tensor(name, shape, F32))
        x24 = sb("gate_x", [P, TT, 24])
        e24 = sb("gate_e", [P, TT, 24])
        l24 = sb("gate_l", [P, TT, 24])
        gg = sb("gate_gg", [P, TT, 24])
        al = sb("gate_al", [P, 16])
        bf = k.sem("gates_by_vector")
        ba = k.sem("gates_by_scalar")
        bp = k.sem("gates_by_tensor")
        with nc.Block() as block:
            @block.vector
            def _(dve):
                dve.tensor_tensor(x24[:, :, 0:16], k.gates[:, :, 16:32], all_heads(k.rowp[:, R_DT:R_DT + 16], TT),
                                  ALU.add)
                dve.scalar_tensor_tensor(out=x24[:, :, 16:24], in0=k.gates[:, :, 40:48], scalar=-1.0,
                                         in1=all_heads(k.rowp[:, R_FB:R_FB + 8], TT), op0=ALU.mult, op1=ALU.subtract)
                dve.tensor_copy(k.ident_bf[:], k.ident)
                for d in range(2):
                    dve.tensor_copy(k.neg_bf[:, d, :], k.neg[d])
                dve.tensor_tensor(k.ci[:], k.gates[:, :, 32:40], all_heads(k.rowp[:, R_IB:R_IB + 8], TT), ALU.add)
                dve.drain()
                dve.scalar_tensor_tensor(out=e24[:], in0=x24[:], scalar=-1.0, in1=x24[:], op0=ALU.mult, op1=ALU.min
                                         ).then_inc(bf, 1)
                dve.wait_ge(ba, 1)
                dve.scalar_tensor_tensor(out=gg[:], in0=x24[:], scalar=0.0, in1=l24[:], op0=ALU.max, op1=ALU.add)
                dve.drain()
                dve.scalar_tensor_tensor(out=gg[:, :, 0:16], in0=gg[:, :, 0:16], scalar=-1.0,
                                         in1=all_heads(al[:], TT), op0=ALU.mult, op1=ALU.mult)
                dve.tensor_scalar(gg[:, :, 16:24], gg[:, :, 16:24], -1.0, None, ALU.mult)
                dve.drain().then_inc(bf, 1)
                dve.wait_ge(bp, 1)
                cum = [k.bank[d][:, 0:TT * 24].rearrange("p (t n) -> p t n", t=TT) for d in range(3)]
                for d in range(2):
                    dve.tensor_copy(k.G[:, :, 8 * d:8 * d + 8], cum[d][:, :, 8 * d:8 * d + 8])
                    dve.tensor_copy(k.b_ml[:, :, 4 * d:4 * d + 4], cum[d][:, :, 16 + 4 * d:20 + 4 * d])
                dve.tensor_copy(k.g_tot[:], cum[2][:, :, 0:16])
                dve.tensor_copy(k.b_tot[:], cum[2][:, :, 16:24])
                dve.drain()
                dve.tensor_scalar(k.nG[:], k.G[:], -1.0, None, ALU.mult)
                dve.tensor_tensor(k.wS[:], k.g_tot[:], k.G[:], ALU.subtract)
                dve.tensor_tensor(k.ci[:], k.ci[:], k.b_ml[:], ALU.subtract)
                dve.drain().then_inc(bf, 1)
                dve.wait_ge(ba, 2)
                dve.tensor_scalar(k.neg_eG[:], k.eG[:], -1.0, None, ALU.mult)
                dve.tensor_tensor(k.bw[:], k.beta[:], k.wS[:], ALU.mult)

            @block.scalar
            def _(act):
                act.activation(k.beta[:], k.gates[:, :, 0:16], ACT.Sigmoid)
                act.activation(al[:], k.rowp[:, R_AL:R_AL + 16], ACT.Exp)
                act.wait_ge(bf, 1)
                act.activation(e24[:], e24[:], ACT.Exp)
                act.drain()
                act.activation(l24[:], e24[:], ACT.Ln, bias=1.0)
                act.drain().then_inc(ba, 1)
                act.wait_ge(bf, 3)
                act.activation(k.eG[:], k.G[:], ACT.Exp)
                act.activation(k.wS[:], k.wS[:], ACT.Exp)
                act.activation(k.eT[:], k.g_tot[:], ACT.Exp)
                act.drain().then_inc(ba, 1)

            @block.tensor
            def _(pe):
                pe.wait_ge(bf, 2)
                for d, lhs in enumerate((k.tri[0], k.tri[1], k.ones)):
                    mm = pe.matmul(k.bank[d][:, 0:TT * 24], lhs, gg[:].rearrange("p t n -> p (t n)"),
                                   start=True, stop=True)
                mm.then_inc(bp, 1)


A_FILLS = (["kT", "G", "KK", "L1"] + [f"{x}{s}" for s in LEVELS[1:] for x in ("Y", "XT")] + ["KS", "P", "O"])
B_FILLS = (["vT", "QK"] + [f"XY{s}" for s in LEVELS[1:]] + ["QS", "S"])


def phase_deltanet(nc, k):
    with ExitStack() as mem:
        def sb(name, shape):
            return mem.enter_context(nc.sbuf_tensor(name, shape, F32))

        def quads(name):
            return [sb(f"{name}{q}", [P, 4, P]) for q in range(4)]
        staged = [sb(f"dn_staged{d}", [P, 24, P]) for d in range(2)]
        ktok, vtok, dg, DT, NT, sc = (quads(n) for n in ("ktok", "vtok", "diagG", "decayT", "LT", "scoresT"))
        X, XT, R, vn, vs = (quads(n) for n in ("X", "XT", "R", "vnew", "vweighted"))
        Y = [sb(f"Y{q}", [P, 4, P // 2]) for q in range(4)]
        S = [[sb(f"S{'ps'[x]}{q}", [P, 4, P]) for q in range(4)] for x in range(2)]
        A = [Bank(k.bank[q], k.sem(f"dnA_filled{q}"), k.sem(f"dnA_emptied{q}"), A_FILLS) for q in range(4)]
        B = [Bank(k.bank[4 + q], k.sem(f"dnB_filled{q}"), k.sem(f"dnB_emptied{q}"), B_FILLS) for q in range(4)]
        landed = [k.sem(f"dn_landed{d}") for d in range(2)]
        used = [k.sem(f"dn_stage_used{d}") for d in range(2)]
        zeroed, state_in, prompt_done, state_out = (k.sem(n) for n in ("dn_zeroed", "dn_state_in", "dn_prompt_done",
                                                                       "dn_state_out"))
        dg_ready = [k.sem(f"dg_ready{q}") for q in range(4)]
        QUADS = [(q, q % 2, 4 * (q // 2)) for q in range(4)]

        def sources(ap, s, d):
            return ap.rearrange("p (b two s) -> p b two s", two=2, s=s)[:, :, d, :]

        def steps(eng, body):
            body(0, (0, 0), 0)
            with eng.Fori(0, TT - 1) as i:
                body(i + 1, (i + 1, i * -1 + (TT - 1)), 1)

        with nc.Block() as block:
            @block.sync
            def _(sp):
                for q, d, h0 in QUADS:
                    sp.dma_start(S[1][q][:], k.d_sdn[d, h0:h0 + 4].rearrange("h p n -> p h n")).then_inc(state_in, 16)

                def load(step, tiles, _):
                    for d in range(2):
                        if not isinstance(step, int):
                            sp.wait_ge(used[d], step * 2)
                        sp.dma_start(staged[d][:], k.d_proj.rearrange("m p t -> p m t")[
                            :, 0:24, bass.ds(tiles[d] * P, P)]).then_inc(landed[d], 16)
                steps(sp, load)
                sp.wait_ge(prompt_done, 4)
                for q, d, h0 in QUADS:
                    sp.dma_start(k.o_sdn[d, h0:h0 + 4].rearrange("h p n -> p h n"), S[0][q][:]
                                 ).then_inc(state_out, 16)
                sp.wait_ge(state_out, 64)

            @block.gpsimd
            def _(pool):
                pool.memset(k.o_dn[:], 0.0)
                for q in range(4):
                    pool.memset(S[0][q][:], 0.0)
                pool.drain().then_inc(zeroed, 1)

                def diagonals(step, tiles, _):
                    for q, d, h0 in QUADS:
                        if not isinstance(step, int):
                            A[q].wait_filled(pool, step + -1, "G")
                        c = d * 8 + h0
                        pool.tensor_tensor(dg[q][:], all_heads(k.ident), per_head(col(k.G[:], tiles[d], c, c + 4), P),
                                           ALU.mult).then_inc(dg_ready[q], 1)
                steps(pool, diagonals)

            @block.tensor
            def _(pe):
                def fill(bank, step, name, args, width=P):
                    bank.wait_free(pe, step, name)
                    for h in range(4):
                        terms = args(h)
                        for n, (lhs, rhs) in enumerate(terms):
                            mm = pe.matmul(bank.t[:, h * width:(h + 1) * width], lhs, rhs, start=(n == 0),
                                           stop=(n == len(terms) - 1))
                    mm.then_inc(bank.filled, 1)

                def turn(bank, step, name, src):
                    bank.wait_free(pe, step, name)
                    for h in range(4):
                        mm = pe.transpose(bank.t[:, h * P:(h + 1) * P], src(h), k.ident)
                    mm.then_inc(bank.filled, 1)

                def body(step, tiles, x):
                    for q, d, h0 in QUADS:
                        pe.wait_ge(landed[d], step * 16 + 16)
                        turn(A[q], step, "kT", lambda h: staged[d][:, 8 + h0 + h, :])
                        turn(B[q], step, "vT", lambda h: staged[d][:, 16 + h0 + h, :])
                    for q, d, h0 in QUADS:
                        pe.wait_ge(dg_ready[q], step + 1)
                        A[q].wait_free(pe, step, "G")
                        add_mask(pe, k, A[q].t, d)
                        mm = pe.matmul(h4(A[q].t[:]), k.ones, dg[q][:], start=False, stop=True)
                        mm.then_inc(A[q].filled, 1)
                    for q, d, h0 in QUADS:
                        kh = lambda h: staged[d][:, 8 + h0 + h, :]
                        fill(A[q], step, "KK", lambda h: [(kh(h), kh(h))])
                        fill(B[q], step, "QK", lambda h: [(kh(h), staged[d][:, h0 + h, :])])
                    for q, d, h0 in QUADS:
                        A[q].wait_emptied(pe, step, "KK")
                        turn(A[q], step, "L1", lambda h: NT[q][:, h, :])
                    for s in LEVELS[1:]:
                        for q, d, h0 in QUADS:
                            if s > 2:
                                B[q].wait_emptied(pe, step, f"XY{s // 2}")
                                turn(A[q], step, f"XT{s // 2}", lambda h: X[q][:, h, :])
                        for q, d, h0 in QUADS:
                            fill(A[q], step, f"Y{s}", lambda h: [(NT[q][:, h, :], sources(X[q][:, h, :], s, d))],
                                 P // 2)
                        for q, d, h0 in QUADS:
                            A[q].wait_emptied(pe, step, f"Y{s}")
                            fill(B[q], step, f"XY{s}", lambda h: [(XT[q][:, h, :], Y[q][:, h, :])], P // 2)
                    for q, d, h0 in QUADS:
                        B[q].wait_emptied(pe, step, f"XY{LEVELS[-1]}")
                        turn(A[q], step, f"XT{LEVELS[-1]}", lambda h: X[q][:, h, :])
                    pe.wait_ge(zeroed, 1) if x == 0 else pe.wait_ge(state_in, 64)
                    for q, d, h0 in QUADS:
                        fill(B[q], step, "QS", lambda h: [(staged[d][:, h0 + h, :], S[x][q][:, h, :])])
                        fill(A[q], step, "KS", lambda h: [(staged[d][:, 8 + h0 + h, :], S[x][q][:, h, :])])
                    for q, d, h0 in QUADS:
                        A[q].wait_filled(pe, step, "KS")
                        pe.sem_inc(used[d], 1)
                        fill(A[q], step, "P", lambda h: [(XT[q][:, h, :], R[q][:, h, :])])
                    for q, d, h0 in QUADS:
                        fill(A[q], step, "O", lambda h: [(sc[q][:, h, :], vn[q][:, h, :])])
                        fill(B[q], step, "S", lambda h: [(ktok[q][:, h, :], vs[q][:, h, :])])
                steps(pe, body)

            @block.scalar
            def _(act):
                def body(step, tiles, x):
                    for q, d, h0 in QUADS:
                        A[q].wait_filled(act, step, "kT")
                        act.activation(ktok[q][:], h4(A[q].t[:]), ACT.Copy).then_inc(A[q].emptied, 1)
                        B[q].wait_filled(act, step, "vT")
                        act.activation(vtok[q][:], h4(B[q].t[:]), ACT.Copy).then_inc(B[q].emptied, 1)
                    for q, d, h0 in QUADS:
                        A[q].wait_filled(act, step, "G")
                        for h in range(4):
                            c = d * 8 + h0 + h
                            ex = act.activation(DT[q][:, h, :], A[q].t[:, h * P:(h + 1) * P], ACT.Exp,
                                                bias=col(k.nG[:], tiles[d], c, c + 1))
                        ex.then_inc(A[q].emptied, 1)
                    for s in LEVELS[1:]:
                        for q, d, h0 in QUADS:
                            A[q].wait_filled(act, step, f"XT{s}")
                            act.activation(XT[q][:], h4(A[q].t[:]), ACT.Copy).then_inc(A[q].emptied, 1)
                    for q, d, h0 in QUADS:
                        A[q].wait_filled(act, step, "P")
                        for h in range(4):
                            c = d * 8 + h0 + h
                            act.activation(vn[q][:, h, :], A[q].t[:, h * P:(h + 1) * P], ACT.Copy,
                                           scale=col(k.beta[:], tiles[d], c, c + 1))
                            ex = act.activation(vs[q][:, h, :], A[q].t[:, h * P:(h + 1) * P], ACT.Copy,
                                                scale=col(k.bw[:], tiles[d], c, c + 1))
                        ex.then_inc(A[q].emptied, 1)
                steps(act, body)

            @block.vector
            def _(dve):
                dve.wait_ge(zeroed, 1)
                dve.wait_ge(state_in, 64)

                def body(step, tiles, x):
                    for q, d, h0 in QUADS:
                        A[q].wait_filled(dve, step, "KK")
                        A[q].wait_emptied(dve, step, "G")
                        for h in range(4):
                            c = d * 8 + h0 + h
                            op = dve.scalar_tensor_tensor(
                                out=NT[q][:, h, :], in0=A[q].t[:, h * P:(h + 1) * P],
                                scalar=col(k.beta[:], tiles[d], c, c + 1), in1=DT[q][:, h, :],
                                op0=ALU.mult, op1=ALU.mult)
                        op.then_inc(A[q].emptied, 1)
                        B[q].wait_filled(dve, step, "QK")
                        dve.tensor_tensor(sc[q][:], h4(B[q].t[:]), DT[q][:], ALU.mult).then_inc(B[q].emptied, 1)
                    for q, d, h0 in QUADS:
                        A[q].wait_filled(dve, step, "L1")
                        dve.tensor_tensor(XT[q][:], NT[q][:], all_heads(k.level1(d)), ALU.mult)
                        dve.tensor_tensor(X[q][:], h4(A[q].t[:]), all_heads(k.level1(1 - d)), ALU.mult)
                        dve.drain()
                        dve.tensor_tensor(XT[q][:], all_heads(k.ident), XT[q][:], ALU.subtract)
                        dve.tensor_tensor(X[q][:], all_heads(k.ident), X[q][:], ALU.subtract
                                          ).then_inc(A[q].emptied, 1)
                    for n, s in enumerate(LEVELS[1:], 1):
                        for q, d, h0 in QUADS:
                            A[q].wait_filled(dve, step, f"Y{s}")
                            dve.tensor_tensor(Y[q][:], A[q].t[:, 0:2 * P].rearrange("p (h n) -> p h n", h=4),
                                              all_heads(k.level(d, n)), ALU.mult).then_inc(A[q].emptied, 1)
                        for q, d, h0 in QUADS:
                            B[q].wait_filled(dve, step, f"XY{s}")
                            xs = sources(X[q][:].rearrange("p h n -> p (h n)"), s, d)
                            dve.tensor_tensor(xs, xs, B[q].t[:, 0:2 * P].rearrange("p (b s) -> p b s", s=s),
                                              ALU.subtract).then_inc(B[q].emptied, 1)
                    for q, d, h0 in QUADS:
                        B[q].wait_filled(dve, step, "QS")
                        if x == 0 and d == 1:
                            dve.drain()
                        for h in range(4):
                            c = d * 8 + h0 + h
                            o = col(k.o_dn[:], tiles[d], (h0 + h) * P, (h0 + h + 1) * P)
                            op = dve.scalar_tensor_tensor(out=o, in0=B[q].t[:, h * P:(h + 1) * P],
                                                          scalar=col(k.eG[:], tiles[d], c, c + 1), in1=o,
                                                          op0=ALU.mult, op1=ALU.add)
                        op.then_inc(B[q].emptied, 1)
                        A[q].wait_filled(dve, step, "KS")
                        A[q].wait_emptied(dve, step, "kT")
                        B[q].wait_emptied(dve, step, "vT")
                        for h in range(4):
                            c = d * 8 + h0 + h
                            op = dve.scalar_tensor_tensor(out=R[q][:, h, :], in0=A[q].t[:, h * P:(h + 1) * P],
                                                          scalar=col(k.neg_eG[:], tiles[d], c, c + 1),
                                                          in1=vtok[q][:, h, :], op0=ALU.mult, op1=ALU.add)
                        op.then_inc(A[q].emptied, 1)
                    dve.drain()
                    for q, d, h0 in QUADS:
                        A[q].wait_filled(dve, step, "O")
                        if x == 0 and d == 1:
                            dve.drain()
                        o = col(k.o_dn[:], tiles[d], h0 * P, (h0 + 4) * P)
                        dve.tensor_tensor(o, o, A[q].t[:], ALU.add).then_inc(A[q].emptied, 1)
                        B[q].wait_filled(dve, step, "S")
                        for h in range(4):
                            c = d * 8 + h0 + h
                            op = dve.scalar_tensor_tensor(out=S[x][q][:, h, :], in0=S[x][q][:, h, :],
                                                          scalar=col(k.eT[:], tiles[d], c, c + 1),
                                                          in1=B[q].t[:, h * P:(h + 1) * P], op0=ALU.mult, op1=ALU.add)
                        op.then_inc(B[q].emptied, 1)
                    dve.drain()
                    if x == 0:
                        dve.sem_inc(prompt_done, 4)
                steps(dve, body)


M_FILLS = {"A": ["kT", "QK", "NP1", "NP3"], "B": ["v01", "NQ0", "NQ2", "S0", "S2"],
           "C": ["v23", "NQ1", "NQ3", "S1", "S3"], "D": ["Cbc", "Mbc", "NP0", "NP2"]}


def phase_mlstm(nc, k):
    DA = DV_ML + 1
    with ExitStack() as mem:
        def sb(name, shape):
            return mem.enter_context(nc.sbuf_tensor(name, shape, F32))

        def dirs(name, shape):
            return [sb(f"{name}{d}", shape) for d in range(2)]
        staged = dirs("ml_staged", [P, 16, P])
        ktok, dg, dgM, ET, PT, kw = (dirs(n, [P, 4, P]) for n in ("ml_ktok", "diagC", "diagM", "expT", "pT", "kweighted"))
        vtok = dirs("ml_vtok", [P, 4, DA])
        nu = dirs("numerator", [P, 4, DA])
        S = [dirs(f"C{'ps'[x]}", [P, 4, DA]) for x in range(2)]
        m = [dirs(f"m{'ps'[x]}", [P, 4]) for x in range(2)]
        M, nM, mx, nMl, inter, enm, carry, wS, rden, bM = (
            dirs(n, [P, 4]) for n in ("M", "negM", "maxC", "negMend", "inter", "exp_neg_m", "carry", "wend",
                                      "rden", "bM"))
        bank = [{f: Bank(k.bank[4 * d + n], k.sem(f"ml{f}_filled{d}"), k.sem(f"ml{f}_emptied{d}"), M_FILLS[f])
                 for n, f in enumerate("ABCD")} for d in range(2)]
        landed = [k.sem(f"ml_landed{d}") for d in range(2)]
        sems = ("ready", "dgC", "dgM", "max", "expo", "scalars", "kw", "nu", "den")
        s = [{n: k.sem(f"ml_{n}{d}") for n in sems} for d in range(2)]
        state_in, state_out, prompt_done = k.sem("ml_state_in"), k.sem("ml_state_out"), k.sem("ml_prompt_done")
        END = (P - 1, 0)

        def steps(eng, body):
            body(0, (0, 0), 0)
            with eng.Fori(0, TT - 1) as i:
                body(i + 1, (i + 1, i * -1 + (TT - 1)), 1)

        def gate(t3, tiles, d, h=None):
            a, b = (4 * d, 4 * d + 4) if h is None else (4 * d + h, 4 * d + h + 1)
            return col(t3[:], tiles[d], a, b)

        with nc.Block() as block:
            @block.sync
            def _(sp):
                for d in range(2):
                    sp.dma_start(S[1][d][:, :, 0:DV_ML], k.d_smc[d].rearrange("h p n -> p h n")).then_inc(state_in, 16)
                    for h in range(4):
                        sp.dma_start(S[1][d][:, h, DV_ML:DA], k.d_smn[d, h:h + 1, :].rearrange("a p -> p a")
                                     ).then_inc(state_in, 16)

                def load(step, tiles, _):
                    for d in range(2):
                        if not isinstance(step, int):
                            bank[d]["A"].wait_filled(sp, step + -1, "NP3")
                        sp.dma_start(staged[d][:], k.d_proj.rearrange("m p t -> p m t")[
                            :, T_MLQ:T_MLQ + 16, bass.ds(tiles[d] * P, P)]).then_inc(landed[d], 16)
                steps(sp, load)
                sp.wait_ge(prompt_done, 1)
                for d in range(2):
                    sp.dma_start(k.o_smc[d].rearrange("h p n -> p h n"), S[0][d][:, :, 0:DV_ML]).then_inc(state_out, 16)
                    for h in range(4):
                        sp.dma_start(k.o_smn[d, h:h + 1, :].rearrange("a p -> p a"), S[0][d][:, h, DV_ML:DA]
                                     ).then_inc(state_out, 16)
                    sp.dma_start(k.o_smm[d:d + 1, :], m[0][d][0:1, :]).then_inc(state_out, 16)
                sp.wait_ge(state_out, 16 * 12)

            @block.gpsimd
            def _(pool):
                for d in range(2):
                    pool.memset(vtok[d][:], 1.0)
                    pool.memset(S[0][d][:], 0.0)
                    pool.memset(m[0][d][:], 0.0)
                pool.memset(k.o_ml[:], 0.0)
                pool.drain().then_inc(s[0]["ready"], 1)

                def body(step, tiles, _):
                    for d in range(2):
                        if not isinstance(step, int):
                            bank[d]["D"].wait_filled(pool, step + -1, "Cbc")
                        pool.tensor_tensor(dg[d][:], all_heads(k.ident), per_head(gate(k.ci, tiles, d), P), ALU.mult
                                           ).then_inc(s[d]["dgC"], 1)
                steps(pool, body)

            @block.tensor
            def _(pe):
                pe.wait_ge(s[0]["ready"], 1)

                def body(step, tiles, x):
                    for d in range(2):
                        b = bank[d]
                        pe.wait_ge(landed[d], step * 16 + 16)
                        b["A"].wait_free(pe, step, "kT")
                        for h in range(4):
                            mm = pe.transpose(b["A"].t[:, h * P:(h + 1) * P], staged[d][:, 4 + h, :], k.ident)
                        mm.then_inc(b["A"].filled, 1)
                        for n, f in enumerate("BC"):
                            b[f].wait_free(pe, step, ("v01", "v23")[n])
                            for j in range(4):
                                mm = pe.transpose(b[f].t[:, j * P:(j + 1) * P], staged[d][:, 8 + 4 * n + j, :], k.ident)
                            mm.then_inc(b[f].filled, 1)
                        pe.wait_ge(s[d]["dgC"], step + 1)
                        b["D"].wait_free(pe, step, "Cbc")
                        add_mask(pe, k, b["D"].t, 1 - d)
                        pe.matmul(h4(b["D"].t[:]), k.ones, dg[d][:], start=False, stop=True).then_inc(b["D"].filled, 1)
                    for d in range(2):
                        b = bank[d]
                        b["A"].wait_free(pe, step, "QK")
                        for h in range(4):
                            mm = pe.matmul(b["A"].t[:, h * P:(h + 1) * P], staged[d][:, 4 + h, :], staged[d][:, h, :],
                                           start=True, stop=True)
                        mm.then_inc(b["A"].filled, 1)
                    for d in range(2):
                        b = bank[d]
                        pe.wait_ge(s[d]["dgM"], step + 1)
                        b["D"].wait_free(pe, step, "Mbc")
                        add_mask(pe, k, b["D"].t, d)
                        pe.matmul(h4(b["D"].t[:]), k.ones, dgM[d][:], start=False, stop=True).then_inc(b["D"].filled, 1)
                    if x == 1:
                        pe.wait_ge(state_in, 16 * 10)
                    for h in range(4):
                        for d in range(2):
                            b = bank[d]
                            fq, fp = ("B", "D") if h % 2 == 0 else ("C", "A")
                            b[fq].wait_free(pe, step, f"NQ{h}")
                            if h == 0:
                                b["C"].wait_free(pe, step, "NQ1")
                            pe.matmul(b[fq].t[:, 0:DA], staged[d][:, h, :], S[x][d][:, h, :], start=True, stop=True
                                      ).then_inc(b[fq].filled, 1)
                            b["A"].wait_emptied(pe, step, "QK")
                            b[fp].wait_free(pe, step, f"NP{h}")
                            pe.matmul(b[fp].t[:, 0:DA], PT[d][:, h, :], vtok[d][:, h, :], start=True, stop=True
                                      ).then_inc(b[fp].filled, 1)
                    for h in range(4):
                        for d in range(2):
                            b = bank[d]
                            f = "BC"[h % 2]
                            pe.wait_ge(s[d]["kw"], step + 1)
                            b[f].wait_free(pe, step, f"S{h}")
                            pe.matmul(b[f].t[:, 0:DA], kw[d][:, h, :], vtok[d][:, h, :], start=True, stop=True
                                      ).then_inc(b[f].filled, 1)
                steps(pe, body)

            @block.scalar
            def _(act):
                act.wait_ge(s[0]["ready"], 1)

                def body(step, tiles, x):
                    for d in range(2):
                        b = bank[d]
                        b["A"].wait_filled(act, step, "kT")
                        if not isinstance(step, int):
                            act.wait_ge(s[d]["kw"], step)
                        act.activation(ktok[d][:], h4(b["A"].t[:]), ACT.Copy).then_inc(b["A"].emptied, 1)
                        for n, f in enumerate("BC"):
                            b[f].wait_filled(act, step, ("v01", "v23")[n])
                            act.activation(vtok[d][:, 2 * n:2 * n + 2, 0:DV_ML],
                                           b[f].t[:].rearrange("p (h n) -> p h n", h=2), ACT.Copy
                                           ).then_inc(b[f].emptied, 1)
                    for d in range(2):
                        b = bank[d]
                        b["D"].wait_filled(act, step, "Mbc")
                        if not isinstance(step, int):
                            act.wait_ge(s[d]["scalars"], step)
                        act.activation(nMl[d][:].unsqueeze(2), h4(b["D"].t[:])[:, :, END[d]:END[d] + 1], ACT.Copy)
                        for h in range(4):
                            act.activation(ET[d][:, h, :], b["D"].t[:, h * P:(h + 1) * P], ACT.Exp,
                                           bias=gate(k.ci, tiles, d, h))
                        act.drain().then_inc(b["D"].emptied, 1)
                    for d in range(2):
                        act.wait_ge(s[d]["expo"], step + 1)
                        for t4 in (inter, enm, carry, wS):
                            act.activation(t4[d][:], t4[d][:], ACT.Exp)
                        act.drain().then_inc(s[d]["scalars"], 1)
                    for h in range(4):
                        for d in range(2):
                            fq = "BC"[h % 2]
                            bank[d][fq].wait_filled(act, step, f"NQ{h}")
                            act.activation(nu[d][:, h, :], bank[d][fq].t[:, 0:DA], ACT.Copy,
                                           scale=inter[d][:, h:h + 1]).then_inc(bank[d][fq].emptied, 1)
                steps(act, body)

            @block.vector
            def _(dve):
                dve.wait_ge(s[0]["ready"], 1)
                for d in range(2):
                    dve.tensor_copy(m[1][d][:], k.rowp[:, R_M0 + 4 * d:R_M0 + 4 * d + 4])
                dve.drain()

                def body(step, tiles, x):
                    for d in range(2):
                        b = bank[d]
                        b["D"].wait_filled(dve, step, "Cbc")
                        dve.tensor_reduce(mx[d][:], h4(b["D"].t[:]), AX.X, ALU.max).then_inc(b["D"].emptied, 1)
                        dve.drain()
                        dve.tensor_tensor(M[d][:], mx[d][:], m[x][d][:], ALU.max)
                        dve.drain()
                        dve.tensor_scalar(nM[d][:], M[d][:], -1.0, None, ALU.mult)
                        dve.tensor_tensor(inter[d][:], m[x][d][:], M[d][:], ALU.subtract)
                        dve.tensor_tensor(bM[d][:], M[d][:], gate(k.b_ml, tiles, d), ALU.add)
                        dve.drain()
                        dve.tensor_scalar(enm[d][:], bM[d][:], -1.0, None, ALU.mult)
                        dve.tensor_tensor(dgM[d][:], all_heads(k.ident), per_head(nM[d][:], P), ALU.mult
                                          ).then_inc(s[d]["dgM"], 1)
                    for d in range(2):
                        b = bank[d]
                        b["D"].wait_emptied(dve, step, "Mbc")
                        dve.tensor_tensor(carry[d][:], m[x][d][:], nMl[d][:], ALU.add)
                        dve.tensor_tensor(wS[d][:], gate(k.ci, tiles, d), nMl[d][:], ALU.add)
                        dve.drain().then_inc(s[d]["expo"], 1)
                        dve.tensor_tensor(m[x][d][:], gate(k.b_tot, tiles, d), nMl[d][:], ALU.subtract)
                        b["A"].wait_filled(dve, step, "QK")
                        dve.scalar_tensor_tensor(out=PT[d][:], in0=h4(b["A"].t[:]), scalar=K_SCALE, in1=ET[d][:],
                                                 op0=ALU.mult, op1=ALU.mult).then_inc(b["A"].emptied, 1)
                    for d in range(2):
                        dve.wait_ge(s[d]["scalars"], step + 1)
                        bank[d]["A"].wait_emptied(dve, step, "kT")
                        dve.tensor_scalar(wS[d][:], wS[d][:], K_SCALE, None, ALU.mult)
                        dve.drain()
                        dve.tensor_tensor(kw[d][:], ktok[d][:], per_head(wS[d][:], P), ALU.mult
                                          ).then_inc(s[d]["kw"], 1)
                    for h in range(4):
                        for d in range(2):
                            b = bank[d]
                            fq, fp = ("B", "D") if h % 2 == 0 else ("C", "A")
                            b[fq].wait_emptied(dve, step, f"NQ{h}")
                            b[fp].wait_filled(dve, step, f"NP{h}")
                            dve.tensor_tensor(nu[d][:, h, :], nu[d][:, h, :], b[fp].t[:, 0:DA], ALU.add
                                              ).then_inc(b[fp].emptied, 1)
                    dve.drain()
                    for d in range(2):
                        dve.tensor_tensor(rden[d][:].unsqueeze(2), nu[d][:, :, DV_ML:DA], nu[d][:, :, DV_ML:DA], ALU.mult)
                        dve.tensor_scalar(mx[d][:].unsqueeze(2), nu[d][:, :, DV_ML:DA], -1.0, None, ALU.mult)
                        dve.drain()
                        dve.tensor_tensor(rden[d][:].unsqueeze(2), nu[d][:, :, DV_ML:DA], mx[d][:].unsqueeze(2), ALU.max)
                        dve.drain()
                        dve.tensor_tensor(rden[d][:], rden[d][:], enm[d][:], ALU.max)
                        dve.drain()
                        dve.reciprocal(rden[d][:], rden[d][:])
                        dve.drain()
                        for h in range(4):
                            o = col(k.o_ml[:], tiles[d], h * DV_ML, (h + 1) * DV_ML)
                            dve.scalar_tensor_tensor(out=o, in0=nu[d][:, h, 0:DV_ML], scalar=rden[d][:, h:h + 1],
                                                     in1=o, op0=ALU.mult, op1=ALU.add)
                        dve.drain()
                    for h in range(4):
                        for d in range(2):
                            f = bank[d]["BC"[h % 2]]
                            f.wait_filled(dve, step, f"S{h}")
                            dve.scalar_tensor_tensor(out=S[x][d][:, h, :], in0=S[x][d][:, h, :],
                                                     scalar=carry[d][:, h:h + 1], in1=f.t[:, 0:DA],
                                                     op0=ALU.mult, op1=ALU.add).then_inc(f.emptied, 1)
                    dve.drain()
                    if x == 0:
                        dve.sem_inc(prompt_done, 1)
                steps(dve, body)


class Gate2:

    def __init__(self, nc, k, mem, first, buffers):
        self.k, self.first, self.buffers = k, first, buffers
        self.w = [mem.enter_context(nc.sbuf_tensor(f"wmod_gate2_ring{first}_{b}", [P, 4, KT, P], F32))
                  for b in range(buffers)]
        self.rows = mem.enter_context(nc.sbuf_tensor(f"gate2_rows{first}", [2, 512], F32))
        self.landed = [k.sem(f"wmod_gate2_landed{first}_{g}") for g in range(2)]
        self.summed, self.copied, self.turned, self.stored = (k.sem(f"gate2_{n}{first}") for n in (
            "summed", "copied", "turned", "stored"))

    def load(self, sp, g):
        if g >= self.buffers:
            sp.wait_ge(self.summed, g)
        for u in range(4):
            sp.dma_start(self.w[g % self.buffers][:, u], self.k.d_wmod[self.first + 4 * g + u]
                         ).then_inc(self.landed[g], 16)

    def multiply(self, pe, g):
        k, w = self.k, self.w[g % self.buffers]
        pe.wait_ge(self.landed[g], 64)
        for kk in range(KT):
            mm = pe.matmul(k.bank[6][0:2, :].rearrange("p (u n) -> p u n", u=4), k.cond[:, kk, :], w[:, :, kk, :],
                           start=(kk == 0), stop=(kk == KT - 1))
        mm.then_inc(self.summed, 1)
        pe.wait_ge(self.copied, g + 1)
        if g > 0:
            pe.wait_ge(self.stored, g)
        for u in range(4):
            mm = pe.matmul(k.bank[7][:, 2 * u:2 * u + 2], self.rows[:, u * P:(u + 1) * P], k.ident[0:2, 0:2],
                           start=True, stop=True)
        mm.then_inc(self.turned, 1)

    def copy(self, act, g):
        act.wait_ge(self.summed, g + 1)
        if g > 0:
            act.wait_ge(self.turned, g)
        act.activation(self.rows[:], self.k.bank[6][0:2, :], ACT.Copy).then_inc(self.copied, 1)

    def store(self, dve, g):
        k, m = self.k, self.first + 4 * g
        dve.wait_ge(self.turned, g + 1)
        dve.tensor_tensor(k.modT[:, m:m + 4, :], k.bank[7][:, 0:8].rearrange("p (m c) -> p m c", c=2),
                          k.chan[:, V_BMOD + m:V_BMOD + m + 4].unsqueeze(2).to_broadcast([P, 4, 2]), ALU.add
                          ).then_inc(self.stored, 1)


def phase_branch_outputs(nc, k):
    with ExitStack() as mem:
        def sb(name, shape):
            return mem.enter_context(nc.sbuf_tensor(name, shape, F32))
        gate = [sb("z_gate", [P, 8, T]), sb("mo_gate", [P, 8, T])]
        sq = sb("o_squares", [P, TT, 1024])
        ms = [sb("dn_ms", [P, TT * H_DN]), sb("ml_ms", [P, TT * H_ML])]
        rs = [sb("dn_rs", [P, TT * H_DN]), sb("ml_rs", [P, TT * H_ML])]
        gate_in = [k.sem("z_in"), k.sem("mo_in")]
        gated, meaned, rooted, scaled, turned, read = (k.sem(n) for n in ("bo_gated", "bo_meaned", "bo_rooted",
                                                                         "bo_scaled", "bo_turned", "bo_read"))
        o = [k.o_dn, k.o_ml]
        heads = [H_DN, H_ML]
        m = Gate2(nc, k, mem, 5 * KT, 1)
        with nc.Block() as block:
            @block.sync
            def _(sp):
                m.load(sp, 0)
                for b, t0 in enumerate((T_Z, T_MO)):
                    sp.dma_start(gate[b][:], k.d_proj[t0:t0 + 8].rearrange("m p t -> p m t")).then_inc(gate_in[b], 16)
                m.load(sp, 1)

            @block.scalar
            def _(act):
                for b in range(2):
                    act.wait_ge(meaned, b + 1)
                    act.activation(rs[b][:], ms[b][:], ACT.Sqrt).then_inc(rooted, 1)
                m.copy(act, 0)
                for b, f in enumerate((ACT.Silu, ACT.Sigmoid)):
                    act.wait_ge(gate_in[b], 16)
                    act.activation(gate[b][:], gate[b][:], f).then_inc(gated, 1)
                m.copy(act, 1)

            @block.vector
            def _(dve):
                for b in range(2):
                    per = 1024 // heads[b]
                    dve.tensor_tensor(sq[:], o[b][:], o[b][:], ALU.mult)
                    dve.drain()
                    dve.tensor_reduce(ms[b][:], sq[:].rearrange("p t (h n) -> p (t h) n", n=per), AX.X, ALU.add)
                    dve.drain()
                    dve.tensor_scalar(ms[b][:], ms[b][:], 1.0 / per, EPS, ALU.mult, ALU.add).then_inc(meaned, 1)
                for b in range(2):
                    per = 1024 // heads[b]
                    dve.wait_ge(rooted, b + 1)
                    dve.reciprocal(rs[b][:], rs[b][:])
                    dve.drain()
                    v = o[b][:].rearrange("p t (h n) -> p (t h) n", n=per)
                    dve.tensor_tensor(v, v, rs[b][:].unsqueeze(2).to_broadcast([P, TT * heads[b], per]), ALU.mult
                                      ).then_inc(scaled, 1)
                m.store(dve, 0)
                dve.wait_ge(gated, 2)
                n = 0
                for b in range(2):
                    y = (k.yaT, k.ybT)[b]
                    for t in range(TT):
                        for half in range(2):
                            bank = k.bank[n % 6]
                            dve.wait_ge(turned, n + 1)
                            for j in range(4):
                                c = 4 * half + j
                                gain = k.chan[:, V_DNG:V_DNG + 1] if b == 0 else k.chan[:, V_MLG + c:V_MLG + c + 1]
                                src = bank[:, j * P:(j + 1) * P]
                                if b == 1 and t > 0:
                                    w0, wn = (t - 1) * (P // ROWS), P // ROWS
                                    src = src.rearrange("p (c r) -> p c r", r=ROWS)

                                    def raster(a):
                                        return a[:, c, NP_TOK:T].rearrange("p (r c) -> p c r", r=ROWS)[:, w0:w0 + wn, :]
                                    out, g = raster(y), raster(gate[b])
                                else:
                                    out, g = y[:, c, t * P:(t + 1) * P], gate[b][:, c, t * P:(t + 1) * P]
                                op = dve.scalar_tensor_tensor(out=out, in0=src, scalar=gain, in1=g,
                                                              op0=ALU.mult, op1=ALU.mult)
                            op.then_inc(read, 1)
                            n += 1
                m.store(dve, 1)

            @block.tensor
            def _(pe):
                n = 0
                m.multiply(pe, 0)
                for b in range(2):
                    pe.wait_ge(scaled, b + 1)
                    for t in range(TT):
                        if b == 1 and t == 2:
                            m.multiply(pe, 1)
                        for half in range(2):
                            if n >= 6:
                                pe.wait_ge(read, n - 5)
                            for j in range(4):
                                c = 4 * half + j
                                mm = pe.transpose(k.bank[n % 6][:, j * P:(j + 1) * P], o[b][:, t, c * P:(c + 1) * P],
                                                  k.ident)
                            mm.then_inc(turned, 1)
                            n += 1


def phase_merge(nc, k):
    with ExitStack() as mem:
        def sb(name, shape, dt=F32):
            return mem.enter_context(nc.sbuf_tensor(name, shape, dt))
        y = k.y2T
        y_hi, y_lo = (sb(n, [P, KT, T], F32R) for n in ("y_hi", "y_lo"))
        w = sb("merge_ring", [P, 2, KT, P])
        w_hi, w_lo = ([sb(f"{n}{b}", [P, KT, P], F32R) for b in range(2)] for n in ("merge_w_hi", "merge_w_lo"))
        gt = [sb(f"merge_gates{b}", [P, 2, T]) for b in range(2)]
        gated = [sb(f"merge_gated_{j}", [P, T]) for j in "ab"]
        s = {n: k.sem(n) for n in ("w_high", "w_low", "y_high", "y_low", "merge_summed", "merge_sig", "merge_read",
                                   "merged", "out_read")}
        landed = [k.sem(f"merge_landed{u}") for u in range(2)]
        gates_in = [k.sem(f"merge_gates_in{u}") for u in range(2)]
        HALF_K = KT // 2
        zero = sb("zero_rows", [P, 512])
        y_zeroed = k.sem("y_zeroed")

        def tiles(eng, first, body):
            for u in range(2):
                body(0, first, u)
            with eng.Fori(0, KT // 2 - 1) as i:
                for u in range(2):
                    body(i, first + 2, u)

        with nc.Block() as block:
            @block.sync
            def _(sp):
                for src, base in ((k.d_wup, 0), (k.d_wout, KT)):
                    with sp.Fori(0, KT // 2) as i:
                        for u in range(2):
                            sp.wait_ge(s["w_low"], i * 2 + (base + u + 1))
                            sp.dma_start(w[:, u], src[bass.ds(i * 2 + u, 1)].rearrange("a p k n -> p (a k) n")
                                         ).then_inc(landed[u], 16)

            @block.gpsimd
            def _(pool):
                pool.memset(zero[:], 0.0)
                pool.drain()
                for t in range(TT):
                    for c in range(D // 512):
                        pool.dma_start(k.d_y[t * P:(t + 1) * P, c * 512:(c + 1) * 512], zero[:]).then_inc(y_zeroed, 16)
                with pool.Fori(0, KT // 2) as i:
                    for u in range(2):
                        pool.wait_ge(s["merge_read"], i * 2 + u + 1)
                        for j, t0 in enumerate((T_GA, T_GB)):
                            pool.dma_start(gt[u][:, j, :], k.d_proj[bass.ds(i * 2 + (u + t0), 1)].rearrange(
                                "a p t -> p (a t)")).then_inc(gates_in[u], 16)
                pool.wait_ge(y_zeroed, 16 * TT * (D // 512))

            @block.tensor
            def _(pe):
                def products(base, u, kk, banks, start, stop):
                    for wt, ys in ((w_hi[u], (y_hi, y_lo)), (w_lo[u], (y_hi,))):
                        for yy in ys:
                            for c, (lo, hi) in enumerate(CHUNKS):
                                mm = pe.matmul(banks[c][:, 0:hi - lo], wt[:, kk, :], yy[:, kk, lo:hi],
                                               start=(start and wt is w_hi[u] and yy is y_hi),
                                               stop=(stop and wt is w_lo[u]))
                    return mm

                def merge_tile(i, base, u):
                    n = i * 2 + (base + u)
                    pe.wait_ge(s["w_low"], n + 3)
                    pe.wait_ge(s["merge_read"], n + 1)
                    for kk in range(KT):
                        j = kk // HALF_K
                        if isinstance(i, int) and base + u == 0:
                            pe.wait_ge(s["y_low"], kk + 1)
                        mm = products(base, u, kk, k.bank[4 * u + 2 * j:4 * u + 2 * j + 2],
                                      kk % HALF_K == 0, kk % HALF_K == HALF_K - 1)
                    mm.then_inc(s["merge_summed"], 1)

                def out_tile(i, base, u):
                    n = i * 2 + (base + u)
                    pe.wait_ge(s["w_low"], n + 3)
                    pe.wait_ge(s["out_read"], i * 2 + (base + u - KT + 1))
                    for kk in range(KT):
                        if isinstance(i, int) and base + u == KT:
                            pe.wait_ge(s["y_low"], KT + kk + 1)
                        mm = products(base, u, kk, k.bank[4 * u:4 * u + 2], kk == 0, kk == KT - 1)
                    mm.then_inc(s["merge_summed"], 1)
                tiles(pe, 0, merge_tile)
                tiles(pe, KT, out_tile)

            @block.scalar
            def _(act):
                act.sem_inc(s["out_read"], 2)

                def high(i, base, u):
                    if isinstance(i, int):
                        act.wait_ge(landed[u], 16 * ((base + u) // 2 + 1))
                    else:
                        act.wait_ge(landed[u], i * 16 + 16 * (base // 2 + 1))
                    act.activation(w_hi[u][:], w[:, u], ACT.Copy).then_inc(s["w_high"], 1)

                def split_y(first):
                    for kk in range(KT):
                        if first:
                            act.wait_ge(s["merged"], kk + 1)
                        act.activation(y_hi[:, kk, :], y[:, kk, :], ACT.Copy).then_inc(s["y_high"], 1)

                def merge_tile(i, base, u):
                    n = i * 2 + (base + u)
                    act.wait_ge(gates_in[u], i * 32 + 32 * (base // 2 + 1))
                    act.activation(gt[u][:], gt[u][:], ACT.Sigmoid).then_inc(s["merge_sig"], 1)
                    act.wait_ge(s["merge_summed"], n + 1)
                    high(i, base + 2, u)

                def out_tile(i, base, u, more=True):
                    n = i * 2 + (base + u)
                    act.wait_ge(s["merge_summed"], n + 1)
                    for c, (lo, hi) in enumerate(CHUNKS):
                        ev = act.activation(y[:].rearrange("p m t -> p (m t)")[
                            :, bass.ds((i * 2 + (base + u - KT)) * T + lo, hi - lo)],
                            k.bank[4 * u + c][:, 0:hi - lo], ACT.Copy)
                    ev.then_inc(s["out_read"], 1)
                    if more:
                        high(i, base + 2, u)
                high(0, 0, 0)
                high(0, 0, 1)
                split_y(0)
                tiles(act, 0, merge_tile)
                split_y(KT)
                with act.Fori(0, KT // 2 - 1) as i:
                    for u in range(2):
                        out_tile(i, KT, u)
                for u in range(2):
                    out_tile(0, 2 * KT - 2, u, more=False)

            @block.vector
            def _(dve):
                dve.sem_inc(s["w_low"], 2)
                dve.sem_inc(s["merge_read"], 2)

                def low(i, base, u):
                    dve.wait_ge(s["w_high"], i * 2 + (base + u + 1))
                    dve.tensor_tensor(w_lo[u][:], w[:, u], w_hi[u][:].bitcast(F32), ALU.subtract
                                      ).then_inc(s["w_low"], 1)

                def split_y(first):
                    for kk in range(KT):
                        dve.wait_ge(s["y_high"], first + kk + 1)
                        dve.tensor_tensor(y_lo[:, kk, :], y[:, kk, :], y_hi[:, kk, :].bitcast(F32), ALU.subtract
                                          ).then_inc(s["y_low"], 1)

                def merge_tile(i, base, u):
                    n = i * 2 + (base + u)
                    dve.wait_ge(s["merge_summed"], n + 1)
                    dve.wait_ge(s["merge_sig"], n + 1)
                    for j in range(2):
                        for c, (lo, hi) in enumerate(CHUNKS):
                            op = dve.tensor_tensor(gated[j][:, lo:hi], k.bank[4 * u + 2 * j + c][:, 0:hi - lo],
                                                   gt[u][:, j, lo:hi], ALU.mult)
                    op.then_inc(s["merge_read"], 1)
                    dve.drain()
                    dve.tensor_tensor(y[:].rearrange("p m t -> p (m t)")[:, bass.ds(n * T, T)], gated[0][:],
                                      gated[1][:], ALU.add).then_inc(s["merged"], 1)
                    dve.drain()
                    if isinstance(i, int) and base + u == KT - 1:
                        split_y(KT)
                    low(i, base + 2, u)

                low(0, 0, 0)
                low(0, 0, 1)
                split_y(0)
                with dve.Fori(0, KT // 2 - 1) as i:
                    for u in range(2):
                        merge_tile(i, 0, u)
                for u in range(2):
                    merge_tile(0, KT - 2, u)
                with dve.Fori(0, KT // 2 - 1) as i:
                    for u in range(2):
                        low(i, KT + 2, u)


def phase_residual_router(nc, k):
    with ExitStack() as mem:
        def sb(name, shape):
            return mem.enter_context(nc.sbuf_tensor(name, shape, F32))
        sq = [sb(f"rr_sq{b}", [P, T]) for b in range(4)]
        R = sb("rr_R", [P, T])
        wr = sb("w_router", [P, KT, N_EXP])
        tok = [sb(f"rr_tok{b}", [P, D]) for b in range(2)]
        mx = sb("aff_max", [P, TT])
        m = Gate2(nc, k, mem, 5 * KT + 8, 2)
        sm = sb("aff_sum", [P, TT])
        aff = sb("aff", [P, TT, N_EXP])
        s = {n: k.sem(n) for n in ("rr_w", "rr_sq_even", "rr_sq_odd", "rr_xT_turned", "rr_xT", "rr_sum",
                                   "rr_root", "rr_x1", "rr_h2", "rr_turned",
                                   "rr_copied", "rr_logits", "rr_sub", "rr_exp", "rr_aff", "rr_affT")}
        stored = [k.sem(f"rr_stored{b}") for b in range(2)]
        x_in = [k.sem(f"rr_x_in{b}") for b in range(2)]
        src = (k.y2T, k.xT)
        order = [(what, t) for what in range(2) for t in range(TT)]
        with nc.Block() as block:
            @block.sync
            def _(sp):
                for t in range(TT):
                    if t >= 2:
                        sp.wait_ge(s["rr_xT_turned"], t - 1)
                    sp.dma_start(tok[t % 2][:], k.d_x[t * P:(t + 1) * P, :]).then_inc(x_in[t % 2], 16)
                sp.dma_start(wr[:], k.d_wrouter).then_inc(s["rr_w"], 16)
                m.load(sp, 0)
                m.load(sp, 1)
                for n, (what, t) in enumerate(order):
                    sp.wait_ge(s["rr_copied"], 4 * n + 4)
                    sp.dma_start((k.d_x1, k.d_h2)[what][t * P:(t + 1) * P, :], tok[n % 2][:]).then_inc(stored[n % 2], 16)
                for b in range(2):
                    sp.wait_ge(stored[b], 16 * TT)

            @block.gpsimd
            def _(pool):
                for r in range(2):
                    for kk in range(1, KT, 2):
                        if r == 1:
                            pool.wait_ge(s["rr_x1"], kk + 1)
                        if r * KT + kk >= 4:
                            pool.wait_ge(s["rr_sum"], r * KT + kk - 3)
                        pool.tensor_tensor(sq[kk % 4][:], src[r][:, kk, :], src[r][:, kk, :], ALU.mult
                                           ).then_inc(s["rr_sq_odd"], 1)

            @block.tensor
            def _(pe):
                for r in range(2):
                    for kk in range(KT):
                        pe.wait_ge(s["rr_sq_" + ("even", "odd")[kk % 2]], (r * KT + kk) // 2 + 1)
                        pe.matmul(k.bank[0][:], k.ones, sq[kk % 4][:, NP_TOK:T], start=(kk == 0), stop=(kk == KT - 1))
                        pe.matmul(k.bank[1][:, 0:P], k.ones, sq[kk % 4][:, 0:NP_TOK], start=(kk == 0),
                                  stop=(kk == KT - 1)).then_inc(s["rr_sum"], 1)
                    if r == 0:
                        for t in range(TT):
                            pe.wait_ge(x_in[t % 2], 16 * (t // 2 + 1))
                            if t > 0:
                                pe.wait_ge(s["rr_xT"], t)
                            for kk in range(KT):
                                mm = pe.transpose(k.bank[2 + kk // 4][:, (kk % 4) * P:(kk % 4 + 1) * P],
                                                  tok[t % 2][:, kk * P:(kk + 1) * P], k.ident)
                            mm.then_inc(s["rr_xT_turned"], 1)
                for n, (what, t) in enumerate(order):
                    if n == 0:
                        m.multiply(pe, 0)
                        pe.wait_ge(s["rr_xT"], TT)
                    if n == TT:
                        m.multiply(pe, 1)
                        pe.wait_ge(s["rr_h2"], 1)
                        pe.wait_ge(s["rr_w"], 16)
                        for tt in range(TT):
                            for kk in range(KT):
                                mm = pe.matmul(k.bank[6][:, tt * N_EXP:(tt + 1) * N_EXP],
                                               k.y2T[:, kk, tt * P:(tt + 1) * P], wr[:, kk, :],
                                               start=(kk == 0), stop=(kk == KT - 1))
                        mm.then_inc(s["rr_logits"], 1)
                    for b in range(4):
                        i = 4 * n + b
                        if i >= 4:
                            pe.wait_ge(s["rr_copied"], i - 3)
                        for j in range(4):
                            mm = pe.transpose(k.bank[2 + b][:, j * P:(j + 1) * P],
                                              (k.xT, k.y2T)[what][:, 4 * b + j, t * P:(t + 1) * P], k.ident)
                        mm.then_inc(s["rr_turned"], 1)
                pe.wait_ge(s["rr_aff"], 1)
                pe.wait_ge(m.stored, 2)
                for t in range(TT):
                    mm = pe.transpose(k.bank[7][0:N_EXP, 0:P] if t == 0 else
                                      k.bank[0][0:N_EXP, (t - 1) * P:t * P], aff[:, t, :], k.ident)
                mm.then_inc(s["rr_affT"], 1)

            @block.scalar
            def _(act):
                for r in range(2):
                    for kk in range(0, KT, 2):
                        if r == 1:
                            act.wait_ge(s["rr_x1"], kk + 1)
                        if r * KT + kk >= 4:
                            act.wait_ge(s["rr_sum"], r * KT + kk - 3)
                        act.activation(sq[kk % 4][:], src[r][:, kk, :], ACT.Square).then_inc(s["rr_sq_even"], 1)
                    act.wait_ge(s["rr_sum"], (r + 1) * KT)
                    act.activation(R[:, NP_TOK:T], k.bank[0][:], ACT.Sqrt, bias=k.eps, scale=1.0 / D)
                    act.activation(R[:, 0:NP_TOK], k.bank[1][:, 0:P], ACT.Sqrt, bias=k.eps, scale=1.0 / D
                                   ).then_inc(s["rr_root"], 1)
                    if r == 0:
                        for t in range(TT):
                            act.wait_ge(s["rr_xT_turned"], t + 1)
                            for b in range(4):
                                ev = act.activation(k.xT[:, 4 * b:4 * b + 4, t * P:(t + 1) * P],
                                                    h4(k.bank[2 + b][:]), ACT.Copy)
                            ev.then_inc(s["rr_xT"], 1)
                for n, _ in enumerate(order):
                    if n == 0:
                        m.copy(act, 0)
                    if n == TT:
                        m.copy(act, 1)
                        act.wait_ge(s["rr_sub"], 1)
                        act.activation(aff[:], aff[:], ACT.Exp).then_inc(s["rr_exp"], 1)
                    if n >= 2:
                        act.wait_ge(stored[n % 2], 16 * (n // 2))
                    for b in range(4):
                        act.wait_ge(s["rr_turned"], 4 * n + b + 1)
                        act.activation(tok[n % 2][:, 4 * b * P:(4 * b + 4) * P], k.bank[2 + b][:], ACT.Copy
                                       ).then_inc(s["rr_copied"], 1)

            @block.vector
            def _(dve):
                for r in range(2):
                    dve.wait_ge(s["rr_root"], r + 1)
                    dve.reciprocal(R[:], R[:])
                    if r == 1:
                        m.store(dve, 0)
                    dve.drain()
                    for kk in range(KT):
                        dve.tensor_tensor(k.y2T[:, kk, :], src[r][:, kk, :], R[:], ALU.mult)
                    dve.drain()
                    if r == 0:
                        dve.wait_ge(s["rr_xT"], TT)
                    for kk in range(KT):
                        for c, (lo, hi) in enumerate(((0, NP_TOK), (NP_TOK, T))):
                            v = k.y2T[:, kk, lo:hi]
                            if r == 0:
                                op = dve.scalar_tensor_tensor(out=k.xT[:, kk, lo:hi], in0=v, scalar=k.g1[:, kk, c:c + 1],
                                                         in1=k.xT[:, kk, lo:hi], op0=ALU.mult, op1=ALU.add)
                            else:
                                dve.tensor_scalar(v, v, k.a2[:, kk, c:c + 1], k.modT[:, 3 * KT + kk, c:c + 1],
                                                  ALU.mult, ALU.add)
                        if r == 0:
                            op.then_inc(s["rr_x1"], 1)
                    if r == 1:
                        dve.drain().then_inc(s["rr_h2"], 1)
                        m.store(dve, 1)
                        dve.drain()
                        with_gain(dve, k, k.g2, V_POST2, 5, 0.0)
                    else:
                        dve.drain()
                dve.wait_ge(s["rr_logits"], 1)
                lg = k.bank[6][:, 0:TT * N_EXP].rearrange("p (t n) -> p t n", t=TT)
                dve.tensor_reduce(mx[:], lg, AX.X, ALU.max)
                dve.drain()
                dve.tensor_tensor(aff[:], lg, mx[:].unsqueeze(2).to_broadcast([P, TT, N_EXP]), ALU.subtract
                                  ).then_inc(s["rr_sub"], 1)
                dve.wait_ge(s["rr_exp"], 1)
                dve.tensor_reduce(sm[:], aff[:], AX.X, ALU.add)
                dve.drain()
                dve.reciprocal(sm[:], sm[:])
                dve.drain()
                dve.tensor_tensor(aff[:], aff[:], sm[:].unsqueeze(2).to_broadcast([P, TT, N_EXP]), ALU.mult
                                  ).then_inc(s["rr_aff"], 1)
                dve.wait_ge(s["rr_affT"], 1)
                dve.tensor_copy(k.affT[:, 0:P], k.bank[7][0:N_EXP, 0:P])
                dve.tensor_copy(k.affT[:, P:T], k.bank[0][0:N_EXP, :])


def phase_choice(nc, k):
    with ExitStack() as mem:
        val = mem.enter_context(nc.sbuf_tensor("top_val", [N_EXP, CAP], F32))
        ind = mem.enter_context(nc.sbuf_tensor("top_ind", [N_EXP, CAP], U32))
        indf = mem.enter_context(nc.sbuf_tensor("top_indf", [N_EXP, CAP], F32))
        chosen, turned = k.sem("chosen"), k.sem("choice_turned")
        with nc.Block() as block:
            @block.sync
            def _(sp):
                for j in range(EXP_SLOTS):
                    load_split_tile(k, sp, 0, 0, j)
            @block.vector
            def _(dve):
                for lo, hi, s0, cap in ((0, NP_TOK, 0, CAP_P), (NP_TOK, T, CAP_P, CAP_S)):
                    v = k.affT[:, lo:hi]
                    for r in range(cap // 8):
                        a, b = s0 + 8 * r, s0 + 8 * r + 8
                        dve.max(val[:, a:b], v)
                        dve.drain()
                        dve.max_index(ind[:, a:b], val[:, a:b], v)
                        dve.drain()
                        dve.match_replace(v, val[:, a:b], v, MASKED_ROW)
                        dve.drain()
                dve.tensor_copy(indf[:], ind[:])
                dve.drain()
                dve.tensor_scalar(indf[:, CAP_P:CAP], indf[:, CAP_P:CAP], float(NP_TOK), None, ALU.add)
                dve.drain().then_inc(chosen, 1)
                dve.wait_ge(turned, 1)
                dve.tensor_copy(k.gateT[:], k.bank[0][0:CAP, 0:N_EXP])
                dve.tensor_copy(k.idx[:], k.bank[0][0:CAP, N_EXP:2 * N_EXP])

            @block.tensor
            def _(pe):
                pe.wait_ge(chosen, 1)
                pe.transpose(k.bank[0][0:CAP, 0:N_EXP], val[:], k.ident[0:N_EXP, 0:N_EXP])
                pe.transpose(k.bank[0][0:CAP, N_EXP:2 * N_EXP], indf[:], k.ident[0:N_EXP, 0:N_EXP]
                             ).then_inc(turned, 1)


def load_split_tile(k, sp, i, first, j):
    half, which, part = j // 8, j // 4 % 2, j % 4
    src = (k.d_wgate, k.d_wup_e)[which][bass.ds(i * 8 + (8 * first + 4 * half + part), 1)]
    sp.dma_start(k.expert_ring[:, j % EXP_SLOTS], src.rearrange("a p k n -> p (a k n)")
                 ).then_inc(k.expert_landed[j % EXP_SLOTS], 16)


def phase_experts(nc, k):
    NSLOT, NSPLIT = EXP_SLOTS, EXP_AHEAD
    NGU = 16
    FT = F_EXP // P
    DC = 256
    HALF = 512
    with ExitStack() as mem:
        def sb(name, shape, dt=F32):
            return mem.enter_context(nc.sbuf_tensor(name, shape, dt))
        w, landed = k.expert_ring, k.expert_landed
        w_hi, w_lo = ([sb(f"{n}{r}", [P, 4, HALF], F32R) for r in range(NSPLIT)] for n in ("expert_hi", "expert_lo"))
        xe = [sb(f"xe{b}", [CAP, D]) for b in range(2)]
        x_hi, x_lo = (sb(n, [P, KT, P], F32R) for n in ("xeT_hi", "xeT_lo"))
        sg = sb("silu_gate", [CAP, HALF])
        hr = sb("hidden_rows", [CAP, HALF])
        hT = sb("hiddenT", [P, FT, CAP])
        ye = [sb(f"ye{b}", [CAP, D]) for b in range(2)]
        s = {n: k.sem(n) for n in ("xe_landed0", "xe_landed1", "xe_turned", "x_high", "x_low", "x_padded",
                                   "we_high", "we_low", "we_used", "down_used", "silu_done", "hidden", "h_turned",
                                   "h_copied", "ye_done", "scattered", "rows_free")}
        g2_out = k.sem("g2_out")
        gate_bank, up_bank = k.bank[0:2], k.bank[2:4]
        x_bank, h_bank, down_bank = k.bank[4:6], k.bank[4], k.bank[6:8]

        def experts(eng, body):
            with eng.Fori(0, N_EXP // 2 - 1) as i:
                for b in range(2):
                    body(i, b, True)
            for b in range(2):
                body(N_EXP // 2 - 1, b, b == 0)

        with nc.Block() as block:
            @block.sync
            def _(sp):
                def load(i, first, more=True):
                    for j in range(NSPLIT if first > 0 else NSLOT, NGU + NSPLIT):
                        if j < NSPLIT + 8 and first > 0:
                            sp.wait_ge(s["down_used"], i * 8 + (8 * (first - 1) + j - NSPLIT + 1))
                        elif j >= NSLOT:
                            sp.wait_ge(s["we_low"], i * NGU + (NGU * first + j - NSLOT + 1))
                        if j < NGU:
                            load_split_tile(k, sp, i, first, j)
                        elif more:
                            load_split_tile(k, sp, i, first + 1, j - NGU)
                    for c in range(8):
                        if more or c < 4:
                            sp.wait_ge(s["we_low"], i * NGU + (NGU * first + 12 + c + 1))
                        slot = (NSPLIT + c) % NSLOT
                        sp.dma_start(w[:, slot], k.d_wdown[bass.ds(i * 8 + (8 * first + c), 1)].rearrange(
                            "a p k n -> p (a k n)")).then_inc(landed[slot], 16)
                with nc.allow_non_contiguous_dma(reason="4096 gate values, once"):
                    for c in range(2):
                        sp.dma_start(k.d_g2[c:c + 1].rearrange("a (k p) -> p (a k)", p=P), k.g2[:, :, c]
                                     ).then_inc(g2_out, 16)
                load(0, 0)
                with sp.Fori(0, N_EXP - 2) as i:
                    load(i, 1)
                load(0, N_EXP - 1, more=False)
                sp.wait_ge(g2_out, 32)

            @block.gpsimd
            def _(pool):
                def gather(e_col, b):
                    pool.indirect_dma_start(xe[b][:], None, k.d_h2[:, :],
                                            bass.IndirectOffsetOnAxis(ap=k.idx[:, e_col:e_col + 1], axis=0)
                                            ).then_inc(s[f"xe_landed{b}"], 16)

                pool.sem_inc(s["rows_free"], 2)
                for e in range(2):
                    gather(e, e)
                for e in range(N_EXP):
                    if e + 2 < N_EXP:
                        pool.wait_ge(s["xe_turned"], 4 * e + 4)
                        gather(e + 2, e % 2)
                    pool.wait_ge(s["ye_done"], 4 * e + 4 + 2)
                    if e > 0:
                        pool.wait_ge(s["scattered"], 16 * e)
                        pool.sem_inc(s["rows_free"], 1)
                    pool.indirect_dma_start(k.d_y[:, :], bass.IndirectOffsetOnAxis(ap=k.idx[:, e:e + 1], axis=0),
                                            ye[e % 2][:], None, compute_op=ALU.add).then_inc(s["scattered"], 16)
                pool.wait_ge(s["scattered"], 16 * N_EXP)

            def wait_split(eng, i, b, j):
                if j >= NSPLIT:
                    eng.wait_ge(landed[j % NSLOT], i * 96 + (48 * b + 16 * (j // NSLOT + 1)))
                elif isinstance(i, int) and i == 0 and b == 0:
                    eng.wait_ge(landed[j], 16)
                else:
                    eng.wait_ge(landed[j], i * 96 + 48 * b)

            def wait_down(eng, i, b, c, more):
                fills = 3 if c < 4 or not more else 4
                eng.wait_ge(landed[(NSPLIT + c) % NSLOT], i * 96 + (48 * b + 16 * fills))

            @block.tensor
            def _(pe):
                def turn_x(i, b):
                    pe.wait_ge(s[f"xe_landed{b % 2}"], i * 16 + (16 * (b // 2) + 16))
                    for r in range(4):
                        if r >= 2:
                            pe.wait_ge(s["x_low"], i * 8 + (4 * b + r - 1))
                        for j in range(4):
                            kk = 4 * r + j
                            mm = pe.transpose(x_bank[r % 2][:, j * P:j * P + CAP],
                                              xe[b % 2][:, kk * P:(kk + 1) * P], k.ident[0:CAP, 0:CAP])
                        mm.then_inc(s["xe_turned"], 1)

                def turn_hidden(i, b, c):
                    pe.wait_ge(s["hidden"], i * 4 + (2 * b + c + 3))
                    pe.wait_ge(s["h_copied"], i * 4 + (2 * b + c + 1))
                    for f in range(4):
                        mm = pe.transpose(h_bank[:, f * P:f * P + CAP], hr[:, f * P:(f + 1) * P],
                                          k.ident[0:CAP, 0:CAP])
                    mm.then_inc(s["h_turned"], 1)

                def body(i, b, more):
                    pe.wait_ge(s["x_low"], i * 8 + (4 * b + 4))
                    for j in range(NGU):
                        c, which, part = j // 8, j // 4 % 2, j % 4
                        out = (gate_bank, up_bank)[which][c]
                        if j % 8 == 0:
                            pe.wait_ge(s["hidden"], i * 4 + (2 * b + c + 1))
                        pe.wait_ge(s["we_low"], i * (2 * NGU) + (NGU * b + j + 1))
                        for q in range(4):
                            kk = 4 * part + q
                            hi, lo = w_hi[j % NSPLIT][:, q, :], w_lo[j % NSPLIT][:, q, :]
                            pe.matmul(out[:], x_hi[:, kk, :], hi, start=(kk == 0), stop=False)
                            pe.matmul(out[:], x_hi[:, kk, :], lo, start=False, stop=False)
                            mm = pe.matmul(out[:], x_lo[:, kk, :], hi, start=False, stop=(kk == KT - 1))
                        mm.then_inc(s["we_used"], 1)
                        if j == 9:
                            turn_hidden(i, b, 0)
                    turn_hidden(i, b, 1)
                    for c in range(8):
                        if c == 4 and more:
                            turn_x(i, b + 1)
                        wait_down(pe, i, b, c, more)
                        wd = w[:, (NSPLIT + c) % NSLOT].rearrange("p (k n) -> p k n", n=DC)
                        if c % 2 == 0:
                            pe.wait_ge(s["ye_done"], i * 8 + (4 * b + c // 2 + 1))
                        for kk in range(FT):
                            if c == 0 and kk % 4 == 0:
                                pe.wait_ge(s["h_copied"], i * 4 + (2 * b + kk // 4 + 2))
                            mm = pe.matmul(down_bank[c // 2 % 2][0:CAP, (c % 2) * DC:(c % 2 + 1) * DC],
                                           hT[:, kk, :], wd[:, kk, :], start=(kk == 0), stop=(kk == FT - 1))
                        mm.then_inc(s["down_used"], 1)
                pe.wait_ge(s["x_padded"], 1)
                turn_x(0, 0)
                experts(pe, body)

            @block.scalar
            def _(act):
                act.sem_inc(s["h_copied"], 1)

                def high(i, b, j):
                    wait_split(act, i, b, j)
                    if not (isinstance(i, int) and i == 0 and b == 0 and j < NSPLIT):
                        act.wait_ge(s["we_used"], i * (2 * NGU) + (NGU * b + j + 1 - NSPLIT))
                    act.activation(w_hi[j % NSPLIT][:], w[:, j % NSLOT].rearrange("p (k n) -> p k n", n=HALF), ACT.Copy
                                   ).then_inc(s["we_high"], 1)

                def x_high(i, b):
                    for r in range(4):
                        act.wait_ge(s["xe_turned"], i * 8 + (4 * b + r + 1))
                        act.activation(x_hi[:, 4 * r:4 * r + 4, 0:CAP], h4(x_bank[r % 2][:])[:, :, 0:CAP], ACT.Copy
                                       ).then_inc(s["x_high"], 1)

                def silu(i, b, c):
                    act.wait_ge(s["we_used"], i * (2 * NGU) + (NGU * b + 8 * c + 4))
                    act.wait_ge(s["hidden"], i * 4 + (2 * b + c + 2))
                    act.activation(sg[:], gate_bank[c][0:CAP, :], ACT.Silu).then_inc(s["silu_done"], 1)

                def copy_hidden(i, b, c):
                    act.wait_ge(s["h_turned"], i * 4 + (2 * b + c + 2))
                    act.activation(hT[:, 4 * c:4 * c + 4, :], h4(h_bank[:])[:, :, 0:CAP], ACT.Copy
                                   ).then_inc(s["h_copied"], 1)

                def body(i, b, more):
                    for j in range(NGU):
                        if j in (3, 11):
                            silu(i, b, j // 8)
                        if j == 15:
                            copy_hidden(i, b, 1)
                        if j + NSPLIT < NGU:
                            high(i, b, j + NSPLIT)
                        elif more:
                            high(i, b + 1, j + NSPLIT - NGU)
                        if j == 9:
                            copy_hidden(i, b, 0)
                    if more:
                        x_high(i, b + 1)
                for j in range(NSPLIT):
                    high(0, 0, j)
                act.wait_ge(s["x_padded"], 1)
                x_high(0, 0)
                experts(act, body)

            @block.vector
            def _(dve):
                dve.sem_inc(s["hidden"], 2)
                dve.sem_inc(s["h_turned"], 1)
                dve.sem_inc(s["ye_done"], 2)
                ones = k.ones[:, CAP:P].unsqueeze(1).to_broadcast([P, KT, P - CAP])
                for x in (x_hi, x_lo):
                    dve.tensor_tensor(x[:, :, CAP:P], ones, ones, ALU.subtract)
                dve.drain().then_inc(s["x_padded"], 1)

                def low(i, b, j):
                    dve.wait_ge(s["we_high"], i * (2 * NGU) + (NGU * b + j + 1))
                    dve.tensor_tensor(w_lo[j % NSPLIT][:], w[:, j % NSLOT].rearrange("p (k n) -> p k n", n=HALF),
                                      w_hi[j % NSPLIT][:].bitcast(F32), ALU.subtract).then_inc(s["we_low"], 1)

                def x_low(i, b):
                    for r in range(4):
                        dve.wait_ge(s["x_high"], i * 8 + (4 * b + r + 1))
                        dve.tensor_tensor(x_lo[:, 4 * r:4 * r + 4, 0:CAP], h4(x_bank[r % 2][:])[:, :, 0:CAP],
                                          x_hi[:, 4 * r:4 * r + 4, 0:CAP].bitcast(F32), ALU.subtract
                                          ).then_inc(s["x_low"], 1)

                def hidden(i, b, c):
                    dve.wait_ge(s["silu_done"], i * 4 + (2 * b + c + 1))
                    dve.wait_ge(s["we_used"], i * (2 * NGU) + (NGU * b + 8 * c + 8))
                    dve.wait_ge(s["h_turned"], i * 4 + (2 * b + c + 1))
                    dve.tensor_tensor(hr[:], up_bank[c][0:CAP, :], sg[:], ALU.mult).then_inc(s["hidden"], 1)

                def gated(i, b, c):
                    dve.wait_ge(s["down_used"], i * 16 + (8 * b + 2 * c + 2))
                    dve.tensor_scalar(ye[b][:, c * 512:(c + 1) * 512], down_bank[c % 2][0:CAP, :],
                                      k.gateT[:, bass.ds(i * 2 + b, 1)], None, ALU.mult).then_inc(s["ye_done"], 1)

                def body(i, b, more):
                    for j in range(NGU):
                        if j in (7, 15):
                            hidden(i, b, j // 8)
                        if j + NSPLIT < NGU:
                            low(i, b, j + NSPLIT)
                        elif more:
                            low(i, b + 1, j + NSPLIT - NGU)
                    dve.wait_ge(s["rows_free"], i * 2 + (b + 1))
                    gated(i, b, 0)
                    gated(i, b, 1)
                    if more:
                        x_low(i, b + 1)
                    gated(i, b, 2)
                    gated(i, b, 3)
                for j in range(NSPLIT):
                    low(0, 0, j)
                x_low(0, 0)
                experts(dve, body)


def phase_final(nc, k):
    with ExitStack() as mem:
        def sb(name, shape):
            return mem.enter_context(nc.sbuf_tensor(name, shape, F32))
        row = [sb(f"g2_row{c}", [P, D]) for c in range(2)]
        y = [sb(f"y_in{b}", [P, D]) for b in range(2)]
        x1 = [sb(f"x1_in{b}", [P, D]) for b in range(2)]
        sq = sb("y_sq", [P, D])
        ms = [sb(f"y_ms{b}", [P, 1]) for b in range(2)]
        rs = [sb(f"y_rs{b}", [P, 1]) for b in range(2)]
        rows_in, summed, rooted, done = (k.sem(n) for n in ("g2_rows_in", "y_summed", "y_rooted", "y_done"))
        landed = [k.sem(f"y_landed{b}") for b in range(2)]
        stored = [k.sem(f"out_stored{b}") for b in range(2)]
        with nc.Block() as block:
            @block.sync
            def _(sp):
                for t in range(TT):
                    b = t % 2
                    if t >= 2:
                        sp.wait_ge(done, t - 1)
                        sp.wait_ge(stored[b], 16 * (t // 2))
                    sp.dma_start(y[b][:], k.d_y[t * P:(t + 1) * P, :]).then_inc(landed[b], 16)
                    sp.dma_start(x1[b][:], k.d_x1[t * P:(t + 1) * P, :]).then_inc(landed[b], 16)
                    if t < 2:
                        sp.dma_start(row[t][:], k.d_g2[t:t + 1, :].to_broadcast([P, D])).then_inc(rows_in, 16)

            @block.gpsimd
            def _(pool):
                for t in range(TT):
                    pool.wait_ge(done, t + 1)
                    dst = k.o_yp[:, :] if t == 0 else k.o_ys[(t - 1) * P:t * P, :]
                    pool.dma_start(dst, x1[t % 2][:]).then_inc(stored[t % 2], 16)
                pool.wait_ge(stored[0], 48)
                pool.wait_ge(stored[1], 32)

            @block.scalar
            def _(act):
                for t in range(TT):
                    b = t % 2
                    act.wait_ge(landed[b], 32 * (t // 2 + 1))
                    if t >= 2:
                        act.wait_ge(rooted, t - 1)
                    act.activation(sq[:], y[b][:], ACT.Square, accum_out=ms[b][:])
                    act.drain()
                    if t >= 2:
                        act.wait_ge(done, t - 1)
                    act.activation(rs[b][:], ms[b][:], ACT.Sqrt, bias=k.eps, scale=1.0 / D).then_inc(rooted, 1)

            @block.vector
            def _(dve):
                dve.wait_ge(rows_in, 32)
                for t in range(TT):
                    b = t % 2
                    dve.wait_ge(rooted, t + 1)
                    dve.reciprocal(rs[b][:], rs[b][:])
                    dve.drain()
                    dve.scalar_tensor_tensor(out=y[b][:], in0=y[b][:], scalar=rs[b][:, 0:1], in1=row[min(t, 1)][:],
                                             op0=ALU.mult, op1=ALU.mult)
                    dve.drain()
                    dve.tensor_tensor(x1[b][:], x1[b][:], y[b][:], ALU.add).then_inc(done, 1)


def build(nc, ins, outs):
    with ExitStack() as ctx:
        taken = []

        def take(name):
            taken.append(nc.alloc_semaphore(name=name))
            return taken[-1]

        def give_back():
            nc.clear_and_free_semaphores(taken)
            taken.clear()
            nc.all_engine_barrier()

        def sb(stack, name, shape, dt=F32):
            return stack.enter_context(nc.sbuf_tensor(name, shape, dt))

        scratch = {name: nc.dram_tensor(name, shape, F32).ap() for name, shape in (
            ("d_proj", [N_TILES, P, T]), ("d_x1", [T, D]), ("d_h2", [T, D]), ("d_y", [T, D]), ("d_g2", [2, D]))}
        k = Chip(take, ins, outs, scratch)
        k.bank = [ctx.enter_context(nc.psum_tensor(f"bank{b}", [P, 512], F32)) for b in range(8)]
        k.const = sb(ctx, "const", [P, N_CONST])
        k.chan = sb(ctx, "chan", [P, N_CHAN])
        k.rowp = sb(ctx, "rowp", [P, N_ROWP])
        k.modT = sb(ctx, "modT", [P, N_MOD_TILES, 2])
        k.cond = sb(ctx, "cond", [P, KT, 2])
        k.a1, k.a2, k.g1, k.g2 = (sb(ctx, n, [P, KT, 2]) for n in ("a1", "a2", "g1", "g2"))
        k.affT = sb(ctx, "affT", [N_EXP, T])
        k.gateT = sb(ctx, "gateT", [CAP, N_EXP])
        k.idx = sb(ctx, "idx", [CAP, N_EXP], U32)
        k.ident = k.const[:, C_ID:C_ID + P]
        k.tri = [k.const[:, C_TRI + d * P:C_TRI + (d + 1) * P] for d in range(2)]
        k.neg = [k.const[:, C_NEG + d * P:C_NEG + (d + 1) * P] for d in range(2)]
        k.ones = k.const[:, C_ONES:C_ONES + P]
        k.level1 = lambda d: k.const[:, C_LEV + d * P:C_LEV + (d + 1) * P]
        k.level = lambda d, n: k.const[:, C_CMP + (2 * n + d) * (P // 2):C_CMP + (2 * n + d + 1) * (P // 2)]
        k.eps = k.chan[:, V_L2B + 8:V_L2B + 9]

        back = ExitStack()
        with ExitStack() as front:
            k.gates = sb(front, "gates", [P, TT, 48])
            with ExitStack() as split:
                with ExitStack() as inner:
                    k.hT = sb(inner, "hT", [P, KT, T])
                    phase_modulation(nc, k)
                    k.h_hi, k.h_lo = (split.enter_context(nc.sbuf_tensor(n, [P, KT, T], F32R, side="right"))
                                      for n in ("h_hi", "h_lo"))
                    phase_first_norm(nc, k)
                phase_projection(nc, k)
            k.o_dn, k.o_ml = (sb(front, n, [P, TT, 1024]) for n in ("o_dn", "o_ml"))
            k.beta, k.G, k.nG, k.eG, k.neg_eG, k.wS, k.bw, k.g_tot, k.eT = (
                sb(front, n, [P, TT, 16]) for n in ("beta", "G", "nG", "eG", "neg_eG", "wS", "bw", "g_tot", "eT"))
            k.ci, k.b_ml, k.b_tot = (sb(front, n, [P, TT, 8]) for n in ("ci", "b_ml", "b_tot"))
            k.ident_bf, k.neg_bf = (sb(front, n, shape, BF16) for n, shape in (
                ("ident_bf", [P, P]), ("neg_bf", [P, 2, P])))
            phase_gates(nc, k)
            phase_deltanet(nc, k)
            phase_mlstm(nc, k)
            give_back()
            k.y2T = back.enter_context(nc.sbuf_tensor("y_parts", [P, KT, T], F32, side="right"))
            k.yaT, k.ybT = k.y2T[:, 0:8, :], k.y2T[:, 8:16, :]
            phase_branch_outputs(nc, k)
        with back:
            phase_merge(nc, k)
            k.xT = sb(back, "xT", [P, KT, T])
            phase_residual_router(nc, k)
        with ExitStack() as experts:
            k.expert_ring = sb(experts, "expert_ring", [P, EXP_SLOTS, D])
            k.expert_landed = [take(f"we_landed{j}") for j in range(EXP_SLOTS)]
            phase_choice(nc, k)
            phase_experts(nc, k)
        phase_final(nc, k)


def constants():
    c = np.zeros((P, N_CONST), np.float32)
    j, i = np.meshgrid(np.arange(P), np.arange(P), indexing="ij")
    c[:, C_ID:C_ID + P] = j == i
    for d, ok in enumerate((j <= i, j >= i)):
        c[:, C_TRI + d * P:C_TRI + (d + 1) * P] = ok
        c[:, C_NEG + d * P:C_NEG + (d + 1) * P] = np.where(ok, 0.0, NEG)
    c[:, C_ONES:C_ONES + P] = 1.0
    for n, s in enumerate(LEVELS):
        same = j // (2 * s) == i // (2 * s)
        low, high = (j // s) % 2, (i // s) % 2
        for d in range(2):
            mask = same & (low == d) & (high == 1 - d)
            if s == 1:
                c[:, C_LEV + d * P:C_LEV + (d + 1) * P] = mask
            a = C_CMP + (2 * n + d) * (P // 2)
            c[:, a:a + P // 2] = mask.T[:, (np.arange(P) // s) % 2 == d]
    return c


def tiles_of(w, width=P):
    kk, n = w.shape
    return np.ascontiguousarray(w.reshape(kk // P, P, n // width, width).transpose(2, 1, 0, 3))


def halves_of(w):
    e, kk, n = w.shape
    w = w.reshape(e, kk // (4 * P), 4, P, n // 512, 512)
    return np.ascontiguousarray(w.transpose(0, 4, 1, 3, 2, 5)).reshape(-1, P, 4, 512)


def channels(v):
    return v.reshape(-1, P).T


def lay_out(x):
    f = np.float32
    w_in, b_in = x["w_in"][0], x["b_in"][0]
    cuts = np.cumsum([0, 1024, 1024, 1024, 1024, 16, 16, 512, 512, 1024, 1024, 8, 8, 2048, 2048])
    names = ("dq", "dk", "dv", "dz", "db", "da", "mq", "mk", "mv", "mo", "mi", "mf", "ga", "gb")
    part = {n: slice(cuts[i], cuts[i + 1]) for i, n in enumerate(names)}
    order = ("dq", "dk", "dv", "mq", "mk", "mv", "dz", "mo", "ga", "gb")
    gates = ("db", "da", "mi", "mf")
    w_gates = np.concatenate([w_in[:, part[n]] for n in gates] + [np.zeros((D, P - 48), f)], 1)
    w_tiles = np.concatenate([tiles_of(w_in[:, part[n]]) for n in order] + [tiles_of(w_gates)])
    chan = np.zeros((P, N_CHAN), f)
    cond = np.stack([x["c_ctx"], x["c"][0]], 1)
    chan[:, V_COND:V_BMOD] = cond.reshape(KT, P, 2).transpose(1, 0, 2).reshape(P, 2 * KT)
    chan[:, V_BMOD:V_PRE1] = channels(x["b_mod"][0])
    for at, n in ((V_PRE1, "pre1_gain"), (V_POST1, "post1_gain"), (V_PRE2, "pre2_gain"), (V_POST2, "post2_gain")):
        chan[:, at:at + KT] = channels(x[n][0])
    chan[:, V_BIN:V_CONV - 1] = np.concatenate([channels(b_in[part[n]]) for n in order], 1)
    chan[0:48, V_CONV - 1] = np.concatenate([b_in[part[n]] for n in gates])
    chan[:, V_CONV:V_L2S] = x["dn_conv_w"][0].reshape(5, 24, P).transpose(2, 1, 0).reshape(P, 120)
    chan[:, V_L2S:V_L2S + 8], chan[:, V_L2S + 8:V_L2S + 16] = float(P), 1.0
    chan[:, V_L2B:V_L2B + 8], chan[:, V_L2B + 8:V_L2B + 16] = P * EPS, EPS
    chan[:, V_DNG] = x["dn_onorm"][0]
    chan[:, V_MLG:V_MLG + 8] = channels(x["ml_onorm"][0].reshape(-1))
    row = np.concatenate([x["dn_dt_bias"].reshape(-1), x["ml_f_bias"].reshape(-1), x["ml_i_bias"].reshape(-1),
                          x["dn_a_log"].reshape(-1), x["state_ml_m"].reshape(-1)])
    return {
        "d_const": constants(), "d_chan": chan, "d_rowp": np.ascontiguousarray(np.broadcast_to(row, (P, N_ROWP))),
        "d_x": np.concatenate([x["x_prompt"][0], x["x_sample"][0]]),
        "d_wmod": tiles_of(x["w_mod"][0]), "d_win": w_tiles,
        "d_sdn": x["state_dn"][0, 0], "d_smc": x["state_ml_c"][0, 0], "d_smn": x["state_ml_n"][0, 0],
        "d_wup": np.concatenate([tiles_of(x["w_up_a"][0]), tiles_of(x["w_up_b"][0])], 2),
        "d_wout": tiles_of(x["w_out"][0]),
        "d_wrouter": np.ascontiguousarray(x["w_router"][0].reshape(KT, P, N_EXP).transpose(1, 0, 2)),
        "d_wgate": halves_of(x["w_gate"][0]), "d_wup_e": halves_of(x["w_up"][0]),
        "d_wdown": np.concatenate([tiles_of(w, 256) for w in x["w_down"][0]]),
    }


_OUTS = [("o_yp", (NP_TOK, D)), ("o_ys", (NS_TOK, D)), ("o_sdn", (2, H_DN, P, P)), ("o_smc", (2, H_ML, P, DV_ML)),
         ("o_smn", (2, H_ML, P)), ("o_smm", (2, H_ML))]


def kernel(**inputs):
    import concourse.bacc as bacc
    from concourse.bass_utils import run_bass_kernel_spmd

    arrays = lay_out({n: np.asarray(a) for n, a in inputs.items()})
    nc = bacc.Bacc("TRN2", target_bir_lowering=False, num_devices=1)
    ins = {n: nc.dram_tensor(n, a.shape, F32, kind="ExternalInput").ap() for n, a in arrays.items()}
    outs = {n: nc.dram_tensor(n, shape, F32, kind="ExternalOutput").ap() for n, shape in _OUTS}
    build(nc, ins, outs)
    r = run_bass_kernel_spmd(nc, [arrays], core_ids=[0]).results[0]
    return (r["o_yp"][None], r["o_ys"][None], r["o_sdn"][None, None], r["o_smc"][None, None],
            r["o_smn"][None, None], r["o_smm"][None, None])
```
